# Optimizing a Trainium2 kernel written in Bass

```python
import jax, jax.numpy as jnp
from jax import lax
import numpy as np

D_MODEL = 1024
BATCH = 1
SEQ = 128
DEPTH = 2
DEC_BATCH = 1
DEC_SEQ = 256
PAST_LEN = 128

GRID_W = 64
N_EVEN = (DEPTH + 1) // 2
N_ODD = DEPTH // 2
CONV_DIM = 512
CONV_K = 3
POOL_WINDOWS = (2, 4, 8, 16)
N_POOL = 4
POOL_DIM = 512
POOL_GROUP = POOL_DIM // N_POOL
EVEN_IN = 3 * CONV_DIM + POOL_DIM
EVEN_MIX = CONV_DIM + POOL_DIM
N_HEADS = 8
QK_NOPE = 128
QK_ROPE = 64
QK_HEAD = QK_NOPE + QK_ROPE
V_DIM = 128
Q_RANK = 384
KV_RANK = 256
ROPE_THETA = 10000.0
Q_BLOCK = 128
FNET_GROUPS = 4
FNET_GROUP_DIM = 64
FNET_DIM = FNET_GROUPS * FNET_GROUP_DIM
ODD_IN = Q_RANK + KV_RANK + QK_ROPE + FNET_DIM
ODD_MIX = N_HEADS * V_DIM + FNET_DIM
D_FF = 2816
N_EXPERTS = 8
TOP_K = 2
D_FF_EXPERT = 1792
ALPHA = (2 * DEPTH) ** 0.25
BETA = (8 * DEPTH) ** -0.25
LN_EPS = 1e-5
RMS_EPS = 1e-6

kernel_name = "hybrid_diffusion_prefix_trunk_step"

def layer_norm(x, g, b):
    xf = x.astype(jnp.float32)
    mu = jnp.mean(xf, axis=-1, keepdims=True)
    var = jnp.mean(jnp.square(xf - mu), axis=-1, keepdims=True)
    return ((xf - mu) * lax.rsqrt(var + LN_EPS) * g + b).astype(x.dtype)

def rms_norm(x, g):
    xf = x.astype(jnp.float32)
    return (xf * lax.rsqrt(jnp.mean(jnp.square(xf), axis=-1, keepdims=True) + RMS_EPS) * g).astype(x.dtype)

def modulation(cond, w, b):
    m = jax.nn.silu(cond) @ w + b
    return jnp.split(m[..., None, :], 6, axis=-1)

def modulate(x, shift, scale):
    return x * (1.0 + scale) + shift

def post_norm(x, y, gate, g, b):
    return layer_norm(ALPHA * x + gate * y, g, b)

def axial_rope(L):
    rows = L // GRID_W
    row = jnp.repeat(jnp.arange(rows), GRID_W).astype(jnp.float32)
    col = jnp.tile(jnp.arange(GRID_W), rows).astype(jnp.float32)
    half = QK_ROPE // 2
    inv = ROPE_THETA ** (-jnp.arange(0, half, 2, dtype=jnp.float32) / half)
    ar, ac = row[:, None] * inv, col[:, None] * inv
    ang = jnp.concatenate([ar, ar, ac, ac], axis=-1)
    return jnp.cos(ang), jnp.sin(ang)

def rotate_half_axial(x):
    q = QK_ROPE // 4
    x = x.reshape(x.shape[:-1] + (2, 2, q))
    x = jnp.stack([-x[..., 1, :], x[..., 0, :]], axis=-2)
    return x.reshape(x.shape[:-3] + (QK_ROPE,))

def apply_rope(x, cos, sin):
    return (x * cos + rotate_half_axial(x) * sin).astype(x.dtype)

def centred_conv3(u, w):
    up = jnp.pad(u, ((0, 0), (1, 1), (0, 0)))
    return up[:, :-2] * w[0] + up[:, 1:-1] * w[1] + up[:, 2:] * w[2]

def pool_mixer(u, w_pool, pool_scale):
    B, L, _ = u.shape
    uf = u.astype(jnp.float32).reshape(B, L, N_POOL, POOL_GROUP)
    cs = jnp.pad(jnp.cumsum(uf, axis=1), ((0, 0), (1, 0), (0, 0), (0, 0)))
    t = jnp.arange(L)
    groups = []
    for g, w in enumerate(POOL_WINDOWS):
        lo = jnp.clip(t - w // 2, 0, L)
        hi = jnp.clip(t + w // 2, 0, L)
        cnt = (hi - lo).astype(jnp.float32)[None, :, None]
        groups.append((cs[:, hi, g] - cs[:, lo, g]) / cnt - uf[:, :, g])
    p = jnp.stack(groups, axis=2).astype(u.dtype)
    y = jnp.einsum('blgc,gcd->blgd', p, w_pool).reshape(B, L, POOL_DIM)
    return y * pool_scale

def even_mixer(h, w_in, conv_w, pool_w, pool_scale, w_out):
    u = h @ w_in
    ux, ub, uc, up = jnp.split(u, [CONV_DIM, 2 * CONV_DIM, 3 * CONV_DIM], axis=-1)
    ya = ub * centred_conv3(uc * ux, conv_w)
    yb = pool_mixer(up, pool_w, pool_scale)
    return jnp.concatenate([ya, yb], axis=-1) @ w_out

def block_attention(q, k, v):
    B, Lq, H, Dq = q.shape
    nb = Lq // Q_BLOCK
    scale = Dq ** -0.5
    qb = jnp.moveaxis(q.reshape(B, nb, Q_BLOCK, H, Dq), 1, 0)

    def one(qi):
        s = jnp.einsum('bqhd,bkhd->bhqk', qi, k).astype(jnp.float32) * scale
        p = jax.nn.softmax(s, axis=-1).astype(v.dtype)
        return jnp.einsum('bhqk,bkhd->bqhd', p, v)

    o = lax.map(one, qb)
    return jnp.moveaxis(o, 0, 1).reshape(B, Lq, H * V_DIM)

def mla_keys_values(ckv, kpe, w_kv_b):
    B, L, _ = ckv.shape
    kv = (ckv @ w_kv_b).reshape(B, L, N_HEADS, QK_NOPE + V_DIM)
    k = jnp.concatenate([kv[..., :QK_NOPE], jnp.broadcast_to(kpe[:, :, None, :], (B, L, N_HEADS, QK_ROPE))], axis=-1)
    return k, kv[..., QK_NOPE:]

def fourier_mixer(u, fnet_w):
    B, L, _ = u.shape
    ug = u.astype(jnp.float32).reshape(B, L, FNET_GROUPS, FNET_GROUP_DIM)
    mu = jnp.mean(ug, axis=-1, keepdims=True)
    var = jnp.mean(jnp.square(ug - mu), axis=-1, keepdims=True)
    ug = (ug - mu) * lax.rsqrt(var + LN_EPS)
    f = jnp.fft.fft2(ug, axes=(1, 3), norm='ortho').real
    return f.reshape(B, L, FNET_DIM).astype(u.dtype) @ fnet_w

def odd_project(h, w_in, q_norm, kv_norm, w_q_b):
    B, L, _ = h.shape
    uq, ukv, upe, uf = jnp.split(h @ w_in, [Q_RANK, Q_RANK + KV_RANK, Q_RANK + KV_RANK + QK_ROPE], axis=-1)
    q = (rms_norm(uq, q_norm) @ w_q_b).reshape(B, L, N_HEADS, QK_HEAD)
    return q, rms_norm(ukv, kv_norm), upe, uf

def odd_merge(attn, uf, fnet_w, w_out):
    return jnp.concatenate([attn, fourier_mixer(uf, fnet_w)], axis=-1) @ w_out

def odd_mixer_context(h, w_in, q_norm, kv_norm, w_q_b, w_kv_b, fnet_w, w_out):
    q, ckv, kpe, uf = odd_project(h, w_in, q_norm, kv_norm, w_q_b)
    k, v = mla_keys_values(ckv, kpe, w_kv_b)
    return odd_merge(block_attention(q, k, v), uf, fnet_w, w_out), ckv, kpe

def odd_mixer_latent(h, ctx_ckv, ctx_kpe, cos, sin, w_in, q_norm, kv_norm, w_q_b, w_kv_b, fnet_w, w_out):
    q, ckv, kpe, uf = odd_project(h, w_in, q_norm, kv_norm, w_q_b)
    q = jnp.concatenate([q[..., :QK_NOPE], apply_rope(q[..., QK_NOPE:], cos[:, None], sin[:, None])], axis=-1)
    kpe = apply_rope(kpe, cos, sin)
    k_ctx, v_ctx = mla_keys_values(ctx_ckv, ctx_kpe, w_kv_b)
    k_lat, v_lat = mla_keys_values(ckv, kpe, w_kv_b)
    k = jnp.concatenate([k_ctx, k_lat], axis=1)
    v = jnp.concatenate([v_ctx, v_lat], axis=1)
    return odd_merge(block_attention(q, k, v), uf, fnet_w, w_out)

def swiglu(h, wg, wu, wd):
    return (jax.nn.silu(h @ wg) * (h @ wu)) @ wd

def moe_swiglu(h, w_router, wg, wu, wd):
    logits = (h @ w_router).astype(jnp.float32)
    top_v, top_i = lax.top_k(logits, TOP_K)
    top_w = jax.nn.softmax(top_v, axis=-1)
    gates = jnp.einsum('blk,blke->ble', top_w, jax.nn.one_hot(top_i, N_EXPERTS, dtype=jnp.float32)).astype(h.dtype)
    y = jnp.zeros_like(h)
    for e in range(N_EXPERTS):
        y = y + gates[..., e:e + 1] * swiglu(h, wg[e], wu[e], wd[e])
    return y

def setup_inputs(seed: int = 0) -> dict:
    key = jax.random.key(seed)
    ks = jax.random.split(key, 32)
    D = D_MODEL

    def nrm(k, shape, scale=1.0):
        return scale * jax.random.normal(k, shape, jnp.float32)

    return {
        "x_prompt": nrm(ks[0], (BATCH, SEQ, D)),
        "x_sample": nrm(ks[1], (DEC_BATCH, DEC_SEQ, D)),
        "cache_ckv": nrm(ks[2], (DEC_BATCH, N_ODD, PAST_LEN, KV_RANK)),
        "cache_kpe": nrm(ks[3], (DEC_BATCH, N_ODD, PAST_LEN, QK_ROPE)),
        "c": nrm(ks[4], (DEC_BATCH, D)),
        "c_ctx": nrm(ks[5], (D,)),
        "ada_w": nrm(ks[6], (DEPTH, D, 6 * D), 0.5 * D ** -0.5),
        "ada_b": nrm(ks[7], (DEPTH, 6 * D), 0.02),
        "ln_g": 1.0 + nrm(ks[8], (DEPTH, 2, D), 0.05),
        "ln_b": nrm(ks[9], (DEPTH, 2, D), 0.02),
        "ev_w_in": nrm(ks[10], (N_EVEN, D, EVEN_IN), D ** -0.5),
        "ev_conv_w": nrm(ks[11], (N_EVEN, CONV_K, CONV_DIM), CONV_K ** -0.5),
        "ev_pool_w": nrm(ks[12], (N_EVEN, N_POOL, POOL_GROUP, POOL_GROUP), POOL_GROUP ** -0.5),
        "ev_pool_scale": 1.0 + nrm(ks[13], (N_EVEN, POOL_DIM), 0.1),
        "ev_w_out": nrm(ks[14], (N_EVEN, EVEN_MIX, D), BETA * EVEN_MIX ** -0.5),
        "ffn_w_gate": nrm(ks[15], (N_EVEN, D, D_FF), D ** -0.5),
        "ffn_w_up": nrm(ks[16], (N_EVEN, D, D_FF), D ** -0.5),
        "ffn_w_down": nrm(ks[17], (N_EVEN, D_FF, D), BETA * D_FF ** -0.5),
        "od_w_in": nrm(ks[18], (N_ODD, D, ODD_IN), D ** -0.5),
        "od_q_norm": 1.0 + nrm(ks[19], (N_ODD, Q_RANK), 0.05),
        "od_kv_norm": 1.0 + nrm(ks[20], (N_ODD, KV_RANK), 0.05),
        "od_w_q_b": nrm(ks[21], (N_ODD, Q_RANK, N_HEADS * QK_HEAD), Q_RANK ** -0.5),
        "od_w_kv_b": nrm(ks[22], (N_ODD, KV_RANK, N_HEADS * (QK_NOPE + V_DIM)), KV_RANK ** -0.5),
        "od_fnet_w": nrm(ks[23], (N_ODD, FNET_DIM, FNET_DIM), FNET_DIM ** -0.5),
        "od_w_out": nrm(ks[24], (N_ODD, ODD_MIX, D), BETA * ODD_MIX ** -0.5),
        "moe_router": nrm(ks[25], (N_ODD, D, N_EXPERTS), D ** -0.5),
        "moe_w_gate": nrm(ks[26], (N_ODD, N_EXPERTS, D, D_FF_EXPERT), D ** -0.5),
        "moe_w_up": nrm(ks[27], (N_ODD, N_EXPERTS, D, D_FF_EXPERT), D ** -0.5),
        "moe_w_down": nrm(ks[28], (N_ODD, N_EXPERTS, D_FF_EXPERT, D), BETA * D_FF_EXPERT ** -0.5),
    }

def reference(x_prompt, x_sample, cache_ckv, cache_kpe, c, c_ctx, ada_w, ada_b, ln_g, ln_b,
              ev_w_in, ev_conv_w, ev_pool_w, ev_pool_scale, ev_w_out,
              ffn_w_gate, ffn_w_up, ffn_w_down,
              od_w_in, od_q_norm, od_kv_norm, od_w_q_b, od_w_kv_b, od_fnet_w, od_w_out,
              moe_router, moe_w_gate, moe_w_up, moe_w_down):
    cos, sin = axial_rope(x_sample.shape[1])
    xp, xs = x_prompt, x_sample
    ckv_layers, kpe_layers = [], []
    for l in range(DEPTH):
        i = l // 2
        mp = modulation(c_ctx, ada_w[l], ada_b[l])
        ms = modulation(c, ada_w[l], ada_b[l])
        hp = modulate(xp, mp[0], mp[1])
        hs = modulate(xs, ms[0], ms[1])
        if l % 2 == 0:
            yp = even_mixer(hp, ev_w_in[i], ev_conv_w[i], ev_pool_w[i], ev_pool_scale[i], ev_w_out[i])
            ys = even_mixer(hs, ev_w_in[i], ev_conv_w[i], ev_pool_w[i], ev_pool_scale[i], ev_w_out[i])
        else:
            yp, ckv, kpe = odd_mixer_context(hp, od_w_in[i], od_q_norm[i], od_kv_norm[i], od_w_q_b[i],
                                             od_w_kv_b[i], od_fnet_w[i], od_w_out[i])
            ys = odd_mixer_latent(hs, cache_ckv[:, i], cache_kpe[:, i], cos, sin, od_w_in[i], od_q_norm[i],
                                  od_kv_norm[i], od_w_q_b[i], od_w_kv_b[i], od_fnet_w[i], od_w_out[i])
            ckv_layers.append(ckv)
            kpe_layers.append(kpe)
        xp = post_norm(xp, yp, mp[2], ln_g[l, 0], ln_b[l, 0])
        xs = post_norm(xs, ys, ms[2], ln_g[l, 0], ln_b[l, 0])
        hp = modulate(xp, mp[3], mp[4])
        hs = modulate(xs, ms[3], ms[4])
        if l % 2 == 0:
            fp = swiglu(hp, ffn_w_gate[i], ffn_w_up[i], ffn_w_down[i])
            fs = swiglu(hs, ffn_w_gate[i], ffn_w_up[i], ffn_w_down[i])
        else:
            fp = moe_swiglu(hp, moe_router[i], moe_w_gate[i], moe_w_up[i], moe_w_down[i])
            fs = moe_swiglu(hs, moe_router[i], moe_w_gate[i], moe_w_up[i], moe_w_down[i])
        xp = post_norm(xp, fp, mp[5], ln_g[l, 1], ln_b[l, 1])
        xs = post_norm(xs, fs, ms[5], ln_g[l, 1], ln_b[l, 1])
    new_ckv = jnp.stack(ckv_layers, axis=1)
    new_kpe = jnp.stack(kpe_layers, axis=1)
    return (xp, xs, new_ckv, new_kpe)


_drawn_inputs = setup_inputs


def setup_inputs(seed=0):
    import zlib

    import numpy as np

    out = dict(_drawn_inputs(seed))
    spreads = {}
    factors = {'cache_ckv': 8.0,
     'cache_kpe': 8.0,
     'ev_pool_scale': 8.0,
     'od_q_norm': 8.0,
     'od_w_q_b': 4.576}
    for name, (base, spread) in spreads.items():
        noise = np.random.default_rng([zlib.crc32(name.encode()), seed]).standard_normal(out[name].shape)
        drawn = base * np.exp(spread * noise) if base else spread * noise
        out[name] = __import__('jax').numpy.asarray(drawn.astype(out[name].dtype))
    for name, factor in factors.items():
        out[name] = (out[name] * factor).astype(out[name].dtype)
    return out
```

```python
from contextlib import ExitStack

import numpy as np

import concourse.bass as bass
from concourse import mybir

F32 = mybir.dt.float32
I32 = mybir.dt.int32
ALU = mybir.AluOpType
ACT = mybir.ActivationFunctionType
AX = mybir.AxisListType

P = 128
D = 1024
KD = D // P
SEQ, DEC, PAST = 128, 256, 128
TOK = SEQ + DEC
NG = TOK // P
DEPTH = 2
CONV = 512
NPOOL = 4
WINDOWS = (2, 4, 8, 16)
FF = 2816
NF = FF // P
NH = 8
NOPE, ROPE, VD = 128, 64, 128
QR, KVR = 384, 256
FG, FGD = 4, 64
FD = FG * FGD
ODD_IN = QR + KVR + ROPE + FD
NE = 8
FFE = 1792
GRID_W = 64
ALPHA = float((2 * DEPTH) ** 0.25)
LN_EPS, RMS_EPS = 1e-5, 1e-6
SCALE = float((NOPE + ROPE) ** -0.5)

SLOT = 6144
PANEL = SLOT // KD
NPANEL = 6 * D // PANEL
UCOL = 256
UNITS_FF = FF // UCOL
UNITS_E = FFE // UCOL
CODES = 3 * NE
SCRATCH = 13600
TABLE = 16


def columns(parts):
    at, out = 0, {}
    for name, a in parts:
        out[name] = (at, a.shape[1])
        at += a.shape[1]
    return out, np.ascontiguousarray(np.concatenate([a for _, a in parts], 1).astype(np.float32))


def base_constants():
    n = np.arange(P)
    row = lambda v: np.tile(np.asarray(v, np.float32)[None, :], (P, 1))
    cand = [(e, r) for e in range(NE) for r in (1, 2)]
    return columns([
        ("ident", np.eye(P)),
        ("iota", row(n)),
        ("before", (n[:, None] < n[None, :]).astype(np.float32)),
        ("ones", np.ones((P, P))),
        ("expert", row(np.tile(np.arange(NE), NG))),
        ("item", row(np.arange(TABLE))),
        ("cand_code", row([e + NE * r for e, r in cand])),
        ("cand_expert", row([e for e, _ in cand])),
        ("base", row([j if j < NE else 0 for j in range(TABLE)])),
        ("eps", row([LN_EPS])),
    ])


def odd_constants():
    t = np.arange(DEC)
    half = ROPE // 2
    inv = 10000.0 ** (-np.arange(0, half, 2) / half)
    ar, ac = (t // GRID_W)[:, None] * inv, (t % GRID_W)[:, None] * inv
    ang = np.concatenate([ar, ar, ac, ac], -1)
    rot = np.zeros((ROPE, ROPE))
    q = ROPE // 4
    for h in range(2):
        for j in range(q):
            rot[h * 2 * q + q + j, h * 2 * q + j] = -1
            rot[h * 2 * q + j, h * 2 * q + q + j] = 1
    two = lambda m: np.kron(np.eye(2), m)
    dft = lambda n: 2 * np.pi * (np.outer(np.arange(n), np.arange(n)) % n) / n
    pos = lambda n: np.concatenate([np.cos(dft(n)), np.sin(dft(n))], 1) / np.sqrt(n * FGD)
    long = pos(DEC).reshape(DEC // P, P, 2 * DEC).transpose(1, 0, 2).reshape(P, -1)
    return columns([
        ("cos", np.tile(np.cos(ang).T, (2, 1))),
        ("sin", np.tile(np.sin(ang).T, (2, 1))),
        ("rot", two(rot)),
        ("chan_cos", two(np.cos(dft(FGD)))),
        ("chan_nsin", two(-np.sin(dft(FGD)))),
    ]), columns([("prompt", pos(SEQ)), ("latent", long)])


def pool_counts():
    out = np.zeros((NPOOL, TOK), np.float32)
    for w, win in enumerate(WINDOWS):
        at = 0
        for n in (SEQ, DEC):
            t = np.arange(n)
            out[w, at:at + n] = 1.0 / (np.minimum(t + win // 2, n) - np.maximum(t - win // 2, 0))
            at += n
    return out


BASE, BASE_ROWS = base_constants()
(ODD, ODD_ROWS), (DFT, DFT_ROWS) = odd_constants()


class Ring:

    def __init__(self):
        self.landed, self.used, self.units = [0] * 4, [0] * 4, {}

    def unit(self, name, slot, dmas):
        before = self.used[slot]
        self.landed[slot] += 16 * dmas
        self.used[slot] += 1
        self.units[name] = (slot, self.landed[slot], before)


class Chain:

    def __init__(self, eng, sem):
        self.eng, self.sem, self.n = eng, sem, 0

    def __call__(self, ins):
        ins.then_inc(self.sem, 1)
        self.n = self.n + 1
        self.eng.wait_ge(self.sem, self.n)


def plan():
    r = Ring()
    for p in range(NPANEL):
        r.unit(("ada", p), p % 4, 1)
    for t in range(4):
        r.unit(("evin", t), t, 1)
    r.unit(("evout", 0), 0, 1)
    r.unit(("evout", 1), 1, 1)
    for p, s in zip(range(4), (2, 3, 1, 2)):
        r.unit(("ada", NPANEL + p), s, 1)
    r.unit(("ff", 0), 0, 3)
    ff = (list(r.landed), list(r.used))
    for i in range((UNITS_FF - 1) // 2):
        r.unit(("ffloop", i, 0), 3, 3)
        r.unit(("ffloop", i, 1), 0, 3)
    for p, s in zip(range(4, 8), (1, 2, 3, 0)):
        r.unit(("ada", NPANEL + p), s, 1)
    r.unit(("odin", 0), 1, 1)
    r.unit(("odin", 1), 2, 1)
    r.unit(("odout", 0), 0, 1)
    r.unit(("odout", 1), 1, 1)
    r.unit(("moe", 0, 0), 2, 3)
    pair = (list(r.landed), list(r.used))
    for i in range(NH // 2):
        r.unit(("pair", i), 3, PAIR_DMAS)
    for u in range(1, UNITS_E):
        r.unit(("moe", 0, u), MOE_SLOTS[u], 3)
    return r, ff, pair


MOE_SLOTS = (2, 3, 0, 1, 2, 3, 0)
MOE_USES = [MOE_SLOTS.count(s) for s in range(4)]
PAIR_DMAS = 3 + 3 + 2 + 2


def build(nc, x_prompt, x_sample, cache_ckv, cache_kpe, c, c_ctx, ada_w, ada_b, ln_g, ln_b, ev_w_in, ev_conv_w,
          ev_pool_w, ev_pool_scale, ev_w_out, ffn_w_gate, ffn_w_up, ffn_w_down, od_w_in, od_q_norm, od_kv_norm,
          od_w_q_b, od_w_kv_b, od_fnet_w, od_w_out, moe_router, moe_w_gate, moe_w_up, moe_w_down,
          base_rows, odd_rows, dft_rows, pool_inv, y_prompt, y_sample, new_ckv, new_kpe):
    ctx = ExitStack()
    with ctx:
        def sb(name, shape, dt=F32):
            return ctx.enter_context(nc.sbuf_tensor("sb_" + name, shape, dt))

        def sem(name):
            return ctx.enter_context(nc.semaphore(name))

        mod_rows = nc.dram_tensor("mod_rows", (DEPTH, 2, 6 * D), F32, kind="Internal").ap()

        WR = sb("ring", [P, 4, SLOT])
        X = sb("x", [P, NG, D])
        HT = sb("ht", [P, KD, TOK])
        GB = sb("gate_rows", [P, 2, D])
        LG = sb("ln_gain", [P, D])
        LB = sb("ln_bias", [P, D])
        T = sb("temp", [P, D])
        CST = sb("constants", [P, BASE_ROWS.shape[1]])
        MT = sb("mod_cols", [P, DEPTH, 6 * KD, 2])
        ROWS = sb("rows", [35, P])
        COLS = sb("cols", [P, 35])
        SC = sb("silu_cond", [P, KD, 2])
        STG = sb("mod_stage", [2, 2, PANEL])
        BROW = sb("mod_bias", [2, PANEL])
        SM = sb("small", [P, 160])
        TAB = sb("item_table", [1, 1 + 2 * TABLE], I32)
        SCR = sb("scratch", [P, SCRATCH])
        PS = ctx.enter_context(nc.psum_tensor("ps", [P, 8, 512], F32))

        def cst(name, rows=P):
            at, n = BASE[name]
            return CST[0:rows, at:at + n]

        ident = cst("ident")

        def carve(*parts):
            at, out = 0, []
            for n in parts:
                out.append(SCR[:, at:at + n])
                at += n
            assert at <= SCRATCH, at
            return out

        ZW, UW = SEQ + DEC + 4, SEQ + DEC + 32
        UX, UB, Z, UP, ICNT, SA, SBB, CV, MIX, PW = carve(
            4 * TOK, 4 * TOK, 4 * ZW, 4 * UW, 4 * TOK, UW, UW, ZW, 8 * TOK, 4 * P)
        PP = UX
        r4 = lambda a, n: a.rearrange("p (a n) -> p a n", a=n)
        UX, UB, Z, UP, ICNT, PP, MIX, PW = (r4(a, n) for a, n in
                                            ((UX, 4), (UB, 4), (Z, 4), (UP, 4), (ICNT, 4), (PP, 4), (MIX, 8), (PW, 4)))
        SEGZ = ((0, 1, SEQ), (SEQ, SEQ + 3, DEC))
        SEGU = ((0, 8, SEQ), (SEQ, SEQ + 24, DEC))
        SIL, HF = carve(TOK, 2 * TOK)
        HF = r4(HF, 2)
        (U, KDUP, CK, QHT, CKT, KPT, OC, FNW, GT, AT) = carve(
            NG * ODD_IN, 4 * P, KVR, 3 * TOK, 2 * 512, 512, ODD_ROWS.shape[1], 2 * FD, 2 * TOK, 4992)
        DC = AT[:, 2304:2304 + DFT_ROWS.shape[1]]
        KVN = AT[:, 3600:3600 + KVR]
        U, KDUP, QHT, CKT, FNW, GT = (r4(a, n) for a, n in ((U, NG), (KDUP, 4), (QHT, 3), (CKT, 2), (FNW, 2), (GT, 2)))
        FA = r4(AT[:, 0:2 * 768], 2)
        FT = r4(AT[:, 1536:1536 + 2 * TOK], 2)
        cut = np.cumsum([0, 2 * TOK, TOK, 256, 1024, 1024, 2 * TOK, 2 * TOK])
        QN, QP, RT, KT, VV, PB, PTB = (AT[:, int(a):int(b)] for a, b in zip(cut[:-1], cut[1:]))
        QN, KT, VV, PB, PTB = (r4(a, n) for a, n in ((QN, 2), (KT, 2), (VV, 4), (PB, 2), (PTB, 2)))
        odc = lambda name: OC[:, ODD[name][0]:ODD[name][0] + ODD[name][1]]
        dft = lambda name: DC[:, DFT[name][0]:DFT[name][0] + DFT[name][1]]
        (HK, YACC, XE, PM, PG, PT, ESIL, EH, EHT, YSB, POSA, GA, ROUT, MS) = carve(
            NG * D, NG * D, D, TOK, TOK, TOK, UCOL, UCOL, UCOL, D, CODES * NG, CODES * NG, KD * NE, 900)
        HK, YACC, XE, PM, PG, PT = (r4(a, n) for a, n in ((HK, NG), (YACC, NG), (XE, KD), (PM, NG), (PG, NG), (PT, NG)))
        EHT = r4(EHT, 2)

        landed = [sem(f"landed{s}") for s in range(4)]
        used = [sem(f"used{s}") for s in range(4)]
        names = """cst_in rows_in x_in brow_in stored0 stored1 lnp_in pw_in icnt_in oddc_in cache_in kvn_in
            fnw_in rout_in out_done kv_out rows_t cols_ready sc_ready mm_a mm_b st_a st_b cols_t cols_done mt_ready
            xt_t ht_a ht_d u_ps u_act u_dve z_pad mix_conv pp_ready pm_ps mix_pool y_ps var_ready sd_ready ln_x
            g_ps up_ps sil ff_h odi_ps odu ssq uvar usd odn kd_ready odt_ps odt_a rot_ps kpt_ready f1_ps fa f2_ps ft
            f3_ps gt pj_ps pj_a pj_d qrot_ps qp_ready s_ps nmax e_done p_ready pt_ps pt_ready o_ps o_ready
            lg_ps hkt_ps hk d_ready ex_ready m_ready pos_ps tab_ready pos_ready q_ready
            gu_ps esil eh t_ps eht yd ysb pg_ready ptt_ps pt_sb cb_ps cb_done mp_ready disp_ps xe_done
            dve_chain act_chain pool_chain dve_tail""".split()
        s = {n: sem(n) for n in names}
        (cst_in, rows_in, x_in, brow_in, stored0, stored1, lnp_in, pw_in, icnt_in, oddc_in, cache_in, kvn_in,
         fnw_in, rout_in, out_done, kv_out, rows_t, cols_ready, sc_ready, mm_a, mm_b, st_a, st_b, cols_t, cols_done, mt_ready,
         xt_t, ht_a, ht_d, u_ps, u_act, u_dve, z_pad, mix_conv, pp_ready, pm_ps, mix_pool, y_ps, var_ready, sd_ready,
         ln_x, g_ps, up_ps, sil, ff_h, odi_ps, odu, ssq, uvar, usd, odn, kd_ready, odt_ps, odt_a, rot_ps, kpt_ready,
         f1_ps, fa, f2_ps, ft, f3_ps, gt, pj_ps, pj_a, pj_d, qrot_ps, qp_ready, s_ps, nmax, e_done, p_ready, pt_ps,
         pt_ready, o_ps, o_ready, lg_ps, hkt_ps, hk, d_ready, ex_ready, m_ready, pos_ps, tab_ready, pos_ready,
         q_ready, gu_ps, esil, eh, t_ps, eht, yd, ysb, pg_ready, ptt_ps, pt_sb, cb_ps, cb_done, mp_ready, disp_ps,
         xe_done, dve_chain, act_chain, pool_chain, dve_tail) = (s[n] for n in names)
        stored = (stored0, stored1)

        ring, ff_base, pair_base = plan()
        FF_ITERS = (UNITS_FF - 1) // 2
        moe_landed = ring.landed
        moe_used = ring.used
        ADA_GROUPS = (range(0, NPANEL), range(NPANEL, NPANEL + 4), range(NPANEL + 4, 2 * NPANEL))
        COMBOS = [(h, qt) for h in range(2) for qt in range(NG)]
        NC6 = len(COMBOS)

        def keys(qt):
            return (0, 1) if qt == 0 else (1, 4)

        def slot(name):
            return WR[:, ring.units[name][0], :]

        def wait_unit(eng, name):
            sl, land, _ = ring.units[name]
            eng.wait_ge(landed[sl], land)

        def more_items(eng):
            eng.wait_ge(tab_ready, 1)
            return eng.value_load(TAB[0:1, 0:1], min_val=NE - 1, max_val=TABLE - 4)

        block = ctx.enter_context(nc.Block())

        @block.sync
        def _(sp):
            def free(name):
                sl, _, before = ring.units[name]
                if before:
                    sp.wait_ge(used[sl], before)

            def panel(dst, src, n, k, name):
                sp.dma_start(dst[:, 0:k * n].rearrange("p (k n) -> p k n", k=k),
                             src.rearrange("(k p) n -> p k n", p=P)).then_inc(landed[ring.units[name][0]], 16)

            def load(name, src):
                free(name)
                rows, n = src.shape
                panel(slot(name), src, n, rows // P, name)

            def mlp(sl, gate, up, down):
                gu = WR[:, sl, 0:4096].rearrange("p (k n) -> p k n", k=KD)
                sp.dma_start(gu[:, :, 0:UCOL], gate).then_inc(landed[sl], 16)
                sp.dma_start(gu[:, :, UCOL:2 * UCOL], up).then_inc(landed[sl], 16)
                sp.dma_start(WR[:, sl, 4096:6144].rearrange("p (k n) -> p k n", k=2), down).then_inc(landed[sl], 16)

            fg = ffn_w_gate[0].rearrange("(k p) n -> p k n", p=P)
            fu = ffn_w_up[0].rearrange("(k p) n -> p k n", p=P)
            fd = ffn_w_down[0].rearrange("(k p) n -> p k n", p=P)

            def ff_unit(sl, u):
                mlp(sl, fg[:, :, bass.ds(u * UCOL, UCOL)], fu[:, :, bass.ds(u * UCOL, UCOL)], fd[:, bass.ds(u * 2, 2), :])

            def moe_unit(sl, e, u):
                one = bass.ds(e, 1)
                mlp(sl, moe_w_gate[0, one, :, u * UCOL:(u + 1) * UCOL].rearrange("e (k p) n -> p (e k) n", p=P),
                    moe_w_up[0, one, :, u * UCOL:(u + 1) * UCOL].rearrange("e (k p) n -> p (e k) n", p=P),
                    moe_w_down[0, one, u * UCOL:(u + 1) * UCOL, :].rearrange("e (k p) n -> p (e k) n", p=P))

            def ada(n):
                l, p = divmod(n, NPANEL)
                load(("ada", n), ada_w[l, :, p * PANEL:(p + 1) * PANEL])

            for n in ADA_GROUPS[0]:
                ada(n)
                if n == 0:
                    sp.dma_start(X[:, 0, :], x_prompt[0]).then_inc(x_in, 16)
                    sp.dma_start(X[:, 1:NG, :], x_sample[0].rearrange("(g p) d -> p g d", p=P)).then_inc(x_in, 16)
            for t in range(4):
                load(("evin", t), ev_w_in[0, :, t * 512:(t + 1) * 512])
            for t in range(2):
                load(("evout", t), ev_w_out[0, t * 512:(t + 1) * 512, :])
            for n in ADA_GROUPS[1]:
                ada(n)
            free(("ff", 0))
            ff_unit(0, 0)
            with sp.Fori(0, FF_ITERS) as i:
                sp.wait_ge(used[3], i + ff_base[1][3])
                ff_unit(3, i * 2 + 1)
                sp.wait_ge(used[0], i + ff_base[1][0])
                ff_unit(0, i * 2 + 2)
            for n in ADA_GROUPS[2]:
                ada(n)
            for t in range(2):
                load(("odin", t), od_w_in[0, :, t * 480:(t + 1) * 480])
            for t in range(2):
                load(("odout", t), od_w_out[0, t * 640:(t + 1) * 640, :])
            free(("moe", 0, 0))
            moe_unit(2, 0, 0)
            qb = od_w_q_b[0].rearrange("(k p) (h c) -> p k h c", p=P, h=NH)
            kvb = od_w_kv_b[0].rearrange("(k p) (h c) -> p k h c", p=P, h=NH)
            with sp.Fori(0, NH // 2) as i:
                sp.wait_ge(used[3], i + pair_base[1][3])
                two = bass.ds(i * 2, 2)
                for k in range(3):
                    sp.dma_start(WR[:, 3, 256 * k:256 * (k + 1)].rearrange("p (h c) -> p h c", h=2),
                                 qb[:, k, two, 0:NOPE]).then_inc(landed[3], 16)
                    sp.dma_start(WR[:, 3, 768 + P * k:768 + P * (k + 1)].rearrange("p (h c) -> p h c", h=2),
                                 qb[:, k, two, NOPE:NOPE + ROPE]).then_inc(landed[3], 16)
                for k in range(2):
                    sp.dma_start(WR[:, 3, 1152 + 256 * k:1408 + 256 * k].rearrange("p (h c) -> p h c", h=2),
                                 kvb[:, k, two, 0:NOPE]).then_inc(landed[3], 16)
                    sp.dma_start(WR[:, 3, 1664 + 256 * k:1920 + 256 * k].rearrange("p (h c) -> p h c", h=2),
                                 kvb[:, k, two, NOPE:NOPE + VD]).then_inc(landed[3], 16)
            for u in range(1, UNITS_E):
                free(("moe", 0, u))
                moe_unit(MOE_SLOTS[u], 0, u)
            more = more_items(sp)
            with sp.Fori(0, more) as j:
                e = sp.value_load(TAB[0:1, bass.ds(j + 2 + TABLE, 1)], min_val=0, max_val=NE - 1)
                seen = [0] * 4
                for u in range(UNITS_E):
                    sl = MOE_SLOTS[u]
                    sp.wait_ge(used[sl], j * MOE_USES[sl] + moe_used[sl] + seen[sl])
                    seen[sl] += 1
                    moe_unit(sl, e, u)
            for g in range(NG):
                sp.wait_ge(ln_x, 3 * NG + g + 1)
                out = y_prompt[0] if g == 0 else y_sample[0, (g - 1) * P:g * P, :]
                sp.dma_start(out, X[:, g, :]).then_inc(out_done, 16)
            sp.wait_ge(out_done, 16 * NG)
            sp.wait_ge(kv_out, 32)

        @block.gpsimd
        def _(pool):
            ch = Chain(pool, pool_chain)
            pool.dma_start(CST[:, :], base_rows).then_inc(cst_in, 16)
            pool.dma_start(ROWS[0:12, :], ev_conv_w[0].rearrange("k (t p) -> (k t) p", p=P)).then_inc(rows_in, 16)
            pool.dma_start(ROWS[12:16, :], ev_pool_scale[0].rearrange("(t p) -> t p", p=P)).then_inc(rows_in, 16)
            pool.dma_start(ROWS[16:19, :], od_q_norm[0].rearrange("(t p) -> t p", p=P)).then_inc(rows_in, 16)
            pool.dma_start(ROWS[19:27, :], c_ctx.rearrange("(t p) -> t p", p=P)).then_inc(rows_in, 16)
            pool.dma_start(ROWS[27:35, :], c[0].rearrange("(t p) -> t p", p=P)).then_inc(rows_in, 16)
            pool.dma_start(PW, ev_pool_w[0].rearrange("g c d -> c g d")).then_inc(pw_in, 16)
            pool.dma_start(ICNT, pool_inv.partition_broadcast(P)).then_inc(icnt_in, 16)

            def ada_io(group):
                def bias(n):
                    l, p = divmod(n, NPANEL)
                    if n:
                        pool.wait_ge(st_b, n)
                        pool.wait_ge(st_a, n)
                    pool.dma_start(BROW[:, :], ada_b[l, p * PANEL:(p + 1) * PANEL].partition_broadcast(2))\
                        .then_inc(brow_in, 16)

                for n in group:
                    bias(n)
                    l, p = divmod(n, NPANEL)
                    pool.wait_ge(st_b, n + 1)
                    pool.wait_ge(st_a, n + 1)
                    pool.dma_start(mod_rows[l, :, p * PANEL:(p + 1) * PANEL], STG[:, n % 2, :])\
                        .then_inc(stored[n % 2], 16)

            def ln_params(l, j):
                done = 2 * l + j
                if done:
                    pool.wait_ge(ln_x, NG * done)
                for b in range(2):
                    pool.wait_ge(stored[b], 16 * NPANEL // 2 * (l + 1))
                at = (3 * j + 2) * D
                pool.dma_start(LG[:, :], ln_g[l, j].partition_broadcast(P)).then_inc(lnp_in, 16)
                pool.dma_start(LB[:, :], ln_b[l, j].partition_broadcast(P)).then_inc(lnp_in, 16)
                pool.dma_start(GB[:, :, :], mod_rows[l, :, at:at + D].partition_broadcast(P)).then_inc(lnp_in, 16)

            ada_io(ADA_GROUPS[0])
            ln_params(0, 0)
            pool.wait_ge(icnt_in, 16)
            pool.wait_ge(z_pad, 2)
            pool.wait_ge(u_dve, 4)
            for g, win in enumerate(WINDOWS):
                pool.wait_ge(u_act, 8 + g + 1)
                src, width, step, bufs = UP[:, g, :], UW, 1, (SA, SBB)
                while step < win:
                    width -= step
                    dst = bufs[0]
                    ch(pool.tensor_tensor(dst[:, 0:width], src[:, 0:width], src[:, step:step + width], ALU.add))
                    src, bufs, step = dst, (bufs[1], bufs[0]), step * 2
                for tok, at, n in SEGU:
                    lo = at - win // 2
                    ch(pool.tensor_tensor(PP[:, g, tok:tok + n], src[:, lo:lo + n], ICNT[:, g, tok:tok + n], ALU.mult))
                for tok, at, n in SEGU:
                    last = pool.tensor_tensor(PP[:, g, tok:tok + n], PP[:, g, tok:tok + n], UP[:, g, at:at + n], ALU.subtract)
                    if tok == 0:
                        ch(last)
                last.then_inc(pp_ready, 1)
            ada_io(ADA_GROUPS[1])
            pool.wait_ge(ln_x, NG)
            pool.wait_ge(g_ps, 1)
            pool.dma_start(OC, odd_rows).then_inc(oddc_in, 16)
            pool.dma_start(DC, dft_rows).then_inc(oddc_in, 16)
            pool.dma_start(KVN, od_kv_norm[0].partition_broadcast(P)).then_inc(kvn_in, 16)
            pool.dma_start(FNW, od_fnet_w[0].rearrange("(k p) n -> p k n", p=P)).then_inc(fnw_in, 16)
            pool.dma_start(CK, cache_ckv[0, 0]).then_inc(cache_in, 16)
            for b in range(2):
                pool.dma_start(KDUP[:, 1, b * ROPE:(b + 1) * ROPE], cache_kpe[0, 0]).then_inc(cache_in, 16)
            pool.wait_ge(ln_x, NG)
            pool.dma_start(LG[:, :], ln_g[0, 1].partition_broadcast(P)).then_inc(lnp_in, 16)
            pool.dma_start(LB[:, :], ln_b[0, 1].partition_broadcast(P)).then_inc(lnp_in, 16)
            pool.dma_start(GB[:, :, :], mod_rows[0, :, 5 * D:6 * D].partition_broadcast(P)).then_inc(lnp_in, 16)
            ada_io(ADA_GROUPS[2])
            ln_params(1, 0)
            for p in range(2 * NG):
                g, b = divmod(p, 2)
                if p == 0:
                    pool.wait_ge(odu, 2 * NG)
                last = pool.tensor_copy(KDUP[:, g if g == 0 else g + 1, b * ROPE:(b + 1) * ROPE],
                                        U[:, g, QR + KVR:QR + KVR + ROPE])
            last.then_inc(kd_ready, 1)
            pool.wait_ge(odn, 2)
            pool.dma_start(new_ckv[0, 0], U[:, 0, QR:QR + KVR]).then_inc(kv_out, 16)
            pool.dma_start(new_kpe[0, 0], U[:, 0, QR + KVR:QR + KVR + ROPE]).then_inc(kv_out, 16)
            ln_params(1, 1)
            pool.wait_ge(xt_t, 4 * 2 * NG)
            pool.dma_start(ROUT.rearrange("p (k e) -> p k e", k=KD),
                           moe_router[0].rearrange("(k p) e -> p k e", p=P)).then_inc(rout_in, 16)

        @block.scalar
        def _(act):
            act.wait_ge(cols_ready, 1)
            nc.scalar.activation(SC[:, :, :].rearrange("p k c -> p c k"),
                                 COLS[:, 19:35].rearrange("p (c k) -> p c k", c=2), ACT.Silu).then_inc(sc_ready, 1)

            def sqrt_of(n, at, count):
                act.wait_ge(var_ready, n)
                nc.scalar.activation(SM[:, at + count:at + 2 * count], SM[:, at:at + count], ACT.Sqrt).then_inc(sd_ready, 1)

            def modulate(st):
                l, j = divmod(st, 2)
                act.wait_ge(mt_ready, l + 1)
                for q in (0, 1, 2, 3, 5):
                    g, half = divmod(q, 2)
                    cond = min(g, 1)
                    act.wait_ge(xt_t, 2 * NG * st + q + 1)
                    for b in range(4):
                        k = half * 4 + b
                        last = nc.scalar.activation(HT[:, k, g * P:(g + 1) * P], PS[:, q, b * P:(b + 1) * P], ACT.Identity,
                                                    scale=MT[:, l, (3 * j + 1) * KD + k, cond:cond + 1],
                                                    bias=MT[:, l, 3 * j * KD + k, cond:cond + 1])
                    last.then_inc(ht_a, 1)

            modulate(0)
            for t in (0, 1, 2, 3, 4, 5, 6, 7, 12, 13, 14, 15):
                act.wait_ge(u_ps, t + 1)
                if t < 8:
                    dst = (UX, UB)[t // 4]
                    nc.scalar.copy(dst[:, t % 4, :], PS[:, t % 4, 0:TOK]).then_inc(u_act, 1)
                else:
                    act.wait_ge(z_pad, 2)
                    for tok, at, n in SEGU:
                        last = nc.scalar.copy(UP[:, t % 4, at:at + n], PS[:, t % 4, tok:tok + n])
                    last.then_inc(u_act, 1)
            for g in range(NPOOL):
                act.wait_ge(pm_ps, g + 1)
                nc.scalar.activation(MIX[:, 4 + g, :], PS[:, 6 + g % 2, 0:TOK], ACT.Identity,
                                     scale=COLS[:, 12 + g:13 + g]).then_inc(mix_pool, 1)
            sqrt_of(1, 0, NG)
            modulate(1)

            def ff_silu(f):
                act.wait_ge(g_ps, f + 1)
                nc.scalar.activation(SIL, PS[:, 6, 0:TOK], ACT.Silu).then_inc(sil, 1)

            ff_silu(0)
            ff_silu(1)
            with act.Fori(0, FF_ITERS) as i:
                for b in range(4):
                    ff_silu(i * 4 + 2 + b)
            sqrt_of(2, 0, NG)
            modulate(2)
            for q in range(2 * NG):
                h, g = divmod(q, NG)
                act.wait_ge(odi_ps, q + 1)
                nc.scalar.copy(U[:, g, h * 480:(h + 1) * 480], PS[:, q, 0:480]).then_inc(odu, 1)
            act.wait_ge(odu, 2 * NG)
            for g in range(NG):
                for b, (lo, n) in enumerate(((0, QR), (QR, KVR))):
                    last = nc.scalar.activation(T[:, b * 512:b * 512 + n], U[:, g, lo:lo + n], ACT.Square,
                                                accum_out=SM[:, 40 + 3 * b + g:41 + 3 * b + g])
                    act_last = last
                    if (g, b) != (NG - 1, 1):
                        act_last.then_inc(act_chain, 1)
                        act.wait_ge(act_chain, 2 * g + b + 1)
            act_last.then_inc(ssq, 1)
            sqrt_of(3, 64, 18)
            for q in range(6):
                act.wait_ge(odt_ps, q + 1)
                if q < 3:
                    ins = nc.scalar.activation(QHT[:, q, :], PS[:, q, 0:TOK], ACT.Identity, scale=COLS[:, 16 + q:17 + q])
                elif q < 5:
                    ins = nc.scalar.copy(CKT[:, q - 3, :], PS[:, q, :])
                else:
                    ins = nc.scalar.copy(KPT, PS[:, q, :])
                ins.then_inc(odt_a, 1)
            act.wait_ge(o_ready, 1)
            with act.Fori(0, NH // 2) as i:
                for q in range(3):
                    act.wait_ge(pj_ps, i * 7 + q + 1)
                    nc.scalar.copy(QN[:, q, :] if q < 2 else QP, PS[:, q, 0:TOK]).then_inc(pj_a, 1)
                for cc in range(NC6 + 2):
                    if cc < NC6:
                        n = P * (keys(COMBOS[cc][1])[1] - keys(COMBOS[cc][1])[0])
                        act.wait_ge(nmax, i * NC6 + cc + 1)
                        nc.scalar.activation(PB[:, cc % 2, 0:n], PS[:, cc % 2, 0:n], ACT.Exp, scale=SCALE,
                                             bias=SM[:, 104 + cc % 2:105 + cc % 2],
                                             accum_out=SM[:, 106 + cc % 2:107 + cc % 2]).then_inc(e_done, 1)
                    if cc >= 2:
                        b = cc - 2
                        n = P * (keys(COMBOS[b][1])[1] - keys(COMBOS[b][1])[0])
                        act.wait_ge(pt_ps, i * NC6 + b + 1)
                        nc.scalar.copy(PTB[:, b % 2, 0:n], PS[:, 2 + b % 2, 0:n]).then_inc(pt_ready, 1)
            sqrt_of(4, 0, NG)
            modulate(3)
            for q in range(2 * NG):
                g, half = divmod(q, 2)
                act.wait_ge(hkt_ps, q + 1)
                nc.scalar.copy(HK[:, g, half * 512:(half + 1) * 512], PS[:, 1 + q, :]).then_inc(hk, 1)
            act.wait_ge(d_ready, 1)
            nc.scalar.activation(MS[:, 3:6], MS[:, 0:3], ACT.Exp).then_inc(ex_ready, 1)

            def dispatched(i):
                act.wait_ge(disp_ps, i + 1)
                for b in range(2):
                    last = nc.scalar.copy(XE[:, 4 * b:4 * b + 4, :].rearrange("p a n -> p (a n)"), PS[:, 4 + b, :])
                last.then_inc(xe_done, 1)

            def y_out(i):
                act.wait_ge(yd, i)
                nc.scalar.copy(YSB, PS[:, 2:4, :].rearrange("p a n -> p (a n)")).then_inc(ysb, 1)

            def item(i, first):
                for u in range(UNITS_E):
                    act.wait_ge(gu_ps, i * UNITS_E + u + 1)
                    nc.scalar.activation(ESIL, PS[:, 0, 0:UCOL], ACT.Silu).then_inc(esil, 1)
                    if u == 0 and not first:
                        y_out(i)
                    if u == UNITS_E - 1:
                        dispatched(i + 1)
                    act.wait_ge(t_ps, i * UNITS_E + u + 1)
                    nc.scalar.copy(EHT.rearrange("p a n -> p (a n)"), PS[:, 1, 0:UCOL]).then_inc(eht, 1)

            more = more_items(act)
            dispatched(0)
            item(0, True)
            with act.Fori(0, more) as j:
                item(j + 1, False)
            y_out(more + 1)
            sqrt_of(5, 0, NG)

        @block.vector
        def _(dve):
            ch = Chain(dve, dve_chain)
            V = nc.vector
            for ct in range(4):
                V.memset(Z[:, ct, :], 0.0)
                V.memset(UP[:, ct, :], 0.0).then_inc(z_pad, 1) if ct >= 2 else V.memset(UP[:, ct, :], 0.0)
            dve.wait_ge(z_pad, 2)
            dve.wait_ge(rows_t, 1)
            V.tensor_copy(COLS[:, :], PS[:, 0, 0:35]).then_inc(cols_ready, 1)

            def ada(group):
                def cols(n):
                    l, p = divmod(n, NPANEL)
                    k = PANEL // P
                    dve.wait_ge(cols_t, n + 1)
                    V.tensor_copy(MT[:, l, p * k:(p + 1) * k, :],
                                  PS[:, 7, 384:384 + 2 * k].rearrange("p (k c) -> p k c", c=2)).then_inc(cols_done, 1)

                for n in group:
                    dve.wait_ge(mm_a, n + 1)
                    dve.wait_ge(brow_in, 16 * (n + 1))
                    if n >= 2:
                        dve.wait_ge(stored[n % 2], 16 * (n // 2))
                        dve.wait_ge(cols_t, n - 1)
                    V.tensor_tensor(STG[:, n % 2, 0:384], PS[0:2, 6, 0:384], BROW[:, 0:384], ALU.add).then_inc(st_a, 1)
                    if n > group[0]:
                        cols(n - 1)
                    dve.wait_ge(mm_b, n + 1)
                    V.tensor_tensor(STG[:, n % 2, 384:768], PS[0:2, 7, 0:384], BROW[:, 384:768], ALU.add)\
                        .then_inc(st_b, 1)
                cols(group[-1])
                l, p = divmod(group[-1], NPANEL)
                if p == NPANEL - 1:
                    dve.wait_ge(cols_done, group[-1] + 1)
                    for j in range(2):
                        part = MT[:, l, (3 * j + 1) * KD:(3 * j + 2) * KD, :]
                        last = V.tensor_scalar(part, part, 1.0, None, ALU.add)
                    last.then_inc(mt_ready, 1)

            def rsqrt(n, at, count):
                v, r, w = SM[:, at:at + count], SM[:, at + count:at + 2 * count], SM[:, 112:112 + count]
                dve.wait_ge(sd_ready, n)
                ch(V.reciprocal(r, r))
                ch(V.tensor_tensor(w, v, r, ALU.mult))
                ch(V.tensor_tensor(w, w, r, ALU.mult))
                ch(V.tensor_scalar(w, w, -0.5, 1.5, ALU.mult, ALU.add))
                ch(V.tensor_tensor(r, r, w, ALU.mult))

            def layer_norm(st, n_sd, y_of):
                dve.wait_ge(lnp_in, 48 * (st + 1))
                for g in range(NG):
                    y = y_of(g)
                    ch(V.tensor_tensor(T[:, :], y, GB[:, min(g, 1), :], ALU.mult))
                    ch(V.scalar_tensor_tensor(X[:, g, :], X[:, g, :], ALPHA, T[:, :], ALU.mult, ALU.add))
                    for b in range(2):
                        ch(V.bn_stats(SM[:, 16 + 6 * b:22 + 6 * b], X[:, g, b * 512:(b + 1) * 512]))
                    ch(V.bn_aggr(SM[:, 28 + 2 * g:30 + 2 * g], SM[:, 16:28]))
                V.tensor_scalar(SM[:, 0:NG], SM[:, 29:29 + 2 * NG:2], LN_EPS, None, ALU.add).then_inc(var_ready, 1)
                rsqrt(n_sd, 0, NG)
                for g in range(NG):
                    x = X[:, g, :]
                    ch(V.tensor_scalar(x, x, SM[:, 28 + 2 * g:29 + 2 * g], SM[:, NG + g:NG + g + 1], ALU.subtract, ALU.mult))
                    ch(V.tensor_tensor(x, x, LG[:, :], ALU.mult))
                    V.tensor_tensor(x, x, LB[:, :], ALU.add).then_inc(ln_x, 1)
                dve.wait_ge(ln_x, NG * (st + 1))

            def y_psum(st):
                def y(g):
                    dve.wait_ge(y_ps, NG * st + g + 1)
                    return PS[:, 2 * g:2 * g + 2, :].rearrange("p a n -> p (a n)")
                return y

            def modulate(st):
                l, j = divmod(st, 2)
                dve.wait_ge(mt_ready, l + 1)
                dve.wait_ge(xt_t, 2 * NG * st + 5)
                for k in range(4):
                    last = V.tensor_scalar(HT[:, k, 2 * P:3 * P], PS[:, 4, k * P:(k + 1) * P],
                                           MT[:, l, (3 * j + 1) * KD + k, 1:2], MT[:, l, 3 * j * KD + k, 1:2],
                                           ALU.mult, ALU.add)
                last.then_inc(ht_d, 1)

            ada(ADA_GROUPS[0])
            modulate(0)
            for ct in range(4):
                dve.wait_ge(u_ps, 8 + ct + 1)
                dve.wait_ge(u_act, 8)
                for tok, at, n in SEGZ:
                    last = V.tensor_tensor(Z[:, ct, at:at + n], PS[:, ct, tok:tok + n], UX[:, ct, tok:tok + n], ALU.mult)
                last.then_inc(u_dve, 1)
            dve.wait_ge(u_dve, 4)
            for ct in range(4):
                w = ZW - 2
                tap = lambda k: COLS[:, 4 * k + ct:4 * k + ct + 1]
                if ct:
                    dve.wait_ge(mix_conv, ct)
                ch(V.tensor_scalar(CV[:, 0:w], Z[:, ct, 0:w], tap(0), None, ALU.mult))
                ch(V.scalar_tensor_tensor(CV[:, 0:w], Z[:, ct, 1:1 + w], tap(1), CV[:, 0:w], ALU.mult, ALU.add))
                ch(V.scalar_tensor_tensor(CV[:, 0:w], Z[:, ct, 2:2 + w], tap(2), CV[:, 0:w], ALU.mult, ALU.add))
                for tok, at, n in SEGZ:
                    last = V.tensor_tensor(MIX[:, ct, tok:tok + n], CV[:, at - 1:at - 1 + n], UB[:, ct, tok:tok + n], ALU.mult)
                last.then_inc(mix_conv, 1)
            layer_norm(0, 1, y_psum(0))
            modulate(1)
            ada(ADA_GROUPS[1])

            def ff_act(f, b):
                dve.wait_ge(sil, f + 1)
                dve.wait_ge(up_ps, f + 1)
                V.tensor_tensor(HF[:, b, :], SIL, PS[:, 7, 0:TOK], ALU.mult).then_inc(ff_h, 1)

            ff_act(0, 0)
            ff_act(1, 1)
            with dve.Fori(0, FF_ITERS) as i:
                for b in range(4):
                    ff_act(i * 4 + 2 + b, b % 2)
            layer_norm(1, 2, y_psum(1))
            ada(ADA_GROUPS[2])
            modulate(2)

            dve.wait_ge(odu, 2 * NG)
            f0 = QR + KVR + ROPE
            dve.wait_ge(ssq, 1)
            for g in range(NG):
                for b in range(FG):
                    at = 6 * (g * FG + b)
                    ch(V.bn_stats(T[:, at:at + 6], U[:, g, f0 + b * FGD:f0 + (b + 1) * FGD]))
                    ch(V.bn_aggr(T[:, 100 + at:102 + at], T[:, at:at + 6]))
            ch(V.tensor_scalar(SM[:, 64:67], SM[:, 40:43], 1.0 / QR, RMS_EPS, ALU.mult, ALU.add))
            ch(V.tensor_scalar(SM[:, 67:70], SM[:, 43:46], 1.0 / KVR, RMS_EPS, ALU.mult, ALU.add))
            V.tensor_scalar(SM[:, 70:82], T[:, 101:101 + 72:6], LN_EPS, None, ALU.add).then_inc(var_ready, 1)
            dve.wait_ge(var_ready, 3)
            rsqrt(3, 64, 18)
            for g in range(NG):
                last = V.tensor_scalar(U[:, g, 0:QR], U[:, g, 0:QR], SM[:, 82 + g:83 + g], None, ALU.mult)
            last.then_inc(odn, 1)
            dve.wait_ge(kvn_in, 16)
            for g in range(NG):
                last = V.scalar_tensor_tensor(U[:, g, QR:QR + KVR], U[:, g, QR:QR + KVR], SM[:, 85 + g:86 + g], KVN,
                                              ALU.mult, ALU.mult)
            last.then_inc(odn, 1)
            for g in range(NG):
                for b in range(FG):
                    j = g * FG + b
                    part = U[:, g, f0 + b * FGD:f0 + (b + 1) * FGD]
                    last = V.tensor_scalar(part, part, T[:, 100 + 6 * j:101 + 6 * j], SM[:, 88 + j:89 + j],
                                           ALU.subtract, ALU.mult)
            last.then_inc(odn, 1)

            def rope(x, ps, signal):
                ch(V.tensor_tensor(T[:, 512:768], x, odc("cos"), ALU.mult))
                ch(V.tensor_tensor(T[:, 768:1024], ps, odc("sin"), ALU.mult))
                V.tensor_tensor(x, T[:, 512:768], T[:, 768:1024], ALU.add).then_inc(signal, 1)

            dve.wait_ge(oddc_in, 32)
            dve.wait_ge(odt_a, 6)
            dve.wait_ge(rot_ps, 1)
            rope(KPT[:, 2 * P:4 * P], PS[:, 6, 0:DEC], kpt_ready)
            for q in range(4):
                j, seg = divmod(q, 2)
                dve.wait_ge(f1_ps, q + 1)
                dst = FA[:, j, 0:256] if seg == 0 else FA[:, j, 256:768]
                V.tensor_copy(dst, PS[:, q, 0:256 if seg == 0 else 512]).then_inc(fa, 1)
            for j in range(2):
                dve.wait_ge(f2_ps, j + 1)
                V.tensor_copy(FT[:, j, :], PS[:, 4 + j, 0:TOK]).then_inc(ft, 1)
            for j in range(2):
                dve.wait_ge(f3_ps, j + 1)
                V.tensor_copy(GT[:, j, :], PS[:, j, 0:TOK]).then_inc(gt if j == 0 else o_ready, 1)

            per = 2 + NC6 * 2
            base = ch.n
            with dve.Fori(0, NH // 2) as i:
                ch.n = i * per + base
                for q in range(3, 7):
                    dve.wait_ge(pj_ps, i * 7 + q + 1)
                    dst = KT[:, q - 3, :] if q < 5 else VV[:, 2 * (q - 5):2 * (q - 5) + 2, :].rearrange("p a n -> p (a n)")
                    V.tensor_copy(dst, PS[:, q, :]).then_inc(pj_d, 1)
                dve.wait_ge(pj_a, i * 3 + 3)
                dve.wait_ge(qrot_ps, i + 1)
                rope(QP[:, P:3 * P], PS[:, 7, 0:DEC], qp_ready)
                for cc in range(NC6 + 3):
                    if cc < NC6:
                        n = P * (keys(COMBOS[cc][1])[1] - keys(COMBOS[cc][1])[0])
                        mx, nm = SM[:, 108 + cc % 2:109 + cc % 2], SM[:, 104 + cc % 2:105 + cc % 2]
                        dve.wait_ge(s_ps, i * NC6 + cc + 1)
                        ch(V.reduce_max(mx, PS[:, cc % 2, 0:n], AX.X))
                        V.tensor_scalar(nm, mx, -SCALE, None, ALU.mult).then_inc(nmax, 1)
                    if 1 <= cc <= NC6:
                        b = cc - 1
                        n = P * (keys(COMBOS[b][1])[1] - keys(COMBOS[b][1])[0])
                        den = SM[:, 106 + b % 2:107 + b % 2]
                        dve.wait_ge(e_done, i * NC6 + b + 1)
                        ch(V.reciprocal(SM[:, 110 + b % 2:111 + b % 2], den))
                        V.tensor_scalar(PB[:, b % 2, 0:n], PB[:, b % 2, 0:n], SM[:, 110 + b % 2:111 + b % 2], None,
                                        ALU.mult).then_inc(p_ready, 1)
                    if cc >= 3:
                        b = cc - 3
                        h, qt = COMBOS[b]
                        dve.wait_ge(o_ps, i * NC6 + b + 1)
                        V.tensor_copy(HT[:, bass.ds(i * 2 + h, 1), qt * P:(qt + 1) * P],
                                      PS[:, 4 + b % 2:5 + b % 2, 0:P]).then_inc(o_ready, 1)
            ch.n = base + per * (NH // 2)
            layer_norm(2, 4, y_psum(2))
            modulate(3)

            b3 = lambda a: a.unsqueeze(2).broadcast_to([P, NG, NE])
            cut = iter(range(8, 900, 24))
            take = lambda: MS[:, next(cut) + 4:][:, 0:24].rearrange("p (g e) -> p g e", g=NG)
            L, EQ, VI, K1, K2, L2, G, G2, M, PMX = (take() for _ in range(10))
            small = MS[:, 270:300]
            m1, m2, im, w1, w2 = (small[:, 3 * j:3 * j + 3] for j in range(5))
            eidx = cst("expert").rearrange("p (g e) -> p g e", g=NG)
            dve.wait_ge(lg_ps, 1)
            ch(V.tensor_copy(L, PS[:, 0, 0:24].rearrange("p (g e) -> p g e", g=NG)))

            def best(src, m, k):
                ch(V.tensor_reduce(m, src, AX.X, ALU.max))
                ch(V.tensor_tensor(EQ, src, b3(m), ALU.is_equal))
                ch(V.scalar_tensor_tensor(VI, EQ, -100.0, eidx, ALU.mult, ALU.add))
                ch(V.tensor_reduce(im, VI, AX.X, ALU.min))
                ch(V.tensor_tensor(k, VI, b3(im), ALU.is_equal))

            best(L, m1, K1)
            ch(V.scalar_tensor_tensor(L2, K1, -1e30, L, ALU.mult, ALU.add))
            best(L2, m2, K2)
            V.tensor_tensor(M, K1, K2, ALU.add).then_inc(m_ready, 1)
            V.tensor_tensor(MS[:, 0:3], m2, m1, ALU.subtract).then_inc(d_ready, 1)
            V.memset(YACC.rearrange("p a n -> p (a n)"), 0.0).then_inc(cb_done, 1)
            dve.wait_ge(ex_ready, 1)
            ch(V.tensor_scalar(w1, MS[:, 3:6], 1.0, None, ALU.add))
            ch(V.reciprocal(w1, w1))
            ch(V.tensor_tensor(w2, MS[:, 3:6], w1, ALU.mult))
            ch(V.tensor_tensor(G, K1, b3(w1), ALU.mult))
            ch(V.tensor_tensor(G2, K2, b3(w2), ALU.mult))
            ch(V.tensor_tensor(G, G, G2, ALU.add))
            dve.wait_ge(m_ready, 1)
            dve.wait_ge(pos_ps, 1)
            ch(V.scalar_tensor_tensor(PMX, PS[:, 7, 0:24].rearrange("p (g e) -> p g e", g=NG), 1.0, M, ALU.add, ALU.mult))
            posa = POSA.rearrange("p (r e g) -> p r e g", r=3, e=NE)
            ga = GA.rearrange("p (r e g) -> p r e g", r=3, e=NE)
            for r in range(3):
                V.tensor_scalar(posa[:, r].rearrange("p e g -> p g e"), PMX, -1.0 - P * r, None, ALU.add)
                last = V.tensor_copy(ga[:, r].rearrange("p e g -> p g e"), G)
            last.then_inc(pos_ready, 1)
            row = lambda at, n: MS[0:1, at:at + n]
            EX, PF, IX, CB, TF = row(320, 16), row(336, 16), row(352, 16), row(370, 256), row(640, 33)
            cand = lambda name: cst(name, 1)
            for r in range(2):
                ch(V.tensor_scalar(EX.rearrange("o (e r) -> o e r", r=2)[:, :, r], PS[0:1, 7, 24:32], float(P * (r + 1)), None,
                                   ALU.is_gt))
            ch(V.tensor_tensor_scan(PF, cst("ones", 1)[:, 0:16], EX, 0.0, ALU.mult, ALU.add))
            ch(V.scalar_tensor_tensor(IX, PF, float(NE), EX, ALU.add, ALU.mult))
            ch(V.tensor_scalar(IX, IX, -1.0, None, ALU.add))
            cb = CB.rearrange("o (j c) -> o j c", j=TABLE)
            jc = [1, TABLE, 16]
            ch(V.tensor_scalar(TF[:, 0:1], PF[:, 15:16], float(NE - 1), None, ALU.add))
            for b, name in enumerate(("cand_code", "cand_expert")):
                part = TF[:, 1 + TABLE * b:1 + TABLE * (b + 1)]
                ch(V.tensor_tensor(cb, cand("item").unsqueeze(2).broadcast_to(jc), IX.unsqueeze(1).broadcast_to(jc),
                                   ALU.is_equal))
                ch(V.tensor_tensor(cb, cb, cand(name).unsqueeze(1).broadcast_to(jc), ALU.mult))
                ch(V.tensor_reduce(part, cb, AX.X, ALU.add))
                ch(V.tensor_tensor(part, part, cand("base"), ALU.add))
            V.tensor_copy(TAB[:, :], TF).then_inc(tab_ready, 1)
            dve.wait_ge(pos_ready, 1)
            more = more_items(dve)

            def one_hot(dst, i, gated, signal):
                code = dve.value_load(TAB[0:1, bass.ds(i + 1, 1)] if not isinstance(i, int) else TAB[0:1, i + 1:i + 2],
                                      min_val=0, max_val=CODES - 1)
                for g in range(NG):
                    at = bass.ds(code * NG + g, 1)
                    last = V.tensor_scalar(dst[:, g, :], cst("iota"), POSA[:, at], GA[:, at] if gated else None,
                                           ALU.is_equal, ALU.mult) if gated else \
                        V.tensor_scalar(dst[:, g, :], cst("iota"), POSA[:, at], None, ALU.is_equal)
                last.then_inc(signal, 1)

            def turned(i):
                dve.wait_ge(ptt_ps, i)
                V.tensor_copy(PT.rearrange("p a n -> p (a n)"), PS[:, 6, 0:TOK]).then_inc(pt_sb, 1)

            def combined(j):
                for q in range(2 * NG):
                    g, half = divmod(q, 2)
                    y = YACC[:, g, half * 512:(half + 1) * 512]
                    dve.wait_ge(cb_ps, j * 2 * NG + q + 1)
                    V.tensor_tensor(y, PS[:, 6 + q % 2, :], y, ALU.add).then_inc(cb_done, 1)

            def item(i, first, j=0):
                dve.wait_ge(disp_ps, i + 1)
                one_hot(PM, i + 1, False, mp_ready)
                if not first:
                    one_hot(PG, j, True, pg_ready)
                for u in range(UNITS_E):
                    dve.wait_ge(esil, i * UNITS_E + u + 1)
                    V.tensor_tensor(EH, ESIL, PS[:, 0, UCOL:2 * UCOL], ALU.mult).then_inc(eh, 1)
                    if u == 0 and not first:
                        turned(i)
                    if u == 1 and not first:
                        dve.wait_ge(cb_done, j * 2 * NG + 1)
                        combined(j)

            one_hot(PM, 0, False, mp_ready)
            item(0, True)
            with dve.Fori(0, more) as j:
                item(j + 1, False, j)
            one_hot(PG, more, True, pg_ready)
            turned(more + 1)
            dve.wait_ge(cb_done, more * 2 * NG + 1)
            combined(more)
            dve.wait_ge(cb_done, more * 2 * NG + (2 * NG + 1))
            layer_norm(3, 5, lambda g: YACC[:, g, :])

        @block.tensor
        def _(pe):
            mm, tr = nc.tensor.matmul, nc.tensor.transpose
            pe.wait_ge(cst_in, 16)
            pe.wait_ge(rows_in, 80)
            tr(PS[:, 0, 0:35], ROWS[:, :], ident[0:35, 0:35]).then_inc(rows_t, 1)

            def ada(group, after=None):
                def turn(n):
                    pe.wait_ge(st_a, n + 1)
                    pe.wait_ge(st_b, n + 1)
                    for k in range(PANEL // P):
                        last = tr(PS[:, 7, 384 + 2 * k:386 + 2 * k], STG[:, n % 2, k * P:(k + 1) * P], ident[0:2, 0:2])
                        if k == 0:
                            release(last, ("ada", n))
                    last.then_inc(cols_t, 1)

                for n in group:
                    w = slot(("ada", n)).rearrange("p (k n) -> p k n", k=KD)
                    wait_unit(pe, ("ada", n))
                    if n:
                        pe.wait_ge(st_a, n)
                    for h in range(2):
                        if h:
                            if n > group[0]:
                                turn(n - 1)
                                pe.wait_ge(cols_done, n)
                        for k in range(KD):
                            last = mm(PS[0:2, 6 + h, 0:384], SC[:, k, :], w[:, k, h * 384:(h + 1) * 384],
                                      start=(k == 0), stop=(k == KD - 1))
                            if (n, h, k) == (group[0], 0, 0) and after:
                                last.then_inc(used[after[0]], 1)
                        last.then_inc((mm_a, mm_b)[h], 1)
                turn(group[-1])
                pe.wait_ge(cols_done, group[-1] + 1)

            def release(ins, name):
                ins.then_inc(used[ring.units[name][0]], 1)

            def x_turned(st, after=None):
                for q in range(2 * NG):
                    g, half = divmod(q, 2)
                    if half == 0:
                        pe.wait_ge(ln_x, NG * (st - 1) + g + 1) if st else pe.wait_ge(x_in, 32)
                    for b in range(4):
                        k = half * 4 + b
                        last = tr(PS[:, q, b * P:(b + 1) * P], X[:, g, k * P:(k + 1) * P], ident)
                        if (q, b) == (0, 0) and after:
                            release(last, after)
                    last.then_inc(xt_t, 1)

            def h_ready(st):
                pe.wait_ge(ht_a, 5 * (st + 1))
                pe.wait_ge(ht_d, st + 1)

            pe.wait_ge(sc_ready, 1)
            ada(ADA_GROUPS[0])
            x_turned(0)
            h_ready(0)
            for t in range(16):
                w = slot(("evin", t // 4))[:, 0:4096].rearrange("p (k n) -> p k n", k=KD)
                if t % 4 == 0:
                    wait_unit(pe, ("evin", t // 4))
                if 4 <= t < 12:
                    pe.wait_ge(u_act, t - 3)
                if t >= 12:
                    pe.wait_ge(u_dve, t - 11)
                for k in range(KD):
                    last = mm(PS[:, t % 4, 0:TOK], w[:, k, (t % 4) * P:(t % 4 + 1) * P], HT[:, k, :],
                              start=(k == 0), stop=(k == KD - 1))
                    if t % 4 == 0 and t and k == 0:
                        release(last, ("evin", t // 4 - 1))
                last.then_inc(u_ps, 1)
            pe.wait_ge(pw_in, 16)
            for g in range(NPOOL):
                pe.wait_ge(pp_ready, g + 1)
                if g >= 2:
                    pe.wait_ge(mix_pool, g - 1)
                mm(PS[:, 6 + g % 2, 0:TOK], PW[:, g, :], PP[:, g, :], start=True, stop=True).then_inc(pm_ps, 1)

            def project_out(units, per, lhs, ready, after=None):
                n = len(units) * per
                for k in range(n):
                    w = slot(units[k // per])[:, 0:per * D].rearrange("p (k n) -> p k n", k=per)
                    if k % per == 0:
                        wait_unit(pe, units[k // per])
                    ready(k)
                    for g in range(NG):
                        for h in range(2):
                            last = mm(PS[:, 2 * g + h, :], lhs(k)[:, g * P:(g + 1) * P], w[:, k % per, h * 512:(h + 1) * 512],
                                      start=(k == 0), stop=(k == n - 1))
                            if (k, g, h) == (0, 0, 0) and after:
                                release(last, after)
                        if k == n - 1:
                            last.then_inc(y_ps, 1)
                    if k % per == per - 1 and k < n - 1:
                        release(last, units[k // per])

            def mix_ready(k):
                if k == 0:
                    pe.wait_ge(u_act, 12)
                    pe.wait_ge(mix_pool, 4)
                if k < 4:
                    pe.wait_ge(mix_conv, k + 1)

            project_out([("evout", 0), ("evout", 1)], 4, lambda k: MIX[:, k, :], mix_ready, ("evin", 3))
            x_turned(1, ("evout", 1))
            ada(ADA_GROUPS[1])
            h_ready(1)

            def ff_gu(f, sl, b):
                w = WR[:, sl, 0:4096].rearrange("p (k n) -> p k n", k=KD)
                if not (isinstance(f, int) and f == 0):
                    pe.wait_ge(ff_h, f)
                for j, sig in enumerate((g_ps, up_ps)):
                    for k in range(KD):
                        last = mm(PS[:, 6 + j, 0:TOK], w[:, k, j * UCOL + b * P:j * UCOL + (b + 1) * P], HT[:, k, :],
                                  start=(k == 0), stop=(k == KD - 1))
                    last.then_inc(sig, 1)

            def ff_down(f, sl, b, start=False, stop=False, release=False):
                pe.wait_ge(ff_h, f + 1)
                w = WR[:, sl, 4096:6144].rearrange("p (k n) -> p k n", k=2)
                for g in range(NG):
                    for h in range(2):
                        last = mm(PS[:, 2 * g + h, :], HF[:, b, g * P:(g + 1) * P], w[:, b, h * 512:(h + 1) * 512],
                                  start=start, stop=stop, skip_group_check=True)
                    if stop:
                        last.then_inc(y_ps, 1)
                if release and not stop:
                    last.then_inc(used[sl], 1)

            wait_unit(pe, ("ff", 0))
            ff_gu(0, 0, 0)
            ff_gu(1, 0, 1)
            ff_down(0, 0, 0, start=True)
            with pe.Fori(0, FF_ITERS) as i:
                f = i * 4 + 2
                pe.wait_ge(landed[3], i * 48 + (ff_base[0][3] + 48))
                ff_gu(f, 3, 0)
                ff_down(f - 1, 0, 1, release=True)
                ff_gu(f + 1, 3, 1)
                ff_down(f, 3, 0)
                pe.wait_ge(landed[0], i * 48 + (ff_base[0][0] + 48))
                ff_gu(f + 2, 0, 0)
                ff_down(f + 1, 3, 1, release=True)
                ff_gu(f + 3, 0, 1)
                ff_down(f + 2, 0, 0)
            ff_down(NF - 1, 0, 1, stop=True)
            ada(ADA_GROUPS[2], after=(0,))
            x_turned(2)
            h_ready(2)
            for q in range(2 * NG):
                h, g = divmod(q, NG)
                w = slot(("odin", h))[:, 0:3840].rearrange("p (k n) -> p k n", k=KD)
                if g == 0:
                    wait_unit(pe, ("odin", h))
                for k in range(KD):
                    last = mm(PS[:, q, 0:480], HT[:, k, g * P:(g + 1) * P], w[:, k, :], start=(k == 0), stop=(k == KD - 1))
                    if (q, k) == (NG, 0):
                        release(last, ("odin", 0))
                last.then_inc(odi_ps, 1)
            pe.wait_ge(odu, 2 * NG)
            pe.wait_ge(odn, 1)
            for q in range(3):
                for g in range(NG):
                    last = tr(PS[:, q, g * P:(g + 1) * P], U[:, g, q * P:(q + 1) * P], ident)
                    if (q, g) == (0, 0):
                        release(last, ("odin", 1))
                last.then_inc(odt_ps, 1)
            pe.wait_ge(cache_in, 48)
            pe.wait_ge(odn, 2)
            for q in range(2):
                for kg in range(4):
                    src = CK[:, q * P:(q + 1) * P] if kg == 1 else U[:, max(kg - 1, 0), QR + q * P:QR + (q + 1) * P]
                    last = tr(PS[:, 3 + q, kg * P:(kg + 1) * P], src, ident)
                last.then_inc(odt_ps, 1)
            pe.wait_ge(kd_ready, 1)
            for kg in range(4):
                last = tr(PS[:, 5, kg * P:(kg + 1) * P], KDUP[:, kg, :], ident)
            last.then_inc(odt_ps, 1)
            pe.wait_ge(oddc_in, 32)
            pe.wait_ge(odt_a, 6)
            mm(PS[:, 6, 0:DEC], odc("rot"), KPT[:, 2 * P:4 * P], start=True, stop=True).then_inc(rot_ps, 1)
            pe.wait_ge(odn, 3)
            dl = dft("latent").rearrange("p (k n) -> p k n", k=2)
            f0 = QR + KVR + ROPE
            for j in range(2):
                cols = slice(f0 + j * P, f0 + (j + 1) * P)
                mm(PS[:, 2 * j, 0:256], U[:, 0, cols], dft("prompt"), start=True, stop=True).then_inc(f1_ps, 1)
                for k in range(2):
                    last = mm(PS[:, 2 * j + 1, :], U[:, 1 + k, cols], dl[:, k, :], start=(k == 0), stop=(k == 1))
                last.then_inc(f1_ps, 1)
            for j in range(2):
                pe.wait_ge(fa, 2 * j + 2)
                for lo, n, a in ((0, SEQ, 0), (SEQ, DEC, 256)):
                    mm(PS[:, 4 + j, lo:lo + n], odc("chan_cos"), FA[:, j, a:a + n], start=True, stop=False)
                    last = mm(PS[:, 4 + j, lo:lo + n], odc("chan_nsin"), FA[:, j, a + n:a + 2 * n], start=False, stop=True)
                last.then_inc(f2_ps, 1)
            pe.wait_ge(fnw_in, 16)
            pe.wait_ge(ft, 2)
            for j in range(2):
                for k in range(2):
                    last = mm(PS[:, j, 0:TOK], FNW[:, k, j * P:(j + 1) * P], FT[:, k, :], start=(k == 0), stop=(k == 1))
                last.then_inc(f3_ps, 1)
            pe.wait_ge(kpt_ready, 1)

            wq = WR[:, 3, 0:768].rearrange("p (k h c) -> p k h c", k=3, h=2)
            wp = WR[:, 3, 768:1152].rearrange("p (k n) -> p k n", k=3)
            wk = WR[:, 3, 1152:1664].rearrange("p (k h c) -> p k h c", k=2, h=2)
            wv = WR[:, 3, 1664:2176].rearrange("p (k n) -> p k n", k=2)
            with pe.Fori(0, NH // 2) as i:
                pe.wait_ge(landed[3], i * 16 * PAIR_DMAS + (pair_base[0][3] + 16 * PAIR_DMAS))
                pe.wait_ge(o_ready, i * NC6 + 1)
                for h in range(2):
                    for k in range(3):
                        last = mm(PS[:, h, 0:TOK], wq[:, k, h, :], QHT[:, k, :], start=(k == 0), stop=(k == 2))
                    last.then_inc(pj_ps, 1)
                for k in range(3):
                    last = mm(PS[:, 2, 0:TOK], wp[:, k, :], QHT[:, k, :], start=(k == 0), stop=(k == 2))
                last.then_inc(pj_ps, 1)
                for h in range(2):
                    for k in range(2):
                        last = mm(PS[:, 3 + h, :], wk[:, k, h, :], CKT[:, k, :], start=(k == 0), stop=(k == 1))
                    last.then_inc(pj_ps, 1)
                for kg in range(4):
                    for k in range(2):
                        last = mm(PS[:, 5 + kg // 2, (kg % 2) * 256:(kg % 2 + 1) * 256], CKT[:, k, kg * P:(kg + 1) * P],
                                  wv[:, k, :], start=(k == 0), stop=(k == 1))
                    if kg % 2:
                        last.then_inc(pj_ps, 1)
                pe.wait_ge(pj_a, i * 3 + 3)
                mm(PS[:, 7, 0:DEC], odc("rot"), QP[:, P:3 * P], start=True, stop=True).then_inc(qrot_ps, 1)
                pe.wait_ge(pj_d, i * 4 + 4)
                pe.wait_ge(qp_ready, i + 1)
                for cc in range(NC6 + 2):
                    if cc < NC6:
                        h, qt = COMBOS[cc]
                        lo, hi = (P * v for v in keys(qt))
                        if cc >= 2:
                            pe.wait_ge(e_done, i * NC6 + cc - 1)
                        first = mm(PS[:, cc % 2, 0:hi - lo], QN[:, h, qt * P:(qt + 1) * P], KT[:, h, lo:hi],
                                   start=True, stop=False)
                        if cc == 0:
                            first.then_inc(used[3], 1)
                        mm(PS[:, cc % 2, 0:hi - lo], QP[h * ROPE:(h + 1) * ROPE, qt * P:(qt + 1) * P],
                           KPT[h * ROPE:(h + 1) * ROPE, lo:hi], start=False, stop=True).then_inc(s_ps, 1)
                    if 1 <= cc <= NC6:
                        b = cc - 1
                        lo, hi = keys(COMBOS[b][1])
                        pe.wait_ge(p_ready, i * NC6 + b + 1)
                        for j in range(hi - lo):
                            last = tr(PS[:, 2 + b % 2, j * P:(j + 1) * P], PB[:, b % 2, j * P:(j + 1) * P], ident)
                        last.then_inc(pt_ps, 1)
                    if cc >= 2:
                        b = cc - 2
                        h, qt = COMBOS[b]
                        lo, hi = keys(qt)
                        pe.wait_ge(pt_ready, i * NC6 + b + 1)
                        if b >= 2:
                            pe.wait_ge(o_ready, i * NC6 + b)
                        for j in range(hi - lo):
                            last = mm(PS[:, 4 + b % 2, 0:P], VV[:, lo + j, h * P:(h + 1) * P], PTB[:, b % 2, j * P:(j + 1) * P],
                                      start=(j == 0), stop=(j == hi - lo - 1))
                        last.then_inc(o_ps, 1)

            def attn_ready(k):
                if k == 0:
                    pe.wait_ge(o_ready, NC6 * NH // 2 + 1)
                    pe.wait_ge(gt, 1)

            project_out([("odout", 0), ("odout", 1)], 5, lambda k: HT[:, k, :] if k < 8 else GT[:, k - 8, :], attn_ready)
            x_turned(3, ("odout", 1))
            h_ready(3)

            pe.wait_ge(rout_in, 16)
            rw = ROUT.rearrange("p (k e) -> p k e", k=KD)
            for g in range(NG):
                for k in range(KD):
                    last = mm(PS[:, 0, g * NE:(g + 1) * NE], HT[:, k, g * P:(g + 1) * P], rw[:, k, :],
                              start=(k == 0), stop=(k == KD - 1))
            last.then_inc(lg_ps, 1)
            for q in range(2 * NG):
                g, half = divmod(q, 2)
                for b in range(4):
                    last = tr(PS[:, 1 + q, b * P:(b + 1) * P], HT[:, half * 4 + b, g * P:(g + 1) * P], ident)
                last.then_inc(hkt_ps, 1)
            pe.wait_ge(m_ready, 1)
            mask = MS[:, 8 + 4 + 8 * 24:8 + 4 + 9 * 24].rearrange("p (g e) -> p g e", g=NG)
            for g in range(NG + 1):
                for b in range(min(g + 1, NG)):
                    m = cst("before") if b == g else cst("ones")
                    last = mm(PS[:, 7, g * NE:(g + 1) * NE], m, mask[:, b, :], start=(b == 0), stop=(b == min(g, NG - 1)))
            last.then_inc(pos_ps, 1)
            pe.wait_ge(hk, 2 * NG)
            pe.wait_ge(pos_ready, 1)
            more = more_items(pe)

            def dispatch(i):
                pe.wait_ge(mp_ready, i + 1)
                if not (isinstance(i, int) and i == 0):
                    pe.wait_ge(xe_done, i)
                for k in range(KD):
                    for g in range(NG):
                        last = mm(PS[:, 4 + k // 4, (k % 4) * P:(k % 4 + 1) * P], HK[:, g, k * P:(k + 1) * P], PM[:, g, :],
                                  start=(g == 0), stop=(g == NG - 1))
                last.then_inc(disp_ps, 1)

            def gate_up(i, u):
                w = WR[:, MOE_SLOTS[u], 0:4096].rearrange("p (k n) -> p k n", k=KD)
                if not (isinstance(i, int) and i == 0 and u == 0):
                    pe.wait_ge(eh, i * UNITS_E + u)
                for k in range(KD):
                    last = mm(PS[:, 0, :], XE[:, k, :], w[:, k, :], start=(k == 0), stop=(k == KD - 1))
                last.then_inc(gu_ps, 1)

            def down(i, u):
                w = WR[:, MOE_SLOTS[u], 4096:6144].rearrange("p (k n) -> p k n", k=2)
                pe.wait_ge(eht, i * UNITS_E + u + 1)
                for b in range(2):
                    for h in range(2):
                        last = mm(PS[:, 2 + h, :], EHT[:, b, :], w[:, b, h * 512:(h + 1) * 512],
                                  start=(u == 0 and b == 0), stop=(u == UNITS_E - 1 and b == 1))
                if u == UNITS_E - 1:
                    last.then_inc(yd, 1)
                else:
                    last.then_inc(used[MOE_SLOTS[u]], 1)

            def turn_selection(i):
                pe.wait_ge(pg_ready, i)
                for g in range(NG):
                    last = tr(PS[:, 6, g * P:(g + 1) * P], PG[:, g, :], ident)
                    if g == 0:
                        last.then_inc(used[MOE_SLOTS[-1]], 1)
                last.then_inc(ptt_ps, 1)

            def combine(i, j):
                pe.wait_ge(ysb, i)
                pe.wait_ge(pt_sb, i)
                for q in range(2 * NG):
                    g, half = divmod(q, 2)
                    if q >= 2:
                        pe.wait_ge(cb_done, j * 2 * NG + q)
                    mm(PS[:, 6 + q % 2, :], PT[:, g, :], YSB[:, half * 512:(half + 1) * 512], start=True, stop=True)\
                        .then_inc(cb_ps, 1)

            def item(i, first, j=0):
                seen = [0] * 4
                for u in range(UNITS_E):
                    sl = MOE_SLOTS[u]
                    if first:
                        wait_unit(pe, ("moe", 0, u))
                    else:
                        seen[sl] += 1
                        pe.wait_ge(landed[sl], j * (48 * MOE_USES[sl]) + moe_landed[sl] + 48 * seen[sl])
                    if u == 0:
                        pe.wait_ge(xe_done, i + 1)
                    gate_up(i, u)
                    if u == 0 and not first:
                        down(j, UNITS_E - 1)
                        pe.wait_ge(cb_done, j * 2 * NG + 1)
                        turn_selection(i)
                    if u == 1 and not first:
                        combine(i, j)
                    if u > 0:
                        down(i, u - 1)
                    if u == 2:
                        dispatch(i + 1)
                    pe.wait_ge(eh, i * UNITS_E + u + 1)
                    for b in range(2):
                        last = tr(PS[:, 1, b * P:(b + 1) * P], EH[:, b * P:(b + 1) * P], ident)
                    last.then_inc(t_ps, 1)

            dispatch(0)
            item(0, True)
            with pe.Fori(0, more) as j:
                item(j + 1, False, j)
            down(more, UNITS_E - 1)
            pe.wait_ge(cb_done, more * 2 * NG + 1)
            turn_selection(more + 1)
            combine(more + 1, more)


_INS = ["x_prompt", "x_sample", "cache_ckv", "cache_kpe", "c", "c_ctx", "ada_w", "ada_b", "ln_g", "ln_b", "ev_w_in",
        "ev_conv_w", "ev_pool_w", "ev_pool_scale", "ev_w_out", "ffn_w_gate", "ffn_w_up", "ffn_w_down", "od_w_in",
        "od_q_norm", "od_kv_norm", "od_w_q_b", "od_w_kv_b", "od_fnet_w", "od_w_out", "moe_router", "moe_w_gate",
        "moe_w_up", "moe_w_down"]
_OUTS = [(1, SEQ, D), (1, DEC, D), (1, 1, SEQ, KVR), (1, 1, SEQ, ROPE)]


def kernel(**inputs):
    import concourse.bacc as _bacc
    from concourse.bass_utils import run_bass_kernel_spmd as _run

    nc = _bacc.Bacc("TRN2", target_bir_lowering=False, num_devices=1)
    arrays, args = {}, []
    given = {name: np.ascontiguousarray(inputs[name]) for name in _INS}
    given |= {"base_rows": BASE_ROWS, "odd_rows": ODD_ROWS, "dft_rows": DFT_ROWS, "pool_inv": pool_counts()}
    for name, a in given.items():
        arrays[f"in_{name}"] = a
        args.append(nc.dram_tensor(f"in_{name}", a.shape, mybir.dt.from_np(a.dtype), kind="ExternalInput").ap())
    for i, shape in enumerate(_OUTS):
        args.append(nc.dram_tensor(f"out_{i}", shape, F32, kind="ExternalOutput").ap())
    build(nc, *args)
    r = _run(nc, [arrays], core_ids=[0])
    return tuple(r.results[0][f"out_{i}"] for i in range(len(_OUTS)))
```

```python
from contextlib import ExitStack

import numpy as np

import concourse.bass as bass
from concourse import mybir

F32 = mybir.dt.float32
F32R = mybir.dt.float32r
I32 = mybir.dt.int32
ALU = mybir.AluOpType
ACT = mybir.ActivationFunctionType
AX = mybir.AxisListType

P = 128
D = 1024
KD = D // P
SEQ, DEC, PAST = 128, 256, 128
TOK = SEQ + DEC
NG = TOK // P
DEPTH = 2
CONV = 512
NPOOL = 4
WINDOWS = (2, 4, 8, 16)
FF = 2816
NF = FF // P
NH = 8
NOPE, ROPE, VD = 128, 64, 128
QR, KVR = 384, 256
FG, FGD = 4, 64
FD = FG * FGD
ODD_IN = QR + KVR + ROPE + FD
NE = 8
FFE = 1792
GRID_W = 64
ALPHA = float((2 * DEPTH) ** 0.25)
LN_EPS, RMS_EPS = 1e-5, 1e-6
SCALE = float((NOPE + ROPE) ** -0.5)

SLOT = 6144
PANEL = SLOT // KD
NPANEL = 6 * D // PANEL
UCOL = 256
UNITS_FF = FF // UCOL
UNITS_E = FFE // UCOL
CODES = 3 * NE
SCRATCH = 13600
TABLE = 16


def columns(parts):
    at, out = 0, {}
    for name, a in parts:
        out[name] = (at, a.shape[1])
        at += a.shape[1]
    return out, np.ascontiguousarray(np.concatenate([a for _, a in parts], 1).astype(np.float32))


def base_constants():
    n = np.arange(P)
    row = lambda v: np.tile(np.asarray(v, np.float32)[None, :], (P, 1))
    cand = [(e, r) for e in range(NE) for r in (1, 2)]
    return columns([
        ("ident", np.eye(P)),
        ("iota", row(n)),
        ("before", (n[:, None] < n[None, :]).astype(np.float32)),
        ("ones", np.ones((P, P))),
        ("expert", row(np.tile(np.arange(NE), NG))),
        ("item", row(np.arange(TABLE))),
        ("cand_code", row([e + NE * r for e, r in cand])),
        ("cand_expert", row([e for e, _ in cand])),
        ("base", row([j if j < NE else 0 for j in range(TABLE)])),
        ("eps", row([LN_EPS])),
    ])


def odd_constants():
    t = np.arange(DEC)
    half = ROPE // 2
    inv = 10000.0 ** (-np.arange(0, half, 2) / half)
    ar, ac = (t // GRID_W)[:, None] * inv, (t % GRID_W)[:, None] * inv
    ang = np.concatenate([ar, ar, ac, ac], -1)
    rot = np.zeros((ROPE, ROPE))
    q = ROPE // 4
    for h in range(2):
        for j in range(q):
            rot[h * 2 * q + q + j, h * 2 * q + j] = -1
            rot[h * 2 * q + j, h * 2 * q + q + j] = 1
    two = lambda m: np.kron(np.eye(2), m)
    dft = lambda n: 2 * np.pi * (np.outer(np.arange(n), np.arange(n)) % n) / n
    pos = lambda n: np.concatenate([np.cos(dft(n)), np.sin(dft(n))], 1) / np.sqrt(n * FGD)
    long = pos(DEC).reshape(DEC // P, P, 2 * DEC).transpose(1, 0, 2).reshape(P, -1)
    return columns([
        ("cos", np.tile(np.cos(ang).T, (2, 1))),
        ("sin", np.tile(np.sin(ang).T, (2, 1))),
        ("rot", two(rot)),
        ("chan_cos", two(np.cos(dft(FGD)))),
        ("chan_nsin", two(-np.sin(dft(FGD)))),
    ]), columns([("prompt", pos(SEQ)), ("latent", long)])


def pool_counts():
    out = np.zeros((NPOOL, TOK), np.float32)
    for w, win in enumerate(WINDOWS):
        at = 0
        for n in (SEQ, DEC):
            t = np.arange(n)
            out[w, at:at + n] = 1.0 / (np.minimum(t + win // 2, n) - np.maximum(t - win // 2, 0))
            at += n
    return out


BASE, BASE_ROWS = base_constants()
(ODD, ODD_ROWS), (DFT, DFT_ROWS) = odd_constants()


class Pieces:

    def __init__(self):
        self.n, self.landed = 0, [0] * RING

    def take(self, dmas):
        n, at = self.n, self.n % RING
        self.n += 1
        self.landed[at] += 16 * dmas
        return n, at, self.landed[at]

    def skip(self, n, landed):
        self.n += n
        self.landed = [a + b for a, b in zip(self.landed, landed)]


class Ring:

    def __init__(self):
        self.landed, self.used, self.units = [0] * 4, [0] * 4, {}

    def unit(self, name, slot, dmas):
        before = self.used[slot]
        self.landed[slot] += 16 * dmas
        self.used[slot] += 1
        self.units[name] = (slot, self.landed[slot], before)


class Chain:

    def __init__(self, eng, sem):
        self.eng, self.sem, self.n = eng, sem, 0

    def __call__(self, ins):
        ins.then_inc(self.sem, 1)
        self.n = self.n + 1
        self.eng.wait_ge(self.sem, self.n)


def plan():
    r = Ring()
    for p in range(NPANEL):
        r.unit(("ada", p), p % 4, 1)
    for t in range(4):
        r.unit(("evin", t), t, 1)
    r.unit(("evout", 0), 0, 1)
    r.unit(("evout", 1), 1, 1)
    for p, s in zip(range(4), (2, 3, 1, 2)):
        r.unit(("ada", NPANEL + p), s, 1)
    before_ff = list(r.used)
    for p, s in zip(range(4, 8), (1, 2, 3, 1)):
        r.unit(("ada", NPANEL + p), s, 1)
    r.unit(("odin", 0), 2, 1)
    r.unit(("odin", 1), 3, 1)
    r.unit(("odout", 0), 1, 1)
    r.unit(("odout", 1), 2, 1)
    pair = (list(r.landed), list(r.used))
    for i in range(NH // 2):
        r.unit(("pair", i), 3, PAIR_DMAS)
    return r, before_ff, pair


RING = 6
PIECE = 1024
PAIR_DMAS = 3 + 3 + 2 + 2


def build(nc, x_prompt, x_sample, cache_ckv, cache_kpe, c, c_ctx, ada_w, ada_b, ln_g, ln_b, ev_w_in, ev_conv_w,
          ev_pool_w, ev_pool_scale, ev_w_out, ffn_w_gate, ffn_w_up, ffn_w_down, od_w_in, od_q_norm, od_kv_norm,
          od_w_q_b, od_w_kv_b, od_fnet_w, od_w_out, moe_router, moe_w_gate, moe_w_up, moe_w_down,
          base_rows, odd_rows, dft_rows, pool_inv, y_prompt, y_sample, new_ckv, new_kpe):
    ctx = ExitStack()
    with ctx:
        def sb(name, shape, dt=F32):
            return ctx.enter_context(nc.sbuf_tensor("sb_" + name, shape, dt))

        def sem(name):
            return ctx.enter_context(nc.semaphore(name))

        mod_rows = nc.dram_tensor("mod_rows", (DEPTH, 2, 6 * D), F32, kind="Internal").ap()

        WR = sb("ring", [P, 4, SLOT])
        ring_at = nc.sbuf_base - 4 * 4 * SLOT
        RAW = WR[:, 0, :].rearrange("p (r n) -> p r n", r=RING)
        WS = nc.alloc_sbuf_tensor_at("sb_split_weights", [P, RING, 2, PIECE], F32R, offset=ring_at + 4 * SLOT)
        AS = nc.alloc_sbuf_tensor_at("sb_split_acts", [P, SLOT], F32R, offset=ring_at + 12 * SLOT)
        X = sb("x", [P, NG, D])
        HT = sb("ht", [P, KD, TOK])
        GB = sb("gate_rows", [P, 2, D])
        LG = sb("ln_gain", [P, D])
        LB = sb("ln_bias", [P, D])
        T = sb("temp", [P, D])
        CST = sb("constants", [P, BASE_ROWS.shape[1]])
        MT = sb("mod_cols", [P, DEPTH, 6 * KD, 2])
        ROWS = sb("rows", [35, P])
        COLS = sb("cols", [P, 35])
        SC = sb("silu_cond", [P, KD, 2])
        STG = sb("mod_stage", [2, 2, PANEL])
        BROW = sb("mod_bias", [2, PANEL])
        SM = sb("small", [P, 160])
        TAB = sb("item_table", [1, 1 + 2 * TABLE], I32)
        SCR = sb("scratch", [P, SCRATCH])
        scratch_at = nc.sbuf_base - 4 * SCRATCH
        PS = ctx.enter_context(nc.psum_tensor("ps", [P, 8, 512], F32))

        def cst(name, rows=P):
            at, n = BASE[name]
            return CST[0:rows, at:at + n]

        ident = cst("ident")

        def carve(*parts):
            at, out = 0, []
            for n in parts:
                out.append(SCR[:, at:at + n])
                at += n
            assert at <= SCRATCH, at
            return out

        ZW, UW = SEQ + DEC + 4, SEQ + DEC + 32
        UX, UB, Z, UP, ICNT, SA, SBB, CV, MIX, PW = carve(
            4 * TOK, 4 * TOK, 4 * ZW, 4 * UW, 4 * TOK, UW, UW, ZW, 8 * TOK, 4 * P)
        PP = UX
        r4 = lambda a, n: a.rearrange("p (a n) -> p a n", a=n)
        UX, UB, Z, UP, ICNT, PP, MIX, PW = (r4(a, n) for a, n in
                                            ((UX, 4), (UB, 4), (Z, 4), (UP, 4), (ICNT, 4), (PP, 4), (MIX, 8), (PW, 4)))
        SEGZ = ((0, 1, SEQ), (SEQ, SEQ + 3, DEC))
        SEGU = ((0, 8, SEQ), (SEQ, SEQ + 24, DEC))
        SIL, HF = carve(TOK, TOK)
        HFS = nc.alloc_sbuf_tensor_at("sb_split_hidden", [P, 2, 2, TOK], F32R, offset=scratch_at + 4 * 1024)
        HX = AS[:, :].rearrange("p (s k n) -> p s k n", s=2, k=KD)
        (U, KDUP, CK, QHT, CKT, KPT, OC, FNW, GT, AT) = carve(
            NG * ODD_IN, 4 * P, KVR, 3 * TOK, 2 * 512, 512, ODD_ROWS.shape[1], 2 * FD, 2 * TOK, 4992)
        DC = AT[:, 2304:2304 + DFT_ROWS.shape[1]]
        KVN = AT[:, 3600:3600 + KVR]
        U, KDUP, QHT, CKT, FNW, GT = (r4(a, n) for a, n in ((U, NG), (KDUP, 4), (QHT, 3), (CKT, 2), (FNW, 2), (GT, 2)))
        FA = r4(AT[:, 0:2 * 768], 2)
        FT = r4(AT[:, 1536:1536 + 2 * TOK], 2)
        cut = np.cumsum([0, 2 * TOK, TOK, 256, 1024, 1024, 2 * TOK, 2 * TOK])
        QN, QP, RT, KT, VV, PB, PTB = (AT[:, int(a):int(b)] for a, b in zip(cut[:-1], cut[1:]))
        QN, KT, VV, PB, PTB = (r4(a, n) for a, n in ((QN, 2), (KT, 2), (VV, 4), (PB, 2), (PTB, 2)))
        odc = lambda name: OC[:, ODD[name][0]:ODD[name][0] + ODD[name][1]]
        dft = lambda name: DC[:, DFT[name][0]:DFT[name][0] + DFT[name][1]]
        (HK, YACC, PM, PG, PT, ESIL, EH, YSB, POSA, GA, ROUT, MS) = carve(
            NG * D, NG * D, TOK, TOK, TOK, UCOL, UCOL, D, CODES * NG, CODES * NG, KD * NE, 900)
        HK, YACC, PM, PG, PT = (r4(a, n) for a, n in ((HK, NG), (YACC, NG), (PM, NG), (PG, NG), (PT, NG)))
        XES = AS[:, 0:2 * D].rearrange("p (s n) -> p s n", s=2)
        EHS = AS[:, 2 * D:2 * D + 2 * UCOL].rearrange("p (s n) -> p s n", s=2)

        landed = [sem(f"landed{s}") for s in range(4)]
        used = [sem(f"used{s}") for s in range(4)]
        names = """cst_in rows_in x_in brow_in stored0 stored1 lnp_in pw_in icnt_in oddc_in cache_in kvn_in
            fnw_in rout_in out_done kv_out rows_t cols_ready sc_ready mm_a mm_b st_a st_b cols_t cols_done mt_ready
            xt_t ht_a ht_d u_ps u_act u_dve z_pad mix_conv pp_ready pm_ps mix_pool y_ps var_ready sd_ready ln_x
            g_ps up_ps sil ff_h odi_ps odu ssq uvar usd odn kd_ready odt_ps odt_a rot_ps kpt_ready f1_ps fa f2_ps ft
            f3_ps gt pj_ps pj_a pj_d qrot_ps qp_ready s_ps nmax e_done p_ready pt_ps pt_ready o_ps o_ready
            lg_ps hkt_ps hk d_ready ex_ready m_ready pos_ps tab_ready pos_ready q_ready
            gu_ps esil eh t_ps eht yd ysb pg_ready ptt_ps pt_sb cb_ps cb_done mp_ready disp_ps xe_done
            hi_done lo_done w_used hx_hi hx_lo fh_hi fh_lo xe_hi xe_lo eht_hi eht_lo
            dve_chain act_chain pool_chain""".split()
        s = {n: sem(n) for n in names}
        (cst_in, rows_in, x_in, brow_in, stored0, stored1, lnp_in, pw_in, icnt_in, oddc_in, cache_in, kvn_in,
         fnw_in, rout_in, out_done, kv_out, rows_t, cols_ready, sc_ready, mm_a, mm_b, st_a, st_b, cols_t, cols_done, mt_ready,
         xt_t, ht_a, ht_d, u_ps, u_act, u_dve, z_pad, mix_conv, pp_ready, pm_ps, mix_pool, y_ps, var_ready, sd_ready,
         ln_x, g_ps, up_ps, sil, ff_h, odi_ps, odu, ssq, uvar, usd, odn, kd_ready, odt_ps, odt_a, rot_ps, kpt_ready,
         f1_ps, fa, f2_ps, ft, f3_ps, gt, pj_ps, pj_a, pj_d, qrot_ps, qp_ready, s_ps, nmax, e_done, p_ready, pt_ps,
         pt_ready, o_ps, o_ready, lg_ps, hkt_ps, hk, d_ready, ex_ready, m_ready, pos_ps, tab_ready, pos_ready,
         q_ready, gu_ps, esil, eh, t_ps, eht, yd, ysb, pg_ready, ptt_ps, pt_sb, cb_ps, cb_done, mp_ready, disp_ps,
         xe_done, hi_done, lo_done, w_used, hx_hi, hx_lo, fh_hi, fh_lo, xe_hi, xe_lo, eht_hi, eht_lo,
         dve_chain, act_chain, pool_chain) = (s[n] for n in names)
        stored = (stored0, stored1)

        raw_in = [sem(f"raw_in{r}") for r in range(RING)]
        ring, ring_before_ff, pair_base = plan()
        FF_ITERS = (UNITS_FF - 1) // 2
        pieces = Pieces()
        FF_FIRST = [pieces.take(2) for _ in range(4)] + [pieces.take(1)]
        ff_n, ff_landed = pieces.n, list(pieces.landed)
        FF_UNIT_LANDED = [32 if (r - ff_n) % RING < 4 else 16 for r in range(RING)]
        pieces.skip(RING * (UNITS_FF - 1), [(UNITS_FF - 1) * v for v in FF_UNIT_LANDED])
        FF_LAST = pieces.take(1)
        E_FIRST = [pieces.take(2) for _ in range(4)]
        e_n, e_landed = pieces.n, list(pieces.landed)
        E_UNIT_LANDED = [32 if (r - e_n) % RING < 4 else 16 for r in range(RING)]

        def stream_piece(base_n, base_landed, per_unit, unit, c):
            at = (base_n + c) % RING
            return unit * RING + (base_n + c), at, unit * per_unit[at] + (base_landed[at] + per_unit[at])

        ff_piece = lambda unit, c: stream_piece(ff_n, ff_landed, FF_UNIT_LANDED, unit, c)
        e_piece = lambda unit, c: stream_piece(e_n, e_landed, E_UNIT_LANDED, unit, c)

        ff_used = lambda unit, c: unit * RING + (min(c, 3) + 1 if c < 5 else RING - 1)
        FF_LAST_USED = RING * (UNITS_FF - 1) + 1
        e_used = lambda unit, c: unit * RING + (e_n - RING + c)
        ADA_GROUPS = (range(0, NPANEL), range(NPANEL, NPANEL + 4), range(NPANEL + 4, 2 * NPANEL))
        COMBOS = [(h, qt) for h in range(2) for qt in range(NG)]
        NC6 = len(COMBOS)

        def keys(qt):
            return (0, 1) if qt == 0 else (1, 4)

        def slot(name):
            return WR[:, ring.units[name][0], :]

        def wait_unit(eng, name):
            sl, land, _ = ring.units[name]
            eng.wait_ge(landed[sl], land)

        def more_items(eng):
            eng.wait_ge(tab_ready, 1)
            return eng.value_load(TAB[0:1, 0:1], min_val=NE - 1, max_val=TABLE - 4)

        block = ctx.enter_context(nc.Block())

        @block.sync
        def _(sp):
            def free(name):
                sl, _, before = ring.units[name]
                if before:
                    sp.wait_ge(used[sl], before)

            def panel(dst, src, n, k, name):
                sp.dma_start(dst[:, 0:k * n].rearrange("p (k n) -> p k n", k=k),
                             src.rearrange("(k p) n -> p k n", p=P)).then_inc(landed[ring.units[name][0]], 16)

            def load(name, src):
                free(name)
                rows, n = src.shape
                panel(slot(name), src, n, rows // P, name)

            def raw_free(n, more=0):
                if isinstance(n, int) and n < RING:
                    return
                sp.wait_ge(lo_done, n - (RING - 1) + more)

            def gate_up_piece(piece, gate, up, more=0):
                n, at, _ = piece
                raw_free(n, more)
                dst = RAW[:, at, :].rearrange("p (k n) -> p k n", k=2)
                sp.dma_start(dst[:, :, 0:UCOL], gate).then_inc(raw_in[at], 16)
                sp.dma_start(dst[:, :, UCOL:2 * UCOL], up).then_inc(raw_in[at], 16)

            def down_piece(piece, down, free=False):
                n, at, _ = piece
                if not free:
                    raw_free(n)
                sp.dma_start(RAW[:, at, :], down).then_inc(raw_in[at], 16)

            fg = ffn_w_gate[0].rearrange("(k p) n -> p k n", p=P)
            fu = ffn_w_up[0].rearrange("(k p) n -> p k n", p=P)
            fd = ffn_w_down[0].rearrange("(u b p) n -> p u b n", b=2, p=P)

            def ff_gate_up(piece, u, c):
                cols = bass.ds(u * UCOL, UCOL)
                gate_up_piece(piece, fg[:, 2 * c:2 * c + 2, cols], fu[:, 2 * c:2 * c + 2, cols], more=int(c == 0))

            def ff_down(piece, u, b):
                down_piece(piece, fd[:, bass.ds(u, 1), b, :])

            def moe_gate_up(piece, e, u, c, more=0):
                one, rows, cols = bass.ds(e, 1), slice(2 * c * P, (2 * c + 2) * P), slice(u * UCOL, (u + 1) * UCOL)
                gate_up_piece(piece, moe_w_gate[0, one, rows, cols].rearrange("e (k p) n -> p (e k) n", p=P),
                              moe_w_up[0, one, rows, cols].rearrange("e (k p) n -> p (e k) n", p=P), more)

            def moe_down(piece, e, f):
                down_piece(piece, moe_w_down[0, bass.ds(e, 1), f * P:(f + 1) * P, :].rearrange("e p n -> p (e n)"),
                           free=f == 0)

            def moe_item(i, e, e_next):
                for u in range(UNITS_E):
                    for c in range(4):
                        last = u == UNITS_E - 1
                        moe_gate_up(e_piece(i * UNITS_E + u, c), e_next if last else e, 0 if last else u + 1, c,
                                    more=int((u, c) == (0, 3)))
                    for b in range(2):
                        moe_down(e_piece(i * UNITS_E + u, 4 + b), e, 2 * u + b)

            def ada(n):
                l, p = divmod(n, NPANEL)
                load(("ada", n), ada_w[l, :, p * PANEL:(p + 1) * PANEL])

            for n in ADA_GROUPS[0]:
                ada(n)
                if n == 0:
                    sp.dma_start(X[:, 0, :], x_prompt[0]).then_inc(x_in, 16)
                    sp.dma_start(X[:, 1:NG, :], x_sample[0].rearrange("(g p) d -> p g d", p=P)).then_inc(x_in, 16)
            for t in range(4):
                load(("evin", t), ev_w_in[0, :, t * 512:(t + 1) * 512])
            for t in range(2):
                load(("evout", t), ev_w_out[0, t * 512:(t + 1) * 512, :])
            for n in ADA_GROUPS[1]:
                ada(n)
            sp.wait_ge(used[0], ring_before_ff[0])
            for c in range(4):
                ff_gate_up(FF_FIRST[c], 0, c)
            ff_down(FF_FIRST[4], 0, 0)
            with sp.Fori(0, FF_ITERS) as i:
                for b in range(2):
                    for c in range(4):
                        ff_gate_up(ff_piece(i * 2 + b, c), i * 2 + (b + 1), c)
                    ff_down(ff_piece(i * 2 + b, 4), i * 2 + b, 1)
                    ff_down(ff_piece(i * 2 + b, 5), i * 2 + (b + 1), 0)
            ff_down(FF_LAST, UNITS_FF - 1, 1)
            sp.wait_ge(y_ps, 2 * NG)
            for n in ADA_GROUPS[2]:
                ada(n)
            for t in range(2):
                load(("odin", t), od_w_in[0, :, t * 480:(t + 1) * 480])
            for t in range(2):
                load(("odout", t), od_w_out[0, t * 640:(t + 1) * 640, :])
            for c in range(4):
                moe_gate_up(E_FIRST[c], 0, 0, c)
            qb = od_w_q_b[0].rearrange("(k p) (h c) -> p k h c", p=P, h=NH)
            kvb = od_w_kv_b[0].rearrange("(k p) (h c) -> p k h c", p=P, h=NH)
            with sp.Fori(0, NH // 2) as i:
                sp.wait_ge(used[3], i + pair_base[1][3])
                two = bass.ds(i * 2, 2)
                for k in range(3):
                    sp.dma_start(WR[:, 3, 256 * k:256 * (k + 1)].rearrange("p (h c) -> p h c", h=2),
                                 qb[:, k, two, 0:NOPE]).then_inc(landed[3], 16)
                    sp.dma_start(WR[:, 3, 768 + P * k:768 + P * (k + 1)].rearrange("p (h c) -> p h c", h=2),
                                 qb[:, k, two, NOPE:NOPE + ROPE]).then_inc(landed[3], 16)
                for k in range(2):
                    sp.dma_start(WR[:, 3, 1152 + 256 * k:1408 + 256 * k].rearrange("p (h c) -> p h c", h=2),
                                 kvb[:, k, two, 0:NOPE]).then_inc(landed[3], 16)
                    sp.dma_start(WR[:, 3, 1664 + 256 * k:1920 + 256 * k].rearrange("p (h c) -> p h c", h=2),
                                 kvb[:, k, two, NOPE:NOPE + VD]).then_inc(landed[3], 16)
            moe_item(0, 0, 1)
            more = more_items(sp)
            with sp.Fori(0, more) as j:
                e = sp.value_load(TAB[0:1, bass.ds(j + 2 + TABLE, 1)], min_val=0, max_val=NE - 1)
                e_next = sp.value_load(TAB[0:1, bass.ds(j + 3 + TABLE, 1)], min_val=0, max_val=NE - 1)
                moe_item(j + 1, e, e_next)
            for g in range(NG):
                sp.wait_ge(ln_x, 3 * NG + g + 1)
                out = y_prompt[0] if g == 0 else y_sample[0, (g - 1) * P:g * P, :]
                sp.dma_start(out, X[:, g, :]).then_inc(out_done, 16)
            sp.wait_ge(out_done, 16 * NG)
            sp.wait_ge(kv_out, 32)

        @block.gpsimd
        def _(pool):
            ch = Chain(pool, pool_chain)
            pool.dma_start(CST[:, :], base_rows).then_inc(cst_in, 16)
            pool.dma_start(ROWS[0:12, :], ev_conv_w[0].rearrange("k (t p) -> (k t) p", p=P)).then_inc(rows_in, 16)
            pool.dma_start(ROWS[12:16, :], ev_pool_scale[0].rearrange("(t p) -> t p", p=P)).then_inc(rows_in, 16)
            pool.dma_start(ROWS[16:19, :], od_q_norm[0].rearrange("(t p) -> t p", p=P)).then_inc(rows_in, 16)
            pool.dma_start(ROWS[19:27, :], c_ctx.rearrange("(t p) -> t p", p=P)).then_inc(rows_in, 16)
            pool.dma_start(ROWS[27:35, :], c[0].rearrange("(t p) -> t p", p=P)).then_inc(rows_in, 16)
            pool.dma_start(PW, ev_pool_w[0].rearrange("g c d -> c g d")).then_inc(pw_in, 16)
            pool.dma_start(ICNT, pool_inv.partition_broadcast(P)).then_inc(icnt_in, 16)

            def ada_io(group):
                def bias(n):
                    l, p = divmod(n, NPANEL)
                    if n:
                        pool.wait_ge(st_b, n)
                        pool.wait_ge(st_a, n)
                    pool.dma_start(BROW[:, :], ada_b[l, p * PANEL:(p + 1) * PANEL].partition_broadcast(2))\
                        .then_inc(brow_in, 16)

                for n in group:
                    bias(n)
                    l, p = divmod(n, NPANEL)
                    pool.wait_ge(st_b, n + 1)
                    pool.wait_ge(st_a, n + 1)
                    pool.dma_start(mod_rows[l, :, p * PANEL:(p + 1) * PANEL], STG[:, n % 2, :])\
                        .then_inc(stored[n % 2], 16)

            def ln_params(l, j):
                done = 2 * l + j
                if done:
                    pool.wait_ge(ln_x, NG * done)
                for b in range(2):
                    pool.wait_ge(stored[b], 16 * NPANEL // 2 * (l + 1))
                at = (3 * j + 2) * D
                pool.dma_start(LG[:, :], ln_g[l, j].partition_broadcast(P)).then_inc(lnp_in, 16)
                pool.dma_start(LB[:, :], ln_b[l, j].partition_broadcast(P)).then_inc(lnp_in, 16)
                pool.dma_start(GB[:, :, :], mod_rows[l, :, at:at + D].partition_broadcast(P)).then_inc(lnp_in, 16)

            ada_io(ADA_GROUPS[0])
            ln_params(0, 0)
            pool.wait_ge(icnt_in, 16)
            pool.wait_ge(z_pad, 2)
            pool.wait_ge(u_dve, 4)
            for g, win in enumerate(WINDOWS):
                pool.wait_ge(u_act, 8 + g + 1)
                src, width, step, bufs = UP[:, g, :], UW, 1, (SA, SBB)
                while step < win:
                    width -= step
                    dst = bufs[0]
                    ch(pool.tensor_tensor(dst[:, 0:width], src[:, 0:width], src[:, step:step + width], ALU.add))
                    src, bufs, step = dst, (bufs[1], bufs[0]), step * 2
                for tok, at, n in SEGU:
                    lo = at - win // 2
                    ch(pool.tensor_tensor(PP[:, g, tok:tok + n], src[:, lo:lo + n], ICNT[:, g, tok:tok + n], ALU.mult))
                for tok, at, n in SEGU:
                    last = pool.tensor_tensor(PP[:, g, tok:tok + n], PP[:, g, tok:tok + n], UP[:, g, at:at + n], ALU.subtract)
                    if tok == 0:
                        ch(last)
                last.then_inc(pp_ready, 1)
            ada_io(ADA_GROUPS[1])
            pool.wait_ge(ln_x, NG)
            pool.wait_ge(g_ps, 1)
            pool.dma_start(OC, odd_rows).then_inc(oddc_in, 16)
            pool.dma_start(DC, dft_rows).then_inc(oddc_in, 16)
            pool.dma_start(KVN, od_kv_norm[0].partition_broadcast(P)).then_inc(kvn_in, 16)
            pool.dma_start(FNW, od_fnet_w[0].rearrange("(k p) n -> p k n", p=P)).then_inc(fnw_in, 16)
            pool.dma_start(CK, cache_ckv[0, 0]).then_inc(cache_in, 16)
            for b in range(2):
                pool.dma_start(KDUP[:, 1, b * ROPE:(b + 1) * ROPE], cache_kpe[0, 0]).then_inc(cache_in, 16)
            pool.wait_ge(ln_x, NG)
            pool.dma_start(LG[:, :], ln_g[0, 1].partition_broadcast(P)).then_inc(lnp_in, 16)
            pool.dma_start(LB[:, :], ln_b[0, 1].partition_broadcast(P)).then_inc(lnp_in, 16)
            pool.dma_start(GB[:, :, :], mod_rows[0, :, 5 * D:6 * D].partition_broadcast(P)).then_inc(lnp_in, 16)
            ada_io(ADA_GROUPS[2])
            ln_params(1, 0)
            for p in range(2 * NG):
                g, b = divmod(p, 2)
                if p == 0:
                    pool.wait_ge(odu, 2 * NG)
                last = pool.tensor_copy(KDUP[:, g if g == 0 else g + 1, b * ROPE:(b + 1) * ROPE],
                                        U[:, g, QR + KVR:QR + KVR + ROPE])
            last.then_inc(kd_ready, 1)
            pool.wait_ge(odn, 2)
            pool.dma_start(new_ckv[0, 0], U[:, 0, QR:QR + KVR]).then_inc(kv_out, 16)
            pool.dma_start(new_kpe[0, 0], U[:, 0, QR + KVR:QR + KVR + ROPE]).then_inc(kv_out, 16)
            ln_params(1, 1)
            pool.wait_ge(xt_t, 4 * 2 * NG)
            pool.dma_start(ROUT.rearrange("p (k e) -> p k e", k=KD),
                           moe_router[0].rearrange("(k p) e -> p k e", p=P)).then_inc(rout_in, 16)

        @block.scalar
        def _(act):
            act.wait_ge(cols_ready, 1)
            nc.scalar.activation(SC[:, :, :].rearrange("p k c -> p c k"),
                                 COLS[:, 19:35].rearrange("p (c k) -> p c k", c=2), ACT.Silu).then_inc(sc_ready, 1)

            def sqrt_of(n, at, count):
                act.wait_ge(var_ready, n)
                nc.scalar.activation(SM[:, at + count:at + 2 * count], SM[:, at:at + count], ACT.Sqrt).then_inc(sd_ready, 1)

            def modulate(st):
                l, j = divmod(st, 2)
                act.wait_ge(mt_ready, l + 1)
                for q in (0, 1, 2, 3, 5):
                    g, half = divmod(q, 2)
                    cond = min(g, 1)
                    act.wait_ge(xt_t, 2 * NG * st + q + 1)
                    for b in range(4):
                        k = half * 4 + b
                        last = nc.scalar.activation(HT[:, k, g * P:(g + 1) * P], PS[:, q, b * P:(b + 1) * P], ACT.Identity,
                                                    scale=MT[:, l, (3 * j + 1) * KD + k, cond:cond + 1],
                                                    bias=MT[:, l, 3 * j * KD + k, cond:cond + 1])
                    last.then_inc(ht_a, 1)

            modulate(0)
            for t in (0, 1, 2, 3, 4, 5, 6, 7, 12, 13, 14, 15):
                act.wait_ge(u_ps, t + 1)
                if t < 8:
                    dst = (UX, UB)[t // 4]
                    nc.scalar.copy(dst[:, t % 4, :], PS[:, t % 4, 0:TOK]).then_inc(u_act, 1)
                else:
                    act.wait_ge(z_pad, 2)
                    for tok, at, n in SEGU:
                        last = nc.scalar.copy(UP[:, t % 4, at:at + n], PS[:, t % 4, tok:tok + n])
                    last.then_inc(u_act, 1)
            for g in range(NPOOL):
                act.wait_ge(pm_ps, g + 1)
                nc.scalar.activation(MIX[:, 4 + g, :], PS[:, 6 + g % 2, 0:TOK], ACT.Identity,
                                     scale=COLS[:, 12 + g:13 + g]).then_inc(mix_pool, 1)
            sqrt_of(1, 0, NG)
            modulate(1)

            def high(piece, used_up):
                n, at, land = piece
                act.wait_ge(raw_in[at], land)
                if used_up is not None:
                    act.wait_ge(w_used, used_up)
                nc.scalar.copy(WS[:, at, 0, :], RAW[:, at, :]).then_inc(hi_done, 1)

            def ff_hidden(f, b):
                act.wait_ge(g_ps, f + 1)
                nc.scalar.activation(SIL, PS[:, 6, 0:TOK], ACT.Silu).then_inc(sil, 1)
                act.wait_ge(ff_h, f + 1)
                nc.scalar.copy(HFS[:, b, 0, :], HF).then_inc(fh_hi, 1)

            act.wait_ge(ht_d, 2)
            act.wait_ge(ht_a, 10)
            for k in range(KD):
                if k == 0:
                    act.wait_ge(mm_b, NPANEL + 4)
                nc.scalar.copy(HX[:, 0, k, :], HT[:, k, :]).then_inc(hx_hi, 1)
            for c in range(5):
                high(FF_FIRST[c], None)
            ff_hidden(0, 0)
            ff_hidden(1, 1)
            with act.Fori(0, FF_ITERS) as i:
                for b in range(2):
                    for c in range(RING):
                        high(ff_piece(i * 2 + b, c), ff_used(i * 2 + b, c))
                    ff_hidden(i * 4 + (2 + 2 * b), 0)
                    ff_hidden(i * 4 + (3 + 2 * b), 1)
            high(FF_LAST, FF_LAST_USED)
            sqrt_of(2, 0, NG)
            modulate(2)
            for q in range(2 * NG):
                h, g = divmod(q, NG)
                act.wait_ge(odi_ps, q + 1)
                nc.scalar.copy(U[:, g, h * 480:(h + 1) * 480], PS[:, q, 0:480]).then_inc(odu, 1)
            act.wait_ge(odu, 2 * NG)
            for g in range(NG):
                for b, (lo, n) in enumerate(((0, QR), (QR, KVR))):
                    last = nc.scalar.activation(T[:, b * 512:b * 512 + n], U[:, g, lo:lo + n], ACT.Square,
                                                accum_out=SM[:, 40 + 3 * b + g:41 + 3 * b + g])
                    act_last = last
                    if (g, b) != (NG - 1, 1):
                        act_last.then_inc(act_chain, 1)
                        act.wait_ge(act_chain, 2 * g + b + 1)
            act_last.then_inc(ssq, 1)
            sqrt_of(3, 64, 18)
            for q in range(6):
                act.wait_ge(odt_ps, q + 1)
                if q < 3:
                    ins = nc.scalar.activation(QHT[:, q, :], PS[:, q, 0:TOK], ACT.Identity, scale=COLS[:, 16 + q:17 + q])
                elif q < 5:
                    ins = nc.scalar.copy(CKT[:, q - 3, :], PS[:, q, :])
                else:
                    ins = nc.scalar.copy(KPT, PS[:, q, :])
                ins.then_inc(odt_a, 1)
            act.wait_ge(o_ready, 1)
            with act.Fori(0, NH // 2) as i:
                for q in range(3):
                    act.wait_ge(pj_ps, i * 7 + q + 1)
                    nc.scalar.copy(QN[:, q, :] if q < 2 else QP, PS[:, q, 0:TOK]).then_inc(pj_a, 1)
                for cc in range(NC6 + 2):
                    if cc < NC6:
                        n = P * (keys(COMBOS[cc][1])[1] - keys(COMBOS[cc][1])[0])
                        act.wait_ge(nmax, i * NC6 + cc + 1)
                        nc.scalar.activation(PB[:, cc % 2, 0:n], PS[:, cc % 2, 0:n], ACT.Exp, scale=SCALE,
                                             bias=SM[:, 104 + cc % 2:105 + cc % 2],
                                             accum_out=SM[:, 106 + cc % 2:107 + cc % 2]).then_inc(e_done, 1)
                    if cc >= 2:
                        b = cc - 2
                        n = P * (keys(COMBOS[b][1])[1] - keys(COMBOS[b][1])[0])
                        act.wait_ge(pt_ps, i * NC6 + b + 1)
                        nc.scalar.copy(PTB[:, b % 2, 0:n], PS[:, 2 + b % 2, 0:n]).then_inc(pt_ready, 1)
            sqrt_of(4, 0, NG)
            modulate(3)
            for q in range(2 * NG):
                g, half = divmod(q, 2)
                act.wait_ge(hkt_ps, q + 1)
                nc.scalar.copy(HK[:, g, half * 512:(half + 1) * 512], PS[:, 1 + q, :]).then_inc(hk, 1)
            act.wait_ge(d_ready, 1)
            nc.scalar.activation(MS[:, 3:6], MS[:, 0:3], ACT.Exp).then_inc(ex_ready, 1)

            def dispatched(i):
                act.wait_ge(disp_ps, i + 1)
                nc.scalar.copy(XES[:, 0, :], PS[:, 4:6, :].rearrange("p a n -> p (a n)")).then_inc(xe_hi, 1)

            def y_out(i):
                act.wait_ge(yd, i)
                nc.scalar.copy(YSB, PS[:, 2:4, :].rearrange("p a n -> p (a n)")).then_inc(ysb, 1)

            def item(i, first):
                for u in range(UNITS_E):
                    v = i * UNITS_E + u
                    act.wait_ge(gu_ps, v + 1)
                    nc.scalar.activation(ESIL, PS[:, 0, 0:UCOL], ACT.Silu).then_inc(esil, 1)
                    if u == UNITS_E - 1:
                        dispatched(i + 1)
                    for c in range(2):
                        high(e_piece(v, c), e_used(v, c))
                    if u == 0 and not first:
                        y_out(i)
                    act.wait_ge(t_ps, v + 1)
                    nc.scalar.copy(EHS[:, 0, :], PS[:, 1, 0:UCOL]).then_inc(eht_hi, 1)
                    for c in range(2, RING):
                        high(e_piece(v, c), e_used(v, c))

            more = more_items(act)
            act.wait_ge(y_ps, 3 * NG)
            for c in range(4):
                high(E_FIRST[c], None)
            dispatched(0)
            item(0, True)
            with act.Fori(0, more) as j:
                item(j + 1, False)
            y_out(more + 1)
            sqrt_of(5, 0, NG)

        @block.vector
        def _(dve):
            ch = Chain(dve, dve_chain)
            V = nc.vector
            for ct in range(4):
                V.memset(Z[:, ct, :], 0.0)
                V.memset(UP[:, ct, :], 0.0).then_inc(z_pad, 1) if ct >= 2 else V.memset(UP[:, ct, :], 0.0)
            dve.wait_ge(z_pad, 2)
            dve.wait_ge(rows_t, 1)
            V.tensor_copy(COLS[:, :], PS[:, 0, 0:35]).then_inc(cols_ready, 1)

            def ada(group):
                def cols(n):
                    l, p = divmod(n, NPANEL)
                    k = PANEL // P
                    dve.wait_ge(cols_t, n + 1)
                    V.tensor_copy(MT[:, l, p * k:(p + 1) * k, :],
                                  PS[:, 7, 384:384 + 2 * k].rearrange("p (k c) -> p k c", c=2)).then_inc(cols_done, 1)

                for n in group:
                    dve.wait_ge(mm_a, n + 1)
                    dve.wait_ge(brow_in, 16 * (n + 1))
                    if n >= 2:
                        dve.wait_ge(stored[n % 2], 16 * (n // 2))
                        dve.wait_ge(cols_t, n - 1)
                    V.tensor_tensor(STG[:, n % 2, 0:384], PS[0:2, 6, 0:384], BROW[:, 0:384], ALU.add).then_inc(st_a, 1)
                    if n > group[0]:
                        cols(n - 1)
                    dve.wait_ge(mm_b, n + 1)
                    V.tensor_tensor(STG[:, n % 2, 384:768], PS[0:2, 7, 0:384], BROW[:, 384:768], ALU.add)\
                        .then_inc(st_b, 1)
                cols(group[-1])
                l, p = divmod(group[-1], NPANEL)
                if p == NPANEL - 1:
                    dve.wait_ge(cols_done, group[-1] + 1)
                    for j in range(2):
                        part = MT[:, l, (3 * j + 1) * KD:(3 * j + 2) * KD, :]
                        last = V.tensor_scalar(part, part, 1.0, None, ALU.add)
                    last.then_inc(mt_ready, 1)

            def rsqrt(n, at, count):
                v, r, w = SM[:, at:at + count], SM[:, at + count:at + 2 * count], SM[:, 112:112 + count]
                dve.wait_ge(sd_ready, n)
                ch(V.reciprocal(r, r))
                ch(V.tensor_tensor(w, v, r, ALU.mult))
                ch(V.tensor_tensor(w, w, r, ALU.mult))
                ch(V.tensor_scalar(w, w, -0.5, 1.5, ALU.mult, ALU.add))
                ch(V.tensor_tensor(r, r, w, ALU.mult))

            def layer_norm(st, n_sd, y_of):
                dve.wait_ge(lnp_in, 48 * (st + 1))
                for g in range(NG):
                    y = y_of(g)
                    ch(V.tensor_tensor(T[:, :], y, GB[:, min(g, 1), :], ALU.mult))
                    ch(V.scalar_tensor_tensor(X[:, g, :], X[:, g, :], ALPHA, T[:, :], ALU.mult, ALU.add))
                    for b in range(2):
                        ch(V.bn_stats(SM[:, 16 + 6 * b:22 + 6 * b], X[:, g, b * 512:(b + 1) * 512]))
                    ch(V.bn_aggr(SM[:, 28 + 2 * g:30 + 2 * g], SM[:, 16:28]))
                V.tensor_scalar(SM[:, 0:NG], SM[:, 29:29 + 2 * NG:2], LN_EPS, None, ALU.add).then_inc(var_ready, 1)
                rsqrt(n_sd, 0, NG)
                for g in range(NG):
                    x = X[:, g, :]
                    ch(V.tensor_scalar(x, x, SM[:, 28 + 2 * g:29 + 2 * g], SM[:, NG + g:NG + g + 1], ALU.subtract, ALU.mult))
                    ch(V.tensor_tensor(x, x, LG[:, :], ALU.mult))
                    V.tensor_tensor(x, x, LB[:, :], ALU.add).then_inc(ln_x, 1)
                dve.wait_ge(ln_x, NG * (st + 1))

            def y_psum(st):
                def y(g):
                    dve.wait_ge(y_ps, NG * st + g + 1)
                    return PS[:, 2 * g:2 * g + 2, :].rearrange("p a n -> p (a n)")
                return y

            def modulate(st):
                l, j = divmod(st, 2)
                dve.wait_ge(mt_ready, l + 1)
                dve.wait_ge(xt_t, 2 * NG * st + 5)
                for k in range(4):
                    last = V.tensor_scalar(HT[:, k, 2 * P:3 * P], PS[:, 4, k * P:(k + 1) * P],
                                           MT[:, l, (3 * j + 1) * KD + k, 1:2], MT[:, l, 3 * j * KD + k, 1:2],
                                           ALU.mult, ALU.add)
                last.then_inc(ht_d, 1)

            ada(ADA_GROUPS[0])
            modulate(0)
            for ct in range(4):
                dve.wait_ge(u_ps, 8 + ct + 1)
                dve.wait_ge(u_act, 8)
                for tok, at, n in SEGZ:
                    last = V.tensor_tensor(Z[:, ct, at:at + n], PS[:, ct, tok:tok + n], UX[:, ct, tok:tok + n], ALU.mult)
                last.then_inc(u_dve, 1)
            dve.wait_ge(u_dve, 4)
            for ct in range(4):
                w = ZW - 2
                tap = lambda k: COLS[:, 4 * k + ct:4 * k + ct + 1]
                if ct:
                    dve.wait_ge(mix_conv, ct)
                ch(V.tensor_scalar(CV[:, 0:w], Z[:, ct, 0:w], tap(0), None, ALU.mult))
                ch(V.scalar_tensor_tensor(CV[:, 0:w], Z[:, ct, 1:1 + w], tap(1), CV[:, 0:w], ALU.mult, ALU.add))
                ch(V.scalar_tensor_tensor(CV[:, 0:w], Z[:, ct, 2:2 + w], tap(2), CV[:, 0:w], ALU.mult, ALU.add))
                for tok, at, n in SEGZ:
                    last = V.tensor_tensor(MIX[:, ct, tok:tok + n], CV[:, at - 1:at - 1 + n], UB[:, ct, tok:tok + n], ALU.mult)
                last.then_inc(mix_conv, 1)
            layer_norm(0, 1, y_psum(0))
            modulate(1)
            ada(ADA_GROUPS[1])

            def low(piece):
                n, at, _ = piece
                dve.wait_ge(hi_done, n + 1)
                V.tensor_tensor(WS[:, at, 1, :], RAW[:, at, :], WS[:, at, 0, :].bitcast(F32), ALU.subtract)\
                    .then_inc(lo_done, 1)

            def ff_hidden(f, b):
                dve.wait_ge(sil, f + 1)
                dve.wait_ge(up_ps, f + 1)
                if not (isinstance(f, int) and f == 0):
                    dve.wait_ge(fh_lo, f)
                V.tensor_tensor(HF, SIL, PS[:, 7, 0:TOK], ALU.mult).then_inc(ff_h, 1)
                dve.wait_ge(fh_hi, f + 1)
                V.tensor_tensor(HFS[:, b, 1, :], HF, HFS[:, b, 0, :].bitcast(F32), ALU.subtract).then_inc(fh_lo, 1)

            for k in range(KD):
                dve.wait_ge(hx_hi, k + 1)
                V.tensor_tensor(HX[:, 1, k, :], HT[:, k, :], HX[:, 0, k, :].bitcast(F32), ALU.subtract).then_inc(hx_lo, 1)
            for c in range(5):
                low(FF_FIRST[c])
            ff_hidden(0, 0)
            ff_hidden(1, 1)
            with dve.Fori(0, FF_ITERS) as i:
                for b in range(2):
                    for c in range(RING):
                        low(ff_piece(i * 2 + b, c))
                    ff_hidden(i * 4 + (2 + 2 * b), 0)
                    ff_hidden(i * 4 + (3 + 2 * b), 1)
            low(FF_LAST)
            layer_norm(1, 2, y_psum(1))
            ada(ADA_GROUPS[2])
            modulate(2)

            dve.wait_ge(odu, 2 * NG)
            f0 = QR + KVR + ROPE
            dve.wait_ge(ssq, 1)
            for g in range(NG):
                for b in range(FG):
                    at = 6 * (g * FG + b)
                    ch(V.bn_stats(T[:, at:at + 6], U[:, g, f0 + b * FGD:f0 + (b + 1) * FGD]))
                    ch(V.bn_aggr(T[:, 100 + at:102 + at], T[:, at:at + 6]))
            ch(V.tensor_scalar(SM[:, 64:67], SM[:, 40:43], 1.0 / QR, RMS_EPS, ALU.mult, ALU.add))
            ch(V.tensor_scalar(SM[:, 67:70], SM[:, 43:46], 1.0 / KVR, RMS_EPS, ALU.mult, ALU.add))
            V.tensor_scalar(SM[:, 70:82], T[:, 101:101 + 72:6], LN_EPS, None, ALU.add).then_inc(var_ready, 1)
            dve.wait_ge(var_ready, 3)
            rsqrt(3, 64, 18)
            for g in range(NG):
                last = V.tensor_scalar(U[:, g, 0:QR], U[:, g, 0:QR], SM[:, 82 + g:83 + g], None, ALU.mult)
            last.then_inc(odn, 1)
            dve.wait_ge(kvn_in, 16)
            for g in range(NG):
                last = V.scalar_tensor_tensor(U[:, g, QR:QR + KVR], U[:, g, QR:QR + KVR], SM[:, 85 + g:86 + g], KVN,
                                              ALU.mult, ALU.mult)
            last.then_inc(odn, 1)
            for g in range(NG):
                for b in range(FG):
                    j = g * FG + b
                    part = U[:, g, f0 + b * FGD:f0 + (b + 1) * FGD]
                    last = V.tensor_scalar(part, part, T[:, 100 + 6 * j:101 + 6 * j], SM[:, 88 + j:89 + j],
                                           ALU.subtract, ALU.mult)
            last.then_inc(odn, 1)

            def rope(x, ps, signal):
                ch(V.tensor_tensor(T[:, 512:768], x, odc("cos"), ALU.mult))
                ch(V.tensor_tensor(T[:, 768:1024], ps, odc("sin"), ALU.mult))
                V.tensor_tensor(x, T[:, 512:768], T[:, 768:1024], ALU.add).then_inc(signal, 1)

            dve.wait_ge(oddc_in, 32)
            dve.wait_ge(odt_a, 6)
            dve.wait_ge(rot_ps, 1)
            rope(KPT[:, 2 * P:4 * P], PS[:, 6, 0:DEC], kpt_ready)
            for q in range(4):
                j, seg = divmod(q, 2)
                dve.wait_ge(f1_ps, q + 1)
                dst = FA[:, j, 0:256] if seg == 0 else FA[:, j, 256:768]
                V.tensor_copy(dst, PS[:, q, 0:256 if seg == 0 else 512]).then_inc(fa, 1)
            for j in range(2):
                dve.wait_ge(f2_ps, j + 1)
                V.tensor_copy(FT[:, j, :], PS[:, 4 + j, 0:TOK]).then_inc(ft, 1)
            for j in range(2):
                dve.wait_ge(f3_ps, j + 1)
                V.tensor_copy(GT[:, j, :], PS[:, j, 0:TOK]).then_inc(gt if j == 0 else o_ready, 1)

            per = 2 + NC6 * 2
            base = ch.n
            with dve.Fori(0, NH // 2) as i:
                ch.n = i * per + base
                for q in range(3, 7):
                    dve.wait_ge(pj_ps, i * 7 + q + 1)
                    dst = KT[:, q - 3, :] if q < 5 else VV[:, 2 * (q - 5):2 * (q - 5) + 2, :].rearrange("p a n -> p (a n)")
                    V.tensor_copy(dst, PS[:, q, :]).then_inc(pj_d, 1)
                dve.wait_ge(pj_a, i * 3 + 3)
                dve.wait_ge(qrot_ps, i + 1)
                rope(QP[:, P:3 * P], PS[:, 7, 0:DEC], qp_ready)
                for cc in range(NC6 + 3):
                    if cc < NC6:
                        n = P * (keys(COMBOS[cc][1])[1] - keys(COMBOS[cc][1])[0])
                        mx, nm = SM[:, 108 + cc % 2:109 + cc % 2], SM[:, 104 + cc % 2:105 + cc % 2]
                        dve.wait_ge(s_ps, i * NC6 + cc + 1)
                        ch(V.reduce_max(mx, PS[:, cc % 2, 0:n], AX.X))
                        V.tensor_scalar(nm, mx, -SCALE, None, ALU.mult).then_inc(nmax, 1)
                    if 1 <= cc <= NC6:
                        b = cc - 1
                        n = P * (keys(COMBOS[b][1])[1] - keys(COMBOS[b][1])[0])
                        den = SM[:, 106 + b % 2:107 + b % 2]
                        dve.wait_ge(e_done, i * NC6 + b + 1)
                        ch(V.reciprocal(SM[:, 110 + b % 2:111 + b % 2], den))
                        V.tensor_scalar(PB[:, b % 2, 0:n], PB[:, b % 2, 0:n], SM[:, 110 + b % 2:111 + b % 2], None,
                                        ALU.mult).then_inc(p_ready, 1)
                    if cc >= 3:
                        b = cc - 3
                        h, qt = COMBOS[b]
                        dve.wait_ge(o_ps, i * NC6 + b + 1)
                        V.tensor_copy(HT[:, bass.ds(i * 2 + h, 1), qt * P:(qt + 1) * P],
                                      PS[:, 4 + b % 2:5 + b % 2, 0:P]).then_inc(o_ready, 1)
            ch.n = base + per * (NH // 2)
            layer_norm(2, 4, y_psum(2))
            modulate(3)

            b3 = lambda a: a.unsqueeze(2).broadcast_to([P, NG, NE])
            cut = iter(range(8, 900, 24))
            take = lambda: MS[:, next(cut) + 4:][:, 0:24].rearrange("p (g e) -> p g e", g=NG)
            L, EQ, VI, K1, K2, L2, G, G2, M, PMX = (take() for _ in range(10))
            small = MS[:, 270:300]
            m1, m2, im, w1, w2 = (small[:, 3 * j:3 * j + 3] for j in range(5))
            eidx = cst("expert").rearrange("p (g e) -> p g e", g=NG)
            dve.wait_ge(lg_ps, 1)
            ch(V.tensor_copy(L, PS[:, 0, 0:24].rearrange("p (g e) -> p g e", g=NG)))

            def best(src, m, k):
                ch(V.tensor_reduce(m, src, AX.X, ALU.max))
                ch(V.tensor_tensor(EQ, src, b3(m), ALU.is_equal))
                ch(V.scalar_tensor_tensor(VI, EQ, -100.0, eidx, ALU.mult, ALU.add))
                ch(V.tensor_reduce(im, VI, AX.X, ALU.min))
                ch(V.tensor_tensor(k, VI, b3(im), ALU.is_equal))

            best(L, m1, K1)
            ch(V.scalar_tensor_tensor(L2, K1, -1e30, L, ALU.mult, ALU.add))
            best(L2, m2, K2)
            V.tensor_tensor(M, K1, K2, ALU.add).then_inc(m_ready, 1)
            V.tensor_tensor(MS[:, 0:3], m2, m1, ALU.subtract).then_inc(d_ready, 1)
            V.memset(YACC.rearrange("p a n -> p (a n)"), 0.0).then_inc(cb_done, 1)
            dve.wait_ge(ex_ready, 1)
            ch(V.tensor_scalar(w1, MS[:, 3:6], 1.0, None, ALU.add))
            ch(V.reciprocal(w1, w1))
            ch(V.tensor_tensor(w2, MS[:, 3:6], w1, ALU.mult))
            ch(V.tensor_tensor(G, K1, b3(w1), ALU.mult))
            ch(V.tensor_tensor(G2, K2, b3(w2), ALU.mult))
            ch(V.tensor_tensor(G, G, G2, ALU.add))
            dve.wait_ge(m_ready, 1)
            dve.wait_ge(pos_ps, 1)
            ch(V.scalar_tensor_tensor(PMX, PS[:, 7, 0:24].rearrange("p (g e) -> p g e", g=NG), 1.0, M, ALU.add, ALU.mult))
            posa = POSA.rearrange("p (r e g) -> p r e g", r=3, e=NE)
            ga = GA.rearrange("p (r e g) -> p r e g", r=3, e=NE)
            for r in range(3):
                V.tensor_scalar(posa[:, r].rearrange("p e g -> p g e"), PMX, -1.0 - P * r, None, ALU.add)
                last = V.tensor_copy(ga[:, r].rearrange("p e g -> p g e"), G)
            last.then_inc(pos_ready, 1)
            row = lambda at, n: MS[0:1, at:at + n]
            EX, PF, IX, CB, TF = row(320, 16), row(336, 16), row(352, 16), row(370, 256), row(640, 33)
            cand = lambda name: cst(name, 1)
            for r in range(2):
                ch(V.tensor_scalar(EX.rearrange("o (e r) -> o e r", r=2)[:, :, r], PS[0:1, 7, 24:32], float(P * (r + 1)), None,
                                   ALU.is_gt))
            ch(V.tensor_tensor_scan(PF, cst("ones", 1)[:, 0:16], EX, 0.0, ALU.mult, ALU.add))
            ch(V.scalar_tensor_tensor(IX, PF, float(NE), EX, ALU.add, ALU.mult))
            ch(V.tensor_scalar(IX, IX, -1.0, None, ALU.add))
            cb = CB.rearrange("o (j c) -> o j c", j=TABLE)
            jc = [1, TABLE, 16]
            ch(V.tensor_scalar(TF[:, 0:1], PF[:, 15:16], float(NE - 1), None, ALU.add))
            for b, name in enumerate(("cand_code", "cand_expert")):
                part = TF[:, 1 + TABLE * b:1 + TABLE * (b + 1)]
                ch(V.tensor_tensor(cb, cand("item").unsqueeze(2).broadcast_to(jc), IX.unsqueeze(1).broadcast_to(jc),
                                   ALU.is_equal))
                ch(V.tensor_tensor(cb, cb, cand(name).unsqueeze(1).broadcast_to(jc), ALU.mult))
                ch(V.tensor_reduce(part, cb, AX.X, ALU.add))
                ch(V.tensor_tensor(part, part, cand("base"), ALU.add))
            V.tensor_copy(TAB[:, :], TF).then_inc(tab_ready, 1)
            dve.wait_ge(pos_ready, 1)
            more = more_items(dve)

            def one_hot(dst, i, gated, signal):
                code = dve.value_load(TAB[0:1, bass.ds(i + 1, 1)] if not isinstance(i, int) else TAB[0:1, i + 1:i + 2],
                                      min_val=0, max_val=CODES - 1)
                for g in range(NG):
                    at = bass.ds(code * NG + g, 1)
                    last = V.tensor_scalar(dst[:, g, :], cst("iota"), POSA[:, at], GA[:, at] if gated else None,
                                           ALU.is_equal, ALU.mult) if gated else \
                        V.tensor_scalar(dst[:, g, :], cst("iota"), POSA[:, at], None, ALU.is_equal)
                last.then_inc(signal, 1)

            def turned(i):
                dve.wait_ge(ptt_ps, i)
                V.tensor_copy(PT.rearrange("p a n -> p (a n)"), PS[:, 6, 0:TOK]).then_inc(pt_sb, 1)

            def combined(j, q):
                g, half = divmod(q, 2)
                y = YACC[:, g, half * 512:(half + 1) * 512]
                dve.wait_ge(cb_ps, j * 2 * NG + q + 1)
                V.tensor_tensor(y, PS[:, 6 + q % 2, :], y, ALU.add).then_inc(cb_done, 1)

            def dispatched(i):
                dve.wait_ge(xe_hi, i + 1)
                V.tensor_tensor(XES[:, 1, :], PS[:, 4:6, :].rearrange("p a n -> p (a n)"), XES[:, 0, :].bitcast(F32),
                                ALU.subtract).then_inc(xe_done, 1)

            def item(i, first, j=0):
                dve.wait_ge(disp_ps, i + 1)
                one_hot(PM, i + 1, False, mp_ready)
                if not first:
                    one_hot(PG, j, True, pg_ready)
                for u in range(UNITS_E):
                    v = i * UNITS_E + u
                    dve.wait_ge(esil, v + 1)
                    V.tensor_tensor(EH, ESIL, PS[:, 0, UCOL:2 * UCOL], ALU.mult).then_inc(eh, 1)
                    if u == UNITS_E - 1:
                        dispatched(i + 1)
                    for c in range(2):
                        low(e_piece(v, c))
                    if u == 0 and not first:
                        turned(i)
                    dve.wait_ge(eht_hi, v + 1)
                    V.tensor_tensor(EHS[:, 1, :], PS[:, 1, 0:UCOL], EHS[:, 0, :].bitcast(F32), ALU.subtract)\
                        .then_inc(eht_lo, 1)
                    for c in range(2, RING):
                        low(e_piece(v, c))
                    if u in (1, 2, 3) and not first:
                        if u == 1:
                            dve.wait_ge(cb_done, j * 2 * NG + 1)
                        for q in (2 * u - 2, 2 * u - 1):
                            combined(j, q)

            one_hot(PM, 0, False, mp_ready)
            for c in range(4):
                low(E_FIRST[c])
            dispatched(0)
            item(0, True)
            with dve.Fori(0, more) as j:
                item(j + 1, False, j)
            one_hot(PG, more, True, pg_ready)
            turned(more + 1)
            dve.wait_ge(cb_done, more * 2 * NG + 1)
            for q in range(2 * NG):
                combined(more, q)
            dve.wait_ge(cb_done, more * 2 * NG + (2 * NG + 1))
            layer_norm(3, 5, lambda g: YACC[:, g, :])

        @block.tensor
        def _(pe):
            mm, tr = nc.tensor.matmul, nc.tensor.transpose
            pe.wait_ge(cst_in, 16)
            pe.wait_ge(rows_in, 80)
            tr(PS[:, 0, 0:35], ROWS[:, :], ident[0:35, 0:35]).then_inc(rows_t, 1)

            def ada(group, after=None):
                def turn(n):
                    pe.wait_ge(st_a, n + 1)
                    pe.wait_ge(st_b, n + 1)
                    for k in range(PANEL // P):
                        last = tr(PS[:, 7, 384 + 2 * k:386 + 2 * k], STG[:, n % 2, k * P:(k + 1) * P], ident[0:2, 0:2])
                        if k == 0:
                            release(last, ("ada", n))
                    last.then_inc(cols_t, 1)

                for n in group:
                    w = slot(("ada", n)).rearrange("p (k n) -> p k n", k=KD)
                    wait_unit(pe, ("ada", n))
                    if n:
                        pe.wait_ge(st_a, n)
                    for h in range(2):
                        if h:
                            if n > group[0]:
                                turn(n - 1)
                                pe.wait_ge(cols_done, n)
                        for k in range(KD):
                            last = mm(PS[0:2, 6 + h, 0:384], SC[:, k, :], w[:, k, h * 384:(h + 1) * 384],
                                      start=(k == 0), stop=(k == KD - 1))
                            if (n, h, k) == (group[0], 0, 0) and after:
                                last.then_inc(used[after[0]], 1)
                        last.then_inc((mm_a, mm_b)[h], 1)
                turn(group[-1])
                pe.wait_ge(cols_done, group[-1] + 1)

            def release(ins, name):
                ins.then_inc(used[ring.units[name][0]], 1)

            def x_turned(st, after=None):
                for q in range(2 * NG):
                    g, half = divmod(q, 2)
                    if half == 0:
                        pe.wait_ge(ln_x, NG * (st - 1) + g + 1) if st else pe.wait_ge(x_in, 32)
                    for b in range(4):
                        k = half * 4 + b
                        last = tr(PS[:, q, b * P:(b + 1) * P], X[:, g, k * P:(k + 1) * P], ident)
                        if (q, b) == (0, 0) and after:
                            release(last, after)
                    last.then_inc(xt_t, 1)

            def h_ready(st):
                pe.wait_ge(ht_a, 5 * (st + 1))
                pe.wait_ge(ht_d, st + 1)

            pe.wait_ge(sc_ready, 1)
            ada(ADA_GROUPS[0])
            x_turned(0)
            h_ready(0)
            for t in range(16):
                w = slot(("evin", t // 4))[:, 0:4096].rearrange("p (k n) -> p k n", k=KD)
                if t % 4 == 0:
                    wait_unit(pe, ("evin", t // 4))
                if 4 <= t < 12:
                    pe.wait_ge(u_act, t - 3)
                if t >= 12:
                    pe.wait_ge(u_dve, t - 11)
                for k in range(KD):
                    last = mm(PS[:, t % 4, 0:TOK], w[:, k, (t % 4) * P:(t % 4 + 1) * P], HT[:, k, :],
                              start=(k == 0), stop=(k == KD - 1))
                    if t % 4 == 0 and t and k == 0:
                        release(last, ("evin", t // 4 - 1))
                last.then_inc(u_ps, 1)
            pe.wait_ge(pw_in, 16)
            for g in range(NPOOL):
                pe.wait_ge(pp_ready, g + 1)
                if g >= 2:
                    pe.wait_ge(mix_pool, g - 1)
                mm(PS[:, 6 + g % 2, 0:TOK], PW[:, g, :], PP[:, g, :], start=True, stop=True).then_inc(pm_ps, 1)

            def project_out(units, per, lhs, ready, after=None):
                n = len(units) * per
                for k in range(n):
                    w = slot(units[k // per])[:, 0:per * D].rearrange("p (k n) -> p k n", k=per)
                    if k % per == 0:
                        wait_unit(pe, units[k // per])
                    ready(k)
                    for g in range(NG):
                        for h in range(2):
                            last = mm(PS[:, 2 * g + h, :], lhs(k)[:, g * P:(g + 1) * P], w[:, k % per, h * 512:(h + 1) * 512],
                                      start=(k == 0), stop=(k == n - 1))
                            if (k, g, h) == (0, 0, 0) and after:
                                release(last, after)
                        if k == n - 1:
                            last.then_inc(y_ps, 1)
                    if k % per == per - 1 and k < n - 1:
                        release(last, units[k // per])

            def mix_ready(k):
                if k == 0:
                    pe.wait_ge(u_act, 12)
                    pe.wait_ge(mix_pool, 4)
                if k < 4:
                    pe.wait_ge(mix_conv, k + 1)

            project_out([("evout", 0), ("evout", 1)], 4, lambda k: MIX[:, k, :], mix_ready, ("evin", 3))
            x_turned(1, ("evout", 1))
            ada(ADA_GROUPS[1])
            h_ready(1)

            def product(out, left, right, start, stop):
                (lh, ll), (rh, rl) = left, right
                first = mm(out, lh, rh, start=start, stop=False)
                mm(out, lh, rl, start=False, stop=False)
                return first, mm(out, ll, rh, start=False, stop=stop)

            def halves(buf, *at):
                return buf[(slice(None), 0) + at], buf[(slice(None), 1) + at]

            def gate_up_w(piece, k, cols):
                at = (k % 2) * 2 * UCOL
                return tuple(WS[:, piece[1], part, at + cols.start:at + cols.stop] for part in range(2))

            def down_w(piece, h):
                return tuple(WS[:, piece[1], part, h * 512:(h + 1) * 512] for part in range(2))

            def ff_gate_up(f, b, four):
                if not (isinstance(f, int) and f == 0):
                    pe.wait_ge(ff_h, f)
                for j, sig in enumerate((g_ps, up_ps)):
                    for k in range(KD):
                        if (b, j, k % 2) == (0, 0, 0):
                            pe.wait_ge(lo_done, four[k // 2][0] + 1)
                        if isinstance(f, int) and (f, j) == (0, 0):
                            pe.wait_ge(hx_lo, k + 1)
                        cols = slice(j * UCOL + b * P, j * UCOL + (b + 1) * P)
                        _, last = product(PS[:, 6 + j, 0:TOK], gate_up_w(four[k // 2], k, cols), halves(HX, k),
                                          k == 0, k == KD - 1)
                        if (b, j, k % 2) == (1, 1, 1) and k < KD - 1:
                            last.then_inc(w_used, 1)
                    last.then_inc(sig, 1)

            def ff_down(f, b, piece, start=False, stop=False, after=False):
                pe.wait_ge(fh_lo, f + 1)
                pe.wait_ge(lo_done, piece[0] + 1)
                for g in range(NG):
                    for h in range(2):
                        left = tuple(HFS[:, b, part, g * P:(g + 1) * P] for part in range(2))
                        first, last = product(PS[:, 2 * g + h, :], left, down_w(piece, h), start, stop)
                        if after and (g, h) == (0, 0):
                            first.then_inc(w_used, 1)
                    if stop:
                        last.then_inc(y_ps, 1)
                if not stop:
                    last.then_inc(w_used, 1)

            ff_gate_up(0, 0, FF_FIRST[0:4])
            ff_gate_up(1, 1, FF_FIRST[0:4])
            ff_down(0, 0, FF_FIRST[4], start=True, after=True)
            with pe.Fori(0, FF_ITERS) as i:
                for b in range(2):
                    f = i * 4 + (2 + 2 * b)
                    unit = [ff_piece(i * 2 + b, c) for c in range(RING)]
                    ff_gate_up(f, 0, unit[0:4])
                    ff_down(f - 1, 1, unit[4])
                    ff_gate_up(f + 1, 1, unit[0:4])
                    ff_down(f, 0, unit[5], after=True)
            ff_down(NF - 1, 1, FF_LAST, stop=True)
            ada(ADA_GROUPS[2])
            x_turned(2)
            h_ready(2)
            for q in range(2 * NG):
                h, g = divmod(q, NG)
                w = slot(("odin", h))[:, 0:3840].rearrange("p (k n) -> p k n", k=KD)
                if g == 0:
                    wait_unit(pe, ("odin", h))
                for k in range(KD):
                    last = mm(PS[:, q, 0:480], HT[:, k, g * P:(g + 1) * P], w[:, k, :], start=(k == 0), stop=(k == KD - 1))
                    if (q, k) == (NG, 0):
                        release(last, ("odin", 0))
                last.then_inc(odi_ps, 1)
            pe.wait_ge(odu, 2 * NG)
            pe.wait_ge(odn, 1)
            for q in range(3):
                for g in range(NG):
                    last = tr(PS[:, q, g * P:(g + 1) * P], U[:, g, q * P:(q + 1) * P], ident)
                    if (q, g) == (0, 0):
                        release(last, ("odin", 1))
                last.then_inc(odt_ps, 1)
            pe.wait_ge(cache_in, 48)
            pe.wait_ge(odn, 2)
            for q in range(2):
                for kg in range(4):
                    src = CK[:, q * P:(q + 1) * P] if kg == 1 else U[:, max(kg - 1, 0), QR + q * P:QR + (q + 1) * P]
                    last = tr(PS[:, 3 + q, kg * P:(kg + 1) * P], src, ident)
                last.then_inc(odt_ps, 1)
            pe.wait_ge(kd_ready, 1)
            for kg in range(4):
                last = tr(PS[:, 5, kg * P:(kg + 1) * P], KDUP[:, kg, :], ident)
            last.then_inc(odt_ps, 1)
            pe.wait_ge(oddc_in, 32)
            pe.wait_ge(odt_a, 6)
            mm(PS[:, 6, 0:DEC], odc("rot"), KPT[:, 2 * P:4 * P], start=True, stop=True).then_inc(rot_ps, 1)
            pe.wait_ge(odn, 3)
            dl = dft("latent").rearrange("p (k n) -> p k n", k=2)
            f0 = QR + KVR + ROPE
            for j in range(2):
                cols = slice(f0 + j * P, f0 + (j + 1) * P)
                mm(PS[:, 2 * j, 0:256], U[:, 0, cols], dft("prompt"), start=True, stop=True).then_inc(f1_ps, 1)
                for k in range(2):
                    last = mm(PS[:, 2 * j + 1, :], U[:, 1 + k, cols], dl[:, k, :], start=(k == 0), stop=(k == 1))
                last.then_inc(f1_ps, 1)
            for j in range(2):
                pe.wait_ge(fa, 2 * j + 2)
                for lo, n, a in ((0, SEQ, 0), (SEQ, DEC, 256)):
                    mm(PS[:, 4 + j, lo:lo + n], odc("chan_cos"), FA[:, j, a:a + n], start=True, stop=False)
                    last = mm(PS[:, 4 + j, lo:lo + n], odc("chan_nsin"), FA[:, j, a + n:a + 2 * n], start=False, stop=True)
                last.then_inc(f2_ps, 1)
            pe.wait_ge(fnw_in, 16)
            pe.wait_ge(ft, 2)
            for j in range(2):
                for k in range(2):
                    last = mm(PS[:, j, 0:TOK], FNW[:, k, j * P:(j + 1) * P], FT[:, k, :], start=(k == 0), stop=(k == 1))
                last.then_inc(f3_ps, 1)
            pe.wait_ge(kpt_ready, 1)

            wq = WR[:, 3, 0:768].rearrange("p (k h c) -> p k h c", k=3, h=2)
            wp = WR[:, 3, 768:1152].rearrange("p (k n) -> p k n", k=3)
            wk = WR[:, 3, 1152:1664].rearrange("p (k h c) -> p k h c", k=2, h=2)
            wv = WR[:, 3, 1664:2176].rearrange("p (k n) -> p k n", k=2)
            with pe.Fori(0, NH // 2) as i:
                pe.wait_ge(landed[3], i * 16 * PAIR_DMAS + (pair_base[0][3] + 16 * PAIR_DMAS))
                pe.wait_ge(o_ready, i * NC6 + 1)
                for h in range(2):
                    for k in range(3):
                        last = mm(PS[:, h, 0:TOK], wq[:, k, h, :], QHT[:, k, :], start=(k == 0), stop=(k == 2))
                    last.then_inc(pj_ps, 1)
                for k in range(3):
                    last = mm(PS[:, 2, 0:TOK], wp[:, k, :], QHT[:, k, :], start=(k == 0), stop=(k == 2))
                last.then_inc(pj_ps, 1)
                for h in range(2):
                    for k in range(2):
                        last = mm(PS[:, 3 + h, :], wk[:, k, h, :], CKT[:, k, :], start=(k == 0), stop=(k == 1))
                    last.then_inc(pj_ps, 1)
                for kg in range(4):
                    for k in range(2):
                        last = mm(PS[:, 5 + kg // 2, (kg % 2) * 256:(kg % 2 + 1) * 256], CKT[:, k, kg * P:(kg + 1) * P],
                                  wv[:, k, :], start=(k == 0), stop=(k == 1))
                    if kg % 2:
                        last.then_inc(pj_ps, 1)
                pe.wait_ge(pj_a, i * 3 + 3)
                mm(PS[:, 7, 0:DEC], odc("rot"), QP[:, P:3 * P], start=True, stop=True).then_inc(qrot_ps, 1)
                pe.wait_ge(pj_d, i * 4 + 4)
                pe.wait_ge(qp_ready, i + 1)
                for cc in range(NC6 + 2):
                    if cc < NC6:
                        h, qt = COMBOS[cc]
                        lo, hi = (P * v for v in keys(qt))
                        if cc >= 2:
                            pe.wait_ge(e_done, i * NC6 + cc - 1)
                        first = mm(PS[:, cc % 2, 0:hi - lo], QN[:, h, qt * P:(qt + 1) * P], KT[:, h, lo:hi],
                                   start=True, stop=False)
                        if cc == 0:
                            first.then_inc(used[3], 1)
                        mm(PS[:, cc % 2, 0:hi - lo], QP[h * ROPE:(h + 1) * ROPE, qt * P:(qt + 1) * P],
                           KPT[h * ROPE:(h + 1) * ROPE, lo:hi], start=False, stop=True).then_inc(s_ps, 1)
                    if 1 <= cc <= NC6:
                        b = cc - 1
                        lo, hi = keys(COMBOS[b][1])
                        pe.wait_ge(p_ready, i * NC6 + b + 1)
                        for j in range(hi - lo):
                            last = tr(PS[:, 2 + b % 2, j * P:(j + 1) * P], PB[:, b % 2, j * P:(j + 1) * P], ident)
                        last.then_inc(pt_ps, 1)
                    if cc >= 2:
                        b = cc - 2
                        h, qt = COMBOS[b]
                        lo, hi = keys(qt)
                        pe.wait_ge(pt_ready, i * NC6 + b + 1)
                        if b >= 2:
                            pe.wait_ge(o_ready, i * NC6 + b)
                        for j in range(hi - lo):
                            last = mm(PS[:, 4 + b % 2, 0:P], VV[:, lo + j, h * P:(h + 1) * P], PTB[:, b % 2, j * P:(j + 1) * P],
                                      start=(j == 0), stop=(j == hi - lo - 1))
                        last.then_inc(o_ps, 1)

            def attn_ready(k):
                if k == 0:
                    pe.wait_ge(o_ready, NC6 * NH // 2 + 1)
                    pe.wait_ge(gt, 1)

            project_out([("odout", 0), ("odout", 1)], 5, lambda k: HT[:, k, :] if k < 8 else GT[:, k - 8, :], attn_ready)
            x_turned(3, ("odout", 1))
            h_ready(3)

            pe.wait_ge(rout_in, 16)
            rw = ROUT.rearrange("p (k e) -> p k e", k=KD)
            for g in range(NG):
                for k in range(KD):
                    last = mm(PS[:, 0, g * NE:(g + 1) * NE], HT[:, k, g * P:(g + 1) * P], rw[:, k, :],
                              start=(k == 0), stop=(k == KD - 1))
            last.then_inc(lg_ps, 1)
            for q in range(2 * NG):
                g, half = divmod(q, 2)
                for b in range(4):
                    last = tr(PS[:, 1 + q, b * P:(b + 1) * P], HT[:, half * 4 + b, g * P:(g + 1) * P], ident)
                last.then_inc(hkt_ps, 1)
            pe.wait_ge(m_ready, 1)
            mask = MS[:, 8 + 4 + 8 * 24:8 + 4 + 9 * 24].rearrange("p (g e) -> p g e", g=NG)
            for g in range(NG + 1):
                for b in range(min(g + 1, NG)):
                    m = cst("before") if b == g else cst("ones")
                    last = mm(PS[:, 7, g * NE:(g + 1) * NE], m, mask[:, b, :], start=(b == 0), stop=(b == min(g, NG - 1)))
            last.then_inc(pos_ps, 1)
            pe.wait_ge(hk, 2 * NG)
            pe.wait_ge(pos_ready, 1)
            more = more_items(pe)

            def dispatch(i):
                pe.wait_ge(mp_ready, i + 1)
                if not (isinstance(i, int) and i == 0):
                    pe.wait_ge(xe_done, i)
                for k in range(KD):
                    for g in range(NG):
                        last = mm(PS[:, 4 + k // 4, (k % 4) * P:(k % 4 + 1) * P], HK[:, g, k * P:(k + 1) * P], PM[:, g, :],
                                  start=(g == 0), stop=(g == NG - 1))
                last.then_inc(disp_ps, 1)

            def gate_up(i, u):
                if not (isinstance(i, int) and i == 0 and u == 0):
                    pe.wait_ge(eh, i * UNITS_E + u)
                for k in range(KD):
                    if isinstance(i, int) and i == 0 and u == 0:
                        piece = E_FIRST[k // 2]
                    else:
                        piece = e_piece(i * UNITS_E + u - 1, k // 2)
                    if k % 2 == 0:
                        pe.wait_ge(lo_done, piece[0] + 1)
                    _, last = product(PS[:, 0, :], halves(XES, slice(k * P, (k + 1) * P)),
                                      gate_up_w(piece, k, slice(0, 2 * UCOL)), k == 0, k == KD - 1)
                    if k % 2 and k < KD - 1:
                        last.then_inc(w_used, 1)
                last.then_inc(gu_ps, 1)

            def down(i, u, after=True):
                pe.wait_ge(eht_lo, i * UNITS_E + u + 1)
                for b in range(2):
                    piece = e_piece(i * UNITS_E + u, 4 + b)
                    pe.wait_ge(lo_done, piece[0] + 1)
                    for h in range(2):
                        first, last = product(PS[:, 2 + h, :], halves(EHS, slice(b * P, (b + 1) * P)), down_w(piece, h),
                                              u == 0 and b == 0, u == UNITS_E - 1 and b == 1)
                        if after and (b, h) == (0, 0):
                            first.then_inc(w_used, 1)
                    if b == 0 or u < UNITS_E - 1:
                        last.then_inc(w_used, 1)
                if u == UNITS_E - 1:
                    last.then_inc(yd, 1)

            def turn_selection(i):
                pe.wait_ge(pg_ready, i)
                for g in range(NG):
                    last = tr(PS[:, 6, g * P:(g + 1) * P], PG[:, g, :], ident)
                    if g == 0:
                        last.then_inc(w_used, 1)
                last.then_inc(ptt_ps, 1)

            def combine(i, j, chunks):
                if chunks[0] == 0:
                    pe.wait_ge(ysb, i)
                    pe.wait_ge(pt_sb, i)
                for q in chunks:
                    g, half = divmod(q, 2)
                    if q >= 2:
                        pe.wait_ge(cb_done, j * 2 * NG + q)
                    mm(PS[:, 6 + q % 2, :], PT[:, g, :], YSB[:, half * 512:(half + 1) * 512], start=True, stop=True)\
                        .then_inc(cb_ps, 1)

            def item(i, first, j=0):
                for u in range(UNITS_E):
                    if u == 0:
                        pe.wait_ge(xe_done, i + 1)
                    gate_up(i, u)
                    if u == 0 and not first:
                        down(j, UNITS_E - 1)
                        pe.wait_ge(cb_done, j * 2 * NG + 1)
                        turn_selection(i)
                    if u in (1, 2, 3) and not first:
                        combine(i, j, (2 * u - 2, 2 * u - 1))
                    if u > 0:
                        down(i, u - 1)
                    if u == 2:
                        dispatch(i + 1)
                    pe.wait_ge(eh, i * UNITS_E + u + 1)
                    for b in range(2):
                        last = tr(PS[:, 1, b * P:(b + 1) * P], EH[:, b * P:(b + 1) * P], ident)
                        if first and (u, b) == (0, 0):
                            last.then_inc(w_used, 1)
                    last.then_inc(t_ps, 1)

            dispatch(0)
            item(0, True)
            with pe.Fori(0, more) as j:
                item(j + 1, False, j)
            down(more, UNITS_E - 1, after=False)
            pe.wait_ge(cb_done, more * 2 * NG + 1)
            turn_selection(more + 1)
            combine(more + 1, more, range(2 * NG))


_INS = ["x_prompt", "x_sample", "cache_ckv", "cache_kpe", "c", "c_ctx", "ada_w", "ada_b", "ln_g", "ln_b", "ev_w_in",
        "ev_conv_w", "ev_pool_w", "ev_pool_scale", "ev_w_out", "ffn_w_gate", "ffn_w_up", "ffn_w_down", "od_w_in",
        "od_q_norm", "od_kv_norm", "od_w_q_b", "od_w_kv_b", "od_fnet_w", "od_w_out", "moe_router", "moe_w_gate",
        "moe_w_up", "moe_w_down"]
_OUTS = [(1, SEQ, D), (1, DEC, D), (1, 1, SEQ, KVR), (1, 1, SEQ, ROPE)]


def kernel(**inputs):
    import concourse.bacc as _bacc
    from concourse.bass_utils import run_bass_kernel_spmd as _run

    nc = _bacc.Bacc("TRN2", target_bir_lowering=False, num_devices=1)
    arrays, args = {}, []
    given = {name: np.ascontiguousarray(inputs[name]) for name in _INS}
    given |= {"base_rows": BASE_ROWS, "odd_rows": ODD_ROWS, "dft_rows": DFT_ROWS, "pool_inv": pool_counts()}
    for name, a in given.items():
        arrays[f"in_{name}"] = a
        args.append(nc.dram_tensor(f"in_{name}", a.shape, mybir.dt.from_np(a.dtype), kind="ExternalInput").ap())
    for i, shape in enumerate(_OUTS):
        args.append(nc.dram_tensor(f"out_{i}", shape, F32, kind="ExternalOutput").ap())
    build(nc, *args)
    r = _run(nc, [arrays], core_ids=[0])
    return tuple(r.results[0][f"out_{i}"] for i in range(len(_OUTS)))
```

```python
from contextlib import ExitStack

import numpy as np

import concourse.bass as bass
from concourse import mybir

F32 = mybir.dt.float32
F32R = mybir.dt.float32r
I32 = mybir.dt.int32
ALU = mybir.AluOpType
ACT = mybir.ActivationFunctionType
AX = mybir.AxisListType

P = 128
D = 1024
KD = D // P
SEQ, DEC, PAST = 128, 256, 128
TOK = SEQ + DEC
NG = TOK // P
DEPTH = 2
CONV = 512
NPOOL = 4
WINDOWS = (2, 4, 8, 16)
FF = 2816
NF = FF // P
NH = 8
NOPE, ROPE, VD = 128, 64, 128
QR, KVR = 384, 256
FG, FGD = 4, 64
FD = FG * FGD
ODD_IN = QR + KVR + ROPE + FD
NE = 8
FFE = 1792
GRID_W = 64
ALPHA = float((2 * DEPTH) ** 0.25)
LN_EPS, RMS_EPS = 1e-5, 1e-6
SCALE = float((NOPE + ROPE) ** -0.5)

SLOT = 6144
PANEL = SLOT // KD
NPANEL = 6 * D // PANEL
UCOL = 256
UNITS_FF = FF // UCOL
UNITS_E = FFE // UCOL
CODES = 3 * NE
SCRATCH = 13600
TABLE = 16


def columns(parts):
    at, out = 0, {}
    for name, a in parts:
        out[name] = (at, a.shape[1])
        at += a.shape[1]
    return out, np.ascontiguousarray(np.concatenate([a for _, a in parts], 1).astype(np.float32))


def base_constants():
    n = np.arange(P)
    row = lambda v: np.tile(np.asarray(v, np.float32)[None, :], (P, 1))
    cand = [(e, r) for e in range(NE) for r in (1, 2)]
    return columns([
        ("ident", np.eye(P)),
        ("iota", row(n)),
        ("before", (n[:, None] < n[None, :]).astype(np.float32)),
        ("ones", np.ones((P, P))),
        ("expert", row(np.tile(np.arange(NE), NG))),
        ("item", row(np.arange(TABLE))),
        ("cand_code", row([e + NE * r for e, r in cand])),
        ("cand_expert", row([e for e, _ in cand])),
        ("base", row([j if j < NE else 0 for j in range(TABLE)])),
        ("eps", row([LN_EPS])),
    ])


def odd_constants():
    t = np.arange(DEC)
    half = ROPE // 2
    inv = 10000.0 ** (-np.arange(0, half, 2) / half)
    ar, ac = (t // GRID_W)[:, None] * inv, (t % GRID_W)[:, None] * inv
    ang = np.concatenate([ar, ar, ac, ac], -1)
    rot = np.zeros((ROPE, ROPE))
    q = ROPE // 4
    for h in range(2):
        for j in range(q):
            rot[h * 2 * q + q + j, h * 2 * q + j] = -1
            rot[h * 2 * q + j, h * 2 * q + q + j] = 1
    two = lambda m: np.kron(np.eye(2), m)
    dft = lambda n: 2 * np.pi * (np.outer(np.arange(n), np.arange(n)) % n) / n
    pos = lambda n: np.concatenate([np.cos(dft(n)), np.sin(dft(n))], 1) / np.sqrt(n * FGD)
    long = pos(DEC).reshape(DEC // P, P, 2 * DEC).transpose(1, 0, 2).reshape(P, -1)
    return columns([
        ("cos", np.tile(np.cos(ang).T, (2, 1))),
        ("sin", np.tile(np.sin(ang).T, (2, 1))),
        ("rot", two(rot)),
        ("chan_cos", two(np.cos(dft(FGD)))),
        ("chan_nsin", two(-np.sin(dft(FGD)))),
    ]), columns([("prompt", pos(SEQ)), ("latent", long)])


def pool_counts():
    out = np.zeros((NPOOL, TOK), np.float32)
    for w, win in enumerate(WINDOWS):
        at = 0
        for n in (SEQ, DEC):
            t = np.arange(n)
            out[w, at:at + n] = 1.0 / (np.minimum(t + win // 2, n) - np.maximum(t - win // 2, 0))
            at += n
    return out


BASE, BASE_ROWS = base_constants()
(ODD, ODD_ROWS), (DFT, DFT_ROWS) = odd_constants()


class Pieces:

    def __init__(self):
        self.n, self.landed = 0, [0] * RING

    def take(self, dmas):
        n, at = self.n, self.n % RING
        self.n += 1
        self.landed[at] += 16 * dmas
        return n, at, self.landed[at]

    def skip(self, n, landed):
        self.n += n
        self.landed = [a + b for a, b in zip(self.landed, landed)]


class Ring:

    def __init__(self):
        self.landed, self.used, self.units = [0] * 4, [0] * 4, {}

    def unit(self, name, slot, dmas):
        before = self.used[slot]
        self.landed[slot] += 16 * dmas
        self.used[slot] += 1
        self.units[name] = (slot, self.landed[slot], before)


class Chain:

    def __init__(self, eng, sem):
        self.eng, self.sem, self.n = eng, sem, 0

    def __call__(self, ins):
        ins.then_inc(self.sem, 1)
        self.n = self.n + 1
        self.eng.wait_ge(self.sem, self.n)


def plan():
    r = Ring()
    for p in range(NPANEL):
        r.unit(("ada", p), p % 4, 1)
    for t in range(4):
        r.unit(("evin", t), t, 1)
    r.unit(("evout", 0), 0, 1)
    r.unit(("evout", 1), 1, 1)
    for n, at in ((8, 2), (9, 3), (10, 1), (11, 2)):
        r.unit(("ada", n), at, 1)
    before_ff = list(r.used)
    for name, at in ((("ada", 12), 1), (("odin", 0), 2), (("odin", 1), 3), (("ada", 13), 0)):
        r.unit(name, at, 1)
    pair = (list(r.landed), list(r.used))
    for i in range(NH // 2):
        r.unit(("pair", i), 3, PAIR_DMAS)
    for name, at in ((("odout", 0), 1), (("odout", 1), 2), (("ada", 15), 3), (("ada", 14), 1)):
        r.unit(name, at, 1)
    return r, before_ff, pair


NROWS = 35 + 2 * 4 * KD
EV_ORDER = (3, 0, 1, 2)
SOON = 4
RING = 6
PIECE = 1024
PAIR_DMAS = 3 + 3 + 2 + 2


def build(nc, x_prompt, x_sample, cache_ckv, cache_kpe, c, c_ctx, ada_w, ada_b, ln_g, ln_b, ev_w_in, ev_conv_w,
          ev_pool_w, ev_pool_scale, ev_w_out, ffn_w_gate, ffn_w_up, ffn_w_down, od_w_in, od_q_norm, od_kv_norm,
          od_w_q_b, od_w_kv_b, od_fnet_w, od_w_out, moe_router, moe_w_gate, moe_w_up, moe_w_down,
          base_rows, odd_rows, dft_rows, pool_inv, y_prompt, y_sample, new_ckv, new_kpe):
    ctx = ExitStack()
    with ctx:
        def sb(name, shape, dt=F32):
            return ctx.enter_context(nc.sbuf_tensor("sb_" + name, shape, dt))

        def sem(name):
            return ctx.enter_context(nc.semaphore(name))

        gate_rows = nc.dram_tensor("gate_rows", (DEPTH, 4, D), F32, kind="Internal").ap()

        WR = sb("ring", [P, 4, SLOT])
        ring_at = nc.sbuf_base - 4 * 4 * SLOT
        RAW = WR[:, 0, :].rearrange("p (r n) -> p r n", r=RING)
        WS = nc.alloc_sbuf_tensor_at("sb_split_weights", [P, RING, 2, PIECE], F32R, offset=ring_at + 4 * SLOT)
        AS = nc.alloc_sbuf_tensor_at("sb_split_acts", [P, SLOT], F32R, offset=ring_at + 12 * SLOT)
        X = sb("x", [P, NG, D])
        HT = sb("ht", [P, KD, TOK])
        GB = sb("gate_rows", [P, 2, D])
        LG = sb("ln_gain", [P, D])
        LB = sb("ln_bias", [P, D])
        T = sb("temp", [P, D])
        CST = sb("constants", [P, BASE_ROWS.shape[1]])
        MT = sb("mod_cols", [P, DEPTH, 6 * KD, 2])
        ROWS = sb("rows", [NROWS, P])
        BROWS = sb("mod_bias_rows", [DEPTH * 6 * KD, P])
        COLS = sb("cols", [P, NROWS])
        BCOLS = sb("mod_bias", [P, DEPTH * 6 * KD])
        SC = sb("silu_cond", [P, KD, 2])
        STG = sb("mod_stage", [2, 2, PANEL])
        GS = sb("gate_stage", [KD, 4, P])
        LT = T[0:NE, 0:TOK]
        ROUT = sb("router", [P, KD, NE])
        SM = sb("small", [P, 160])
        TAB = sb("item_table", [1, 1 + 2 * TABLE], I32)
        SCR = sb("scratch", [P, SCRATCH])
        scratch_at = nc.sbuf_base - 4 * SCRATCH
        PS = ctx.enter_context(nc.psum_tensor("ps", [P, 8, 512], F32))

        def cst(name, rows=P):
            at, n = BASE[name]
            return CST[0:rows, at:at + n]

        ident = cst("ident")

        def carve(*parts):
            at, out = 0, []
            for n in parts:
                out.append(SCR[:, at:at + n])
                at += n
            assert at <= SCRATCH, at
            return out

        ZW, UW = SEQ + DEC + 4, SEQ + DEC + 32
        UX, UB, Z, UP, ICNT, SA, SBB, CV, MIX, PW = carve(
            4 * TOK, 4 * TOK, 4 * ZW, 4 * UW, 4 * TOK, UW, UW, ZW, 8 * TOK, 4 * P)
        r4 = lambda a, n: a.rearrange("p (a n) -> p a n", a=n)
        UX, UB, Z, UP, ICNT, MIX, PW = (r4(a, n) for a, n in
                                            ((UX, 4), (UB, 4), (Z, 4), (UP, 4), (ICNT, 4), (MIX, 8), (PW, 4)))
        PP = MIX[:, 4:8, :]
        SEGZ = ((0, 1, SEQ), (SEQ, SEQ + 3, DEC))
        SEGU = ((0, 8, SEQ), (SEQ, SEQ + 24, DEC))
        SIL, HF = carve(TOK, TOK)
        HFS = nc.alloc_sbuf_tensor_at("sb_split_hidden", [P, 2, 2, TOK], F32R, offset=scratch_at + 4 * 1024)
        HX = AS[:, :].rearrange("p (s k n) -> p s k n", s=2, k=KD)
        (U, KDUP, CK, QHT, CKT, KPT, OC, FNW, GT, AT) = carve(
            NG * ODD_IN, 4 * P, KVR, 3 * TOK, 2 * 512, 512, ODD_ROWS.shape[1], 2 * FD, 2 * TOK, 4992)
        DC = AT[:, 2304:2304 + DFT_ROWS.shape[1]]
        KVN = AT[:, 3600:3600 + KVR]
        U, KDUP, QHT, CKT, FNW, GT = (r4(a, n) for a, n in ((U, NG), (KDUP, 4), (QHT, 3), (CKT, 2), (FNW, 2), (GT, 2)))
        FA = r4(AT[:, 0:2 * 768], 2)
        FT = r4(AT[:, 1536:1536 + 2 * TOK], 2)
        cut = np.cumsum([0, 2 * TOK, TOK, 256, 1024, 1024, 2 * TOK, 2 * TOK])
        QN, QP, RT, KT, VV, PB, PTB = (AT[:, int(a):int(b)] for a, b in zip(cut[:-1], cut[1:]))
        QN, KT, VV, PB, PTB = (r4(a, n) for a, n in ((QN, 2), (KT, 2), (VV, 4), (PB, 2), (PTB, 2)))
        odc = lambda name: OC[:, ODD[name][0]:ODD[name][0] + ODD[name][1]]
        dft = lambda name: DC[:, DFT[name][0]:DFT[name][0] + DFT[name][1]]
        (HK, _, PM, XT, YACC, PG, ESIL, EH, POSA, GA, MS) = carve(
            NG * D, NG * D, TOK, D, NG * D, TOK, UCOL, UCOL, CODES * NG, CODES * NG, 900)
        YACC, PG = r4(YACC, NG), r4(PG, NG)
        HKS = nc.alloc_sbuf_tensor_at("sb_split_tokens", [P, 2, NG, D], F32R, offset=scratch_at)
        PM = nc.alloc_sbuf_tensor_at("sb_selection", [P, NG, P], F32R, offset=scratch_at + 4 * 2 * NG * D)
        XES = AS[:, 0:2 * D].rearrange("p (s n) -> p s n", s=2)
        EHS = AS[:, 2 * D:2 * D + 2 * UCOL].rearrange("p (s n) -> p s n", s=2)
        YS = AS[:, 2 * D + 2 * UCOL:4 * D + 2 * UCOL].rearrange("p (s n) -> p s n", s=2)
        PT = AS[:, 4 * D + 2 * UCOL:4 * D + 2 * UCOL + TOK]

        landed = [sem(f"landed{s}") for s in range(4)]
        used = [sem(f"used{s}") for s in range(4)]
        names = """cst_in rows_in x_in half_in stored lnp_in pw_in icnt_in oddc_in cache_in kvn_in
            fnw_in rout_in out_done kv_out rows_t cols_ready sc_ready mm_a mm_b st_a st_b cols_t cols_done mt_ready
            xt_t ht_a ht_d u_ps u_act u_dve z_pad mix_conv pp_ready pm_ps mix_pool y_ps var_ready sd_ready ln_x
            g_ps up_ps sil ff_h odi_ps odu ssq odn kd_ready odt_ps odt_a rot_ps kpt_ready f1_ps fa f2_ps ft
            f3_ps gt pj_ps pj_a pj_d qrot_ps qp_ready s_ps nmax e_done p_ready pt_ps pt_ready o_ps o_ready
            lgt_ps lgt_sb lg_ps hkt_ps hk hk_lo dx_ps dx_sb d_ready ex_ready m_ready pos_ps tab_ready pos_ready
            gu_ps esil eh t_ps yd ysb y_lo x_last pg_ready ptt_ps pt_sb cb_ps cb_done mp_ready disp_ps xe_done
            gates_t gates_out x_full hi_done lo_done w_used hx_hi hx_lo fh_hi fh_lo xe_hi eht_hi eht_lo
            dve_chain act_chain pool_chain""".split()
        s = {n: sem(n) for n in names}
        (cst_in, rows_in, x_in, half_in, stored, lnp_in, pw_in, icnt_in, oddc_in, cache_in, kvn_in,
         fnw_in, rout_in, out_done, kv_out, rows_t, cols_ready, sc_ready, mm_a, mm_b, st_a, st_b, cols_t, cols_done, mt_ready,
         xt_t, ht_a, ht_d, u_ps, u_act, u_dve, z_pad, mix_conv, pp_ready, pm_ps, mix_pool, y_ps, var_ready, sd_ready,
         ln_x, g_ps, up_ps, sil, ff_h, odi_ps, odu, ssq, odn, kd_ready, odt_ps, odt_a, rot_ps, kpt_ready,
         f1_ps, fa, f2_ps, ft, f3_ps, gt, pj_ps, pj_a, pj_d, qrot_ps, qp_ready, s_ps, nmax, e_done, p_ready, pt_ps,
         pt_ready, o_ps, o_ready, lgt_ps, lgt_sb, lg_ps, hkt_ps, hk, hk_lo, dx_ps, dx_sb, d_ready, ex_ready, m_ready, pos_ps, tab_ready, pos_ready,
         gu_ps, esil, eh, t_ps, yd, ysb, y_lo, x_last, pg_ready, ptt_ps, pt_sb, cb_ps, cb_done, mp_ready, disp_ps,
         xe_done, gates_t, gates_out, x_full, hi_done, lo_done, w_used, hx_hi, hx_lo, fh_hi, fh_lo, xe_hi, eht_hi, eht_lo,
         dve_chain, act_chain, pool_chain) = (s[n] for n in names)

        raw_in = [sem(f"raw_in{r}") for r in range(RING)]
        ring, ring_before_ff, pair_base = plan()
        FF_ITERS = (UNITS_FF - 1) // 2
        pieces = Pieces()
        FF_FIRST = [pieces.take(2) for _ in range(4)] + [pieces.take(1)]
        ff_n, ff_landed = pieces.n, list(pieces.landed)
        FF_UNIT_LANDED = [32 if (r - ff_n) % RING < 4 else 16 for r in range(RING)]
        pieces.skip(RING * (UNITS_FF - 1), [(UNITS_FF - 1) * v for v in FF_UNIT_LANDED])
        FF_LAST = pieces.take(1)
        E_FIRST = [pieces.take(2) for _ in range(4)]
        e_n, e_landed = pieces.n, list(pieces.landed)
        E_UNIT_LANDED = [32 if (r - e_n) % RING < 4 else 16 for r in range(RING)]

        def stream_piece(base_n, base_landed, per_unit, unit, c):
            at = (base_n + c) % RING
            return unit * RING + (base_n + c), at, unit * per_unit[at] + (base_landed[at] + per_unit[at])

        ff_piece = lambda unit, c: stream_piece(ff_n, ff_landed, FF_UNIT_LANDED, unit, c)
        e_piece = lambda unit, c: stream_piece(e_n, e_landed, E_UNIT_LANDED, unit, c)

        ff_used = lambda unit, c: unit * RING + (min(c, 3) + 1 if c < 5 else RING - 1)
        FF_LAST_USED = RING * (UNITS_FF - 1) + 1
        e_used = lambda unit, c: unit * RING + (e_n - RING + c)
        GATES_AT = {7: (0, 1), 11: (2,), 15: (3,)}
        FOLDS_AT = {7: (1,), 11: (2,), 14: (3,)}
        MIXER_PANELS = -(-2 * D // PANEL)
        COMBOS = [(h, qt) for h in range(2) for qt in range(NG)]
        NC6 = len(COMBOS)

        def keys(qt):
            return (0, 1) if qt == 0 else (1, 4)

        def slot(name):
            return WR[:, ring.units[name][0], :]

        def wait_unit(eng, name):
            sl, land, _ = ring.units[name]
            eng.wait_ge(landed[sl], land)

        def more_items(eng):
            eng.wait_ge(tab_ready, 1)
            return eng.value_load(TAB[0:1, 0:1], min_val=NE - 1, max_val=TABLE - 4)

        latent_cond = c[0].rearrange("(t p) -> t p", p=P)
        block = ctx.enter_context(nc.Block())

        @block.sync
        def _(sp):
            def free(name):
                sl, _, before = ring.units[name]
                if before:
                    sp.wait_ge(used[sl], before)

            def panel(dst, src, n, k, name):
                sp.dma_start(dst[:, 0:k * n].rearrange("p (k n) -> p k n", k=k),
                             src.rearrange("(k p) n -> p k n", p=P)).then_inc(landed[ring.units[name][0]], 16)

            def load(name, src):
                free(name)
                rows, n = src.shape
                panel(slot(name), src, n, rows // P, name)

            def raw_free(n, more=0):
                if isinstance(n, int) and n < RING:
                    return
                sp.wait_ge(lo_done, n - (RING - 1) + more)

            def gate_up_piece(piece, gate, up, more=0):
                n, at, _ = piece
                raw_free(n, more)
                dst = RAW[:, at, :].rearrange("p (k n) -> p k n", k=2)
                sp.dma_start(dst[:, :, 0:UCOL], gate).then_inc(raw_in[at], 16)
                sp.dma_start(dst[:, :, UCOL:2 * UCOL], up).then_inc(raw_in[at], 16)

            def down_piece(piece, down, free=False):
                n, at, _ = piece
                if not free:
                    raw_free(n)
                sp.dma_start(RAW[:, at, :], down).then_inc(raw_in[at], 16)

            fg = ffn_w_gate[0].rearrange("(k p) n -> p k n", p=P)
            fu = ffn_w_up[0].rearrange("(k p) n -> p k n", p=P)
            fd = ffn_w_down[0].rearrange("(u b p) n -> p u b n", b=2, p=P)

            def ff_gate_up(piece, u, c):
                cols = bass.ds(u * UCOL, UCOL)
                gate_up_piece(piece, fg[:, 2 * c:2 * c + 2, cols], fu[:, 2 * c:2 * c + 2, cols], more=int(c == 0))

            def ff_down(piece, u, b):
                down_piece(piece, fd[:, bass.ds(u, 1), b, :])

            def moe_gate_up(piece, e, u, c, more=0):
                one, rows, cols = bass.ds(e, 1), slice(2 * c * P, (2 * c + 2) * P), slice(u * UCOL, (u + 1) * UCOL)
                gate_up_piece(piece, moe_w_gate[0, one, rows, cols].rearrange("e (k p) n -> p (e k) n", p=P),
                              moe_w_up[0, one, rows, cols].rearrange("e (k p) n -> p (e k) n", p=P), more)

            def moe_down(piece, e, f):
                down_piece(piece, moe_w_down[0, bass.ds(e, 1), f * P:(f + 1) * P, :].rearrange("e p n -> p (e n)"),
                           free=f == 0)

            def moe_item(i, e, e_next):
                for u in range(UNITS_E):
                    for c in range(4):
                        last = u == UNITS_E - 1
                        moe_gate_up(e_piece(i * UNITS_E + u, c), e_next if last else e, 0 if last else u + 1, c,
                                    more=int((u, c) == (0, 3)))
                    for b in range(2):
                        moe_down(e_piece(i * UNITS_E + u, 4 + b), e, 2 * u + b)

            def ada(n):
                l, p = divmod(n, NPANEL)
                if n:
                    load(("ada", n), ada_w[l, :, p * PANEL:(p + 1) * PANEL])
                else:
                    dst = slot(("ada", 0)).rearrange("p (k n) -> p k n", k=KD)
                    src = ada_w[0].rearrange("(k p) n -> p k n", p=P)
                    half = PANEL // 2
                    sp.dma_start(dst[:, :, 0:half], src[:, :, 0:half]).then_inc(half_in, 16)
                    sp.dma_start(dst[:, :, half:PANEL], src[:, :, half:PANEL]).then_inc(landed[0], 16)

            sp.dma_start(CST[:, :], base_rows).then_inc(cst_in, 16)
            sp.wait_ge(rows_in, 128)
            for n in range(NPANEL):
                ada(n)
                if n == 1:
                    sp.dma_start(X[:, 0, :], x_prompt[0]).then_inc(x_in, 16)
                    sp.dma_start(X[:, 1:NG, :], x_sample[0].rearrange("(g p) d -> p g d", p=P)).then_inc(x_in, 16)
            for t in range(4):
                load(("evin", t), ev_w_in[0, :, EV_ORDER[t] * 512:(EV_ORDER[t] + 1) * 512])
            for t in range(2):
                load(("evout", t), ev_w_out[0, (1 - t) * 512:(2 - t) * 512, :])
            for n in (8, 9):
                ada(n)
            sp.wait_ge(used[0], ring_before_ff[0])
            for c in range(4):
                ff_gate_up(FF_FIRST[c], 0, c)
            for n in (10, 11):
                ada(n)
            ff_down(FF_FIRST[4], 0, 0)
            with sp.Fori(0, FF_ITERS) as i:
                for b in range(2):
                    for c in range(4):
                        ff_gate_up(ff_piece(i * 2 + b, c), i * 2 + (b + 1), c)
                    ff_down(ff_piece(i * 2 + b, 4), i * 2 + b, 1)
                    ff_down(ff_piece(i * 2 + b, 5), i * 2 + (b + 1), 0)
            ff_down(FF_LAST, UNITS_FF - 1, 1)
            sp.wait_ge(y_ps, 2 * NG)
            ada(12)
            for t in range(2):
                load(("odin", t), od_w_in[0, :, t * 480:(t + 1) * 480])
            ada(13)
            qb = od_w_q_b[0].rearrange("(k p) (h c) -> p k h c", p=P, h=NH)
            kvb = od_w_kv_b[0].rearrange("(k p) (h c) -> p k h c", p=P, h=NH)
            with sp.Fori(0, NH // 2) as i:
                sp.wait_ge(used[3], i + pair_base[1][3])
                two = bass.ds(i * 2, 2)
                for k in range(3):
                    sp.dma_start(WR[:, 3, 256 * k:256 * (k + 1)].rearrange("p (h c) -> p h c", h=2),
                                 qb[:, k, two, 0:NOPE]).then_inc(landed[3], 16)
                    sp.dma_start(WR[:, 3, 768 + P * k:768 + P * (k + 1)].rearrange("p (h c) -> p h c", h=2),
                                 qb[:, k, two, NOPE:NOPE + ROPE]).then_inc(landed[3], 16)
                for k in range(2):
                    sp.dma_start(WR[:, 3, 1152 + 256 * k:1408 + 256 * k].rearrange("p (h c) -> p h c", h=2),
                                 kvb[:, k, two, 0:NOPE]).then_inc(landed[3], 16)
                    sp.dma_start(WR[:, 3, 1664 + 256 * k:1920 + 256 * k].rearrange("p (h c) -> p h c", h=2),
                                 kvb[:, k, two, NOPE:NOPE + VD]).then_inc(landed[3], 16)
            for t in range(2):
                load(("odout", t), od_w_out[0, t * 640:(t + 1) * 640, :])
            sp.wait_ge(used[0], ring.used[0])
            for c in range(4):
                moe_gate_up(E_FIRST[c], 0, 0, c)
            ada(15)
            ada(14)
            moe_item(0, 0, 1)
            more = more_items(sp)
            with sp.Fori(0, more) as j:
                e = sp.value_load(TAB[0:1, bass.ds(j + 2 + TABLE, 1)], min_val=0, max_val=NE - 1)
                e_next = sp.value_load(TAB[0:1, bass.ds(j + 3 + TABLE, 1)], min_val=0, max_val=NE - 1)
                moe_item(j + 1, e, e_next)
            for g in range(NG):
                sp.wait_ge(x_full, 3 * NG + g + 1) if g < NG - 1 else sp.wait_ge(x_last, 1)
                out = y_prompt[0] if g == 0 else y_sample[0, (g - 1) * P:g * P, :]
                sp.dma_start(out, X[:, g, :]).then_inc(out_done, 16)
            sp.wait_ge(out_done, 16 * NG)
            sp.wait_ge(kv_out, 32)

        @block.gpsimd
        def _(pool):
            ch = Chain(pool, pool_chain)
            def store_gate(n):
                l, j = divmod(n, 2)
                pool.wait_ge(gates_out, n + 1)
                pool.dma_start(gate_rows[l, 2 * j:2 * j + 2, :].rearrange("a (k p) -> k a p", p=P),
                               GS[:, 2 * j:2 * j + 2, :]).then_inc(stored, 16)

            def ln_params(l, j):
                done = 2 * l + j
                if done:
                    pool.wait_ge(ln_x, NG * done)
                    pool.wait_ge(x_full, NG * done)
                pool.wait_ge(stored, 16 * max(done + 1, 2))
                pool.dma_start(LG[:, :], ln_g[l, j].partition_broadcast(P)).then_inc(lnp_in, 16)
                pool.dma_start(LB[:, :], ln_b[l, j].partition_broadcast(P)).then_inc(lnp_in, 16)
                pool.dma_start(GB[:, :, :], gate_rows[l, 2 * j:2 * j + 2, :].partition_broadcast(P)).then_inc(lnp_in, 16)

            def gain_bias(done):
                pool.wait_ge(lnp_in, 48 * (done + 1))
                for g in range(NG if done < 2 * DEPTH - 1 else NG - 1):
                    pool.wait_ge(ln_x, NG * done + g + 1)
                    if done < 2 * DEPTH - 1:
                        pool.wait_ge(xt_t, 2 * NG * (done + 1) + 2 * g + 2)
                    ch(pool.tensor_tensor(X[:, g, :], X[:, g, :], LG[:, :], ALU.mult))
                    pool.tensor_tensor(X[:, g, :], X[:, g, :], LB[:, :], ALU.add).then_inc(x_full, 1)

            pool.dma_start(PW, ev_pool_w[0].rearrange("g c d -> c g d")).then_inc(pw_in, 16)
            pool.dma_start(ICNT, pool_inv.partition_broadcast(P)).then_inc(icnt_in, 16)
            pool.dma_start(ROUT[:, :, :], moe_router[0].rearrange("(k p) e -> p k e", p=P)).then_inc(rout_in, 16)
            store_gate(0)
            store_gate(1)
            ln_params(0, 0)
            pool.wait_ge(icnt_in, 16)
            pool.wait_ge(z_pad, 2)
            for g, win in enumerate(WINDOWS):
                pool.wait_ge(u_act, g + 1)
                src, width, step, bufs = UP[:, g, :], UW, 1, (SA, SBB)
                while step < win:
                    width -= step
                    dst = bufs[0]
                    ch(pool.tensor_tensor(dst[:, 0:width], src[:, 0:width], src[:, step:step + width], ALU.add))
                    src, bufs, step = dst, (bufs[1], bufs[0]), step * 2
                for tok, at, n in SEGU:
                    lo = at - win // 2
                    ch(pool.tensor_tensor(PP[:, g, tok:tok + n], src[:, lo:lo + n], ICNT[:, g, tok:tok + n], ALU.mult))
                for tok, at, n in SEGU:
                    last = pool.tensor_tensor(PP[:, g, tok:tok + n], PP[:, g, tok:tok + n], UP[:, g, at:at + n], ALU.subtract)
                    if tok == 0:
                        ch(last)
                last.then_inc(pp_ready, 1)
            gain_bias(0)
            ln_params(0, 1)
            pool.wait_ge(g_ps, 1)
            pool.dma_start(OC, odd_rows).then_inc(oddc_in, 16)
            pool.dma_start(DC, dft_rows).then_inc(oddc_in, 16)
            pool.dma_start(KVN, od_kv_norm[0].partition_broadcast(P)).then_inc(kvn_in, 16)
            pool.dma_start(FNW, od_fnet_w[0].rearrange("(k p) n -> p k n", p=P)).then_inc(fnw_in, 16)
            pool.dma_start(CK, cache_ckv[0, 0]).then_inc(cache_in, 16)
            for b in range(2):
                pool.dma_start(KDUP[:, 1, b * ROPE:(b + 1) * ROPE], cache_kpe[0, 0]).then_inc(cache_in, 16)
            store_gate(2)
            gain_bias(1)
            ln_params(1, 0)
            for p in range(2 * NG):
                g, b = divmod(p, 2)
                if p == 0:
                    pool.wait_ge(odu, 2 * NG)
                last = pool.tensor_copy(KDUP[:, g if g == 0 else g + 1, b * ROPE:(b + 1) * ROPE],
                                        U[:, g, QR + KVR:QR + KVR + ROPE])
            last.then_inc(kd_ready, 1)
            pool.wait_ge(odn, 2)
            pool.dma_start(new_ckv[0, 0], U[:, 0, QR:QR + KVR]).then_inc(kv_out, 16)
            pool.dma_start(new_kpe[0, 0], U[:, 0, QR + KVR:QR + KVR + ROPE]).then_inc(kv_out, 16)
            gain_bias(2)
            store_gate(3)
            ln_params(1, 1)
            gain_bias(3)

        @block.scalar
        def _(act):
            act.dma_start(ROWS[19:27, :], c_ctx.rearrange("(t p) -> t p", p=P)).then_inc(rows_in, 16)
            act.dma_start(ROWS[27:35, :], latent_cond).then_inc(rows_in, 16)
            act.dma_start(ROWS[0:12, :], ev_conv_w[0].rearrange("k (t p) -> (k t) p", p=P)).then_inc(rows_in, 16)
            act.dma_start(ROWS[12:16, :], ev_pool_scale[0].rearrange("(t p) -> t p", p=P)).then_inc(rows_in, 16)
            act.dma_start(ROWS[16:19, :], od_q_norm[0].rearrange("(t p) -> t p", p=P)).then_inc(rows_in, 16)
            act.dma_start(ROWS[35:67, :], ln_g.rearrange("l j (t p) -> (l j t) p", p=P)).then_inc(rows_in, 16)
            act.dma_start(ROWS[67:99, :], ln_b.rearrange("l j (t p) -> (l j t) p", p=P)).then_inc(rows_in, 16)
            act.dma_start(BROWS[:, :], ada_b.rearrange("l (t p) -> (l t) p", p=P)).then_inc(rows_in, 16)
            act.wait_ge(cols_ready, 1)
            nc.scalar.activation(SC[:, :, :].rearrange("p k c -> p c k"),
                                 COLS[:, 19:35].rearrange("p (c k) -> p c k", c=2), ACT.Silu).then_inc(sc_ready, 1)

            def sqrt_of(n, at, count):
                act.wait_ge(var_ready, n)
                nc.scalar.activation(SM[:, at + count:at + 2 * count], SM[:, at:at + count], ACT.Sqrt).then_inc(sd_ready, 1)

            def sqrt_ln(n):
                for g in range(NG):
                    sqrt_of(n + g, 2 * g, 1)

            def modulate(st):
                l, j = divmod(st, 2)
                act.wait_ge(mt_ready, st) if st else act.wait_ge(cols_done, MIXER_PANELS)
                for q in (0, 1, 2, 3, 5):
                    g, half = divmod(q, 2)
                    cond = min(g, 1)
                    act.wait_ge(xt_t, 2 * NG * st + q + 1)
                    for b in range(4):
                        k = half * 4 + b
                        last = nc.scalar.activation(HT[:, k, g * P:(g + 1) * P], PS[:, q, b * P:(b + 1) * P], ACT.Identity,
                                                    scale=MT[:, l, (3 * j + 1) * KD + k, cond:cond + 1],
                                                    bias=MT[:, l, 3 * j * KD + k, cond:cond + 1])
                    last.then_inc(ht_a, 1)

            modulate(0)
            for t in range(12):
                act.wait_ge(u_ps, t + 1)
                if t >= 4:
                    dst = (UX, UB)[t // 4 - 1]
                    nc.scalar.copy(dst[:, t % 4, :], PS[:, t % 4, 0:TOK]).then_inc(u_act, 1)
                else:
                    act.wait_ge(z_pad, 2)
                    for tok, at, n in SEGU:
                        last = nc.scalar.copy(UP[:, t % 4, at:at + n], PS[:, t % 4, tok:tok + n])
                    last.then_inc(u_act, 1)
            for g in range(NPOOL):
                act.wait_ge(pm_ps, g + 1)
                nc.scalar.activation(MIX[:, 4 + g, :], PS[:, 6 + g % 2, 0:TOK], ACT.Identity,
                                     scale=COLS[:, 12 + g:13 + g]).then_inc(mix_pool, 1)
            sqrt_ln(1)
            modulate(1)

            def high(piece, used_up):
                n, at, land = piece
                act.wait_ge(raw_in[at], land)
                if used_up is not None:
                    act.wait_ge(w_used, used_up)
                nc.scalar.copy(WS[:, at, 0, :], RAW[:, at, :]).then_inc(hi_done, 1)

            def ff_hidden(f, b):
                act.wait_ge(g_ps, f + 1)
                nc.scalar.activation(SIL, PS[:, 6, 0:TOK], ACT.Silu).then_inc(sil, 1)
                act.wait_ge(ff_h, f + 1)
                nc.scalar.copy(HFS[:, b, 0, :], HF).then_inc(fh_hi, 1)

            act.wait_ge(ht_d, 2)
            act.wait_ge(ht_a, 10)
            for k in range(KD):
                if k == 0:
                    act.wait_ge(used[3], ring_before_ff[3])
                nc.scalar.copy(HX[:, 0, k, :], HT[:, k, :]).then_inc(hx_hi, 1)
            for at in (1, 2):
                act.wait_ge(used[at], ring_before_ff[at])
            for c in range(5):
                high(FF_FIRST[c], None)
            ff_hidden(0, 0)
            ff_hidden(1, 1)
            with act.Fori(0, FF_ITERS) as i:
                for b in range(2):
                    for c in range(RING):
                        high(ff_piece(i * 2 + b, c), ff_used(i * 2 + b, c))
                    ff_hidden(i * 4 + (2 + 2 * b), 0)
                    ff_hidden(i * 4 + (3 + 2 * b), 1)
            high(FF_LAST, FF_LAST_USED)
            sqrt_ln(4)
            modulate(2)
            for q in range(2 * NG):
                h, g = divmod(q, NG)
                act.wait_ge(odi_ps, q + 1)
                nc.scalar.copy(U[:, g, h * 480:(h + 1) * 480], PS[:, q, 0:480]).then_inc(odu, 1)
            act.wait_ge(odu, 2 * NG)
            for g in range(NG):
                for b, (lo, n) in enumerate(((0, QR), (QR, KVR))):
                    last = nc.scalar.activation(T[:, b * 512:b * 512 + n], U[:, g, lo:lo + n], ACT.Square,
                                                accum_out=SM[:, 40 + 3 * b + g:41 + 3 * b + g])
                    act_last = last
                    if (g, b) != (NG - 1, 1):
                        act_last.then_inc(act_chain, 1)
                        act.wait_ge(act_chain, 2 * g + b + 1)
            act_last.then_inc(ssq, 1)
            sqrt_of(7, 64, 18)
            for q in range(6):
                act.wait_ge(odt_ps, q + 1)
                if q < 3:
                    ins = nc.scalar.activation(QHT[:, q, :], PS[:, q, 0:TOK], ACT.Identity, scale=COLS[:, 16 + q:17 + q])
                elif q < 5:
                    ins = nc.scalar.copy(CKT[:, q - 3, :], PS[:, q, :])
                else:
                    ins = nc.scalar.copy(KPT, PS[:, q, :])
                ins.then_inc(odt_a, 1)
            act.wait_ge(o_ready, 1)
            with act.Fori(0, NH // 2) as i:
                for q in range(3):
                    act.wait_ge(pj_ps, i * 7 + q + 1)
                    nc.scalar.copy(QN[:, q, :] if q < 2 else QP, PS[:, q, 0:TOK]).then_inc(pj_a, 1)
                for cc in range(NC6 + 2):
                    if cc < NC6:
                        n = P * (keys(COMBOS[cc][1])[1] - keys(COMBOS[cc][1])[0])
                        act.wait_ge(nmax, i * NC6 + cc + 1)
                        if cc >= 2:
                            act.wait_ge(pt_ps, i * NC6 + cc - 1)
                        nc.scalar.activation(PB[:, cc % 2, 0:n], PS[:, cc % 2, 0:n], ACT.Exp, scale=SCALE,
                                             bias=SM[:, 104 + cc % 2:105 + cc % 2],
                                             accum_out=SM[:, 106 + cc % 2:107 + cc % 2]).then_inc(e_done, 1)
                    if cc >= 2:
                        b = cc - 2
                        n = P * (keys(COMBOS[b][1])[1] - keys(COMBOS[b][1])[0])
                        act.wait_ge(pt_ps, i * NC6 + b + 1)
                        nc.scalar.copy(PTB[:, b % 2, 0:n], PS[:, 2 + b % 2, 0:n]).then_inc(pt_ready, 1)
            sqrt_ln(8)
            modulate(3)
            act.wait_ge(lgt_ps, 1)
            nc.scalar.copy(LT, PS[0:NE, 0, 0:TOK]).then_inc(lgt_sb, 1)
            act.wait_ge(kv_out, 32)
            for q in range(2 * NG):
                g, half = divmod(q, 2)
                act.wait_ge(hkt_ps, q + 1)
                nc.scalar.copy(HKS[:, 0, g, half * 512:(half + 1) * 512], PS[:, 1 + q, :]).then_inc(hk, 1)
            act.wait_ge(d_ready, 1)
            nc.scalar.activation(MS[:, 3:6], MS[:, 0:3], ACT.Exp).then_inc(ex_ready, 1)

            def picked(i):
                act.wait_ge(dx_ps, i + 1)
                nc.scalar.copy(XT, PS[:, 4:6, :].rearrange("p a n -> p (a n)")).then_inc(dx_sb, 1)

            def dispatched(i):
                act.wait_ge(disp_ps, i + 1)
                nc.scalar.copy(XES[:, 0, :], PS[:, 4:6, :].rearrange("p a n -> p (a n)")).then_inc(xe_hi, 1)

            def y_out(i):
                act.wait_ge(yd, i)
                nc.scalar.copy(YS[:, 0, :], PS[:, 2:4, :].rearrange("p a n -> p (a n)")).then_inc(ysb, 1)

            def item(i, first):
                for u in range(UNITS_E):
                    v = i * UNITS_E + u
                    act.wait_ge(gu_ps, v + 1)
                    nc.scalar.activation(ESIL, PS[:, 0, 0:UCOL], ACT.Silu).then_inc(esil, 1)
                    if u == UNITS_E - 1:
                        dispatched(i + 1)
                    for c in range(SOON):
                        high(e_piece(v, c), e_used(v, c))
                    if u == 0 and not first:
                        y_out(i)
                    act.wait_ge(t_ps, v + 1)
                    nc.scalar.copy(EHS[:, 0, :], PS[:, 1, 0:UCOL]).then_inc(eht_hi, 1)
                    for c in range(SOON, RING):
                        high(e_piece(v, c), e_used(v, c))
                    if u == 2:
                        picked(i + 1)

            for at in (1, 2):
                act.wait_ge(used[at], ring.used[at])
            for c in range(4):
                high(E_FIRST[c], None)
            act.wait_ge(used[3], ring.used[3])
            picked(0)
            dispatched(0)
            more = more_items(act)
            item(0, True)
            with act.Fori(0, more) as j:
                item(j + 1, False)
            y_out(more + 1)
            sqrt_ln(11)

        @block.vector
        def _(dve):
            ch = Chain(dve, dve_chain)
            V = nc.vector
            for ct in range(4):
                V.memset(Z[:, ct, :], 0.0)
                V.memset(UP[:, ct, :], 0.0).then_inc(z_pad, 1) if ct >= 2 else V.memset(UP[:, ct, :], 0.0)
            dve.wait_ge(z_pad, 2)
            dve.wait_ge(rows_t, 1)
            V.tensor_copy(COLS[:, :], PS[:, 0, 0:NROWS]).then_inc(cols_ready, 1)
            ch(V.tensor_copy(BCOLS[:, :], PS[:, 0, NROWS:NROWS + DEPTH * 6 * KD]))
            for l in range(DEPTH):
                for j in range(2):
                    at = (6 * l + 3 * j + 1) * KD
                    last = V.tensor_scalar(BCOLS[:, at:at + KD], BCOLS[:, at:at + KD], 1.0, None, ALU.add)
            ch(last)

            def ada(group, between={}):
                def cols(n):
                    l, p = divmod(n, NPANEL)
                    k = PANEL // P
                    at = l * 6 * KD + p * k
                    dve.wait_ge(cols_t, n + 1)
                    V.tensor_tensor(MT[:, l, p * k:(p + 1) * k, :], PS[:, 7, 384:384 + 2 * k].rearrange("p (k c) -> p k c", c=2),
                                    BCOLS[:, at:at + k].unsqueeze(2).broadcast_to([P, k, 2]), ALU.add).then_inc(cols_done, 1)

                for n in group:
                    if n > group[0]:
                        cols(n - 1)
                    dve.wait_ge(mm_a, n + 1)
                    if n >= 2:
                        dve.wait_ge(cols_t, n - 1)
                    V.tensor_copy(STG[:, n % 2, 0:384], PS[0:2, 6, 0:384]).then_inc(st_a, 1)
                    dve.wait_ge(mm_b, n + 1)
                    V.tensor_copy(STG[:, n % 2, 384:768], PS[0:2, 7, 0:384]).then_inc(st_b, 1)
                    if n in between:
                        between[n]()
                cols(group[-1])
                for n in GATES_AT.get(group[-1], ()):
                    a = slice(2 * (n % 2), 2 * (n % 2) + 2)
                    dve.wait_ge(gates_t, GATES_AT[group[-1]][-1] + 1)
                    if n >= 2:
                        dve.wait_ge(stored, 16 * (n - 1))
                    V.tensor_copy(GS[:, a, :], PS[0:KD, 6, 256 * (n % 2):256 * (n % 2) + 256].rearrange("k (a p) -> k a p", a=2))\
                        .then_inc(gates_out, 1)
                for st in FOLDS_AT.get(group[-1], ()):
                    l, j = divmod(st, 2)
                    dve.wait_ge(cols_done, group[-1] + 1)
                    lg, lb = (COLS[:, at + (st - 1) * KD:at + st * KD].unsqueeze(2).broadcast_to([P, KD, 2]) for at in (35, 67))
                    shift, scale = (MT[:, l, (3 * j + i) * KD:(3 * j + i + 1) * KD, :] for i in range(2))
                    tmp = T[:, 0:2 * KD].rearrange("p (k c) -> p k c", c=2)
                    ch(V.tensor_tensor(tmp, scale, lb, ALU.mult))
                    ch(V.tensor_tensor(shift, shift, tmp, ALU.add))
                    V.tensor_tensor(scale, scale, lg, ALU.mult).then_inc(mt_ready, 1)

            def rsqrt(n, at, count):
                v, r, w = SM[:, at:at + count], SM[:, at + count:at + 2 * count], SM[:, 112:112 + count]
                dve.wait_ge(sd_ready, n)
                ch(V.reciprocal(r, r))
                ch(V.tensor_tensor(w, v, r, ALU.mult))
                ch(V.tensor_tensor(w, w, r, ALU.mult))
                ch(V.tensor_scalar(w, w, -0.5, 1.5, ALU.mult, ALU.add))
                ch(V.tensor_tensor(r, r, w, ALU.mult))

            def layer_norm(st, n_sd, y_of):
                dve.wait_ge(lnp_in, 48 * (st + 1))

                def residual(g):
                    x = X[:, g, :]
                    y = y_of(g)
                    if st:
                        dve.wait_ge(x_full, NG * (st - 1) + g + 1)
                    ch(V.tensor_tensor(T[:, :], y, GB[:, min(g, 1), :], ALU.mult))
                    ch(V.scalar_tensor_tensor(x, x, ALPHA, T[:, :], ALU.mult, ALU.add))
                    for b in range(2):
                        ch(V.bn_stats(SM[:, 16 + 6 * b:22 + 6 * b], X[:, g, b * 512:(b + 1) * 512]))
                    ch(V.bn_aggr(SM[:, 28 + 2 * g:30 + 2 * g], SM[:, 16:28]))
                    V.tensor_scalar(SM[:, 2 * g:2 * g + 1], SM[:, 29 + 2 * g:30 + 2 * g], LN_EPS, None, ALU.add).then_inc(var_ready, 1)

                def normalise(g):
                    x = X[:, g, :]
                    dve.wait_ge(var_ready, n_sd + g)
                    rsqrt(n_sd + g, 2 * g, 1)
                    V.tensor_scalar(x, x, SM[:, 28 + 2 * g:29 + 2 * g], SM[:, 2 * g + 1:2 * g + 2], ALU.subtract, ALU.mult)\
                        .then_inc(ln_x, 1)
                    if st == 2 * DEPTH - 1 and g == NG - 1:
                        dve.wait_ge(ln_x, NG * st + g + 1)
                        ch(V.tensor_tensor(x, x, LG[:, :], ALU.mult))
                        V.tensor_tensor(x, x, LB[:, :], ALU.add).then_inc(x_last, 1)

                residual(0)
                for g in range(1, NG):
                    residual(g)
                    normalise(g - 1)
                normalise(NG - 1)

            def y_psum(st):
                def y(g):
                    dve.wait_ge(y_ps, NG * st + g + 1)
                    return PS[:, 2 * g:2 * g + 2, :].rearrange("p a n -> p (a n)")
                return y

            def modulate(st):
                l, j = divmod(st, 2)
                dve.wait_ge(mt_ready, st) if st else dve.wait_ge(cols_done, MIXER_PANELS)
                dve.wait_ge(xt_t, 2 * NG * st + 5)
                for k in range(4):
                    last = V.tensor_scalar(HT[:, k, 2 * P:3 * P], PS[:, 4, k * P:(k + 1) * P],
                                           MT[:, l, (3 * j + 1) * KD + k, 1:2], MT[:, l, 3 * j * KD + k, 1:2],
                                           ALU.mult, ALU.add)
                last.then_inc(ht_d, 1)

            ada(range(NPANEL), {3: lambda: modulate(0)})
            for ct in range(4):
                dve.wait_ge(u_ps, 12 + ct + 1)
                dve.wait_ge(u_act, 12)
                for tok, at, n in SEGZ:
                    last = V.tensor_tensor(Z[:, ct, at:at + n], PS[:, ct, tok:tok + n], UX[:, ct, tok:tok + n], ALU.mult)
                last.then_inc(u_dve, 1)
            dve.wait_ge(u_dve, 4)
            for ct in range(4):
                w = ZW - 2
                tap = lambda k: COLS[:, 4 * k + ct:4 * k + ct + 1]
                if ct:
                    dve.wait_ge(mix_conv, ct)
                ch(V.tensor_scalar(CV[:, 0:w], Z[:, ct, 0:w], tap(0), None, ALU.mult))
                ch(V.scalar_tensor_tensor(CV[:, 0:w], Z[:, ct, 1:1 + w], tap(1), CV[:, 0:w], ALU.mult, ALU.add))
                ch(V.scalar_tensor_tensor(CV[:, 0:w], Z[:, ct, 2:2 + w], tap(2), CV[:, 0:w], ALU.mult, ALU.add))
                for tok, at, n in SEGZ:
                    last = V.tensor_tensor(MIX[:, ct, tok:tok + n], CV[:, at - 1:at - 1 + n], UB[:, ct, tok:tok + n], ALU.mult)
                last.then_inc(mix_conv, 1)
            layer_norm(0, 1, y_psum(0))

            def split_h():
                for k in range(KD):
                    dve.wait_ge(hx_hi, k + 1)
                    V.tensor_tensor(HX[:, 1, k, :], HT[:, k, :], HX[:, 0, k, :].bitcast(F32), ALU.subtract).then_inc(hx_lo, 1)

            ada(range(8, 12), {8: lambda: modulate(1), 10: split_h})

            def low(piece):
                n, at, _ = piece
                dve.wait_ge(hi_done, n + 1)
                V.tensor_tensor(WS[:, at, 1, :], RAW[:, at, :], WS[:, at, 0, :].bitcast(F32), ALU.subtract)\
                    .then_inc(lo_done, 1)

            def ff_hidden(f, b):
                dve.wait_ge(sil, f + 1)
                dve.wait_ge(up_ps, f + 1)
                if not (isinstance(f, int) and f == 0):
                    dve.wait_ge(fh_lo, f)
                V.tensor_tensor(HF, SIL, PS[:, 7, 0:TOK], ALU.mult).then_inc(ff_h, 1)
                dve.wait_ge(fh_hi, f + 1)
                V.tensor_tensor(HFS[:, b, 1, :], HF, HFS[:, b, 0, :].bitcast(F32), ALU.subtract).then_inc(fh_lo, 1)

            for c in range(5):
                low(FF_FIRST[c])
            ff_hidden(0, 0)
            ff_hidden(1, 1)
            with dve.Fori(0, FF_ITERS) as i:
                for b in range(2):
                    for c in range(RING):
                        low(ff_piece(i * 2 + b, c))
                    ff_hidden(i * 4 + (2 + 2 * b), 0)
                    ff_hidden(i * 4 + (3 + 2 * b), 1)
            low(FF_LAST)
            layer_norm(1, 4, y_psum(1))
            modulate(2)
            ada([12])

            dve.wait_ge(odu, 2 * NG)
            f0 = QR + KVR + ROPE
            dve.wait_ge(ssq, 1)
            for g in range(NG):
                for b in range(FG):
                    at = 6 * (g * FG + b)
                    ch(V.bn_stats(T[:, at:at + 6], U[:, g, f0 + b * FGD:f0 + (b + 1) * FGD]))
                    ch(V.bn_aggr(T[:, 100 + at:102 + at], T[:, at:at + 6]))
            ch(V.tensor_scalar(SM[:, 64:67], SM[:, 40:43], 1.0 / QR, RMS_EPS, ALU.mult, ALU.add))
            ch(V.tensor_scalar(SM[:, 67:70], SM[:, 43:46], 1.0 / KVR, RMS_EPS, ALU.mult, ALU.add))
            V.tensor_scalar(SM[:, 70:82], T[:, 101:101 + 72:6], LN_EPS, None, ALU.add).then_inc(var_ready, 1)
            dve.wait_ge(var_ready, 7)
            rsqrt(7, 64, 18)
            for g in range(NG):
                last = V.tensor_scalar(U[:, g, 0:QR], U[:, g, 0:QR], SM[:, 82 + g:83 + g], None, ALU.mult)
            last.then_inc(odn, 1)
            dve.wait_ge(kvn_in, 16)
            for g in range(NG):
                last = V.scalar_tensor_tensor(U[:, g, QR:QR + KVR], U[:, g, QR:QR + KVR], SM[:, 85 + g:86 + g], KVN,
                                              ALU.mult, ALU.mult)
            last.then_inc(odn, 1)
            for g in range(NG):
                for b in range(FG):
                    j = g * FG + b
                    part = U[:, g, f0 + b * FGD:f0 + (b + 1) * FGD]
                    last = V.tensor_scalar(part, part, T[:, 100 + 6 * j:101 + 6 * j], SM[:, 88 + j:89 + j],
                                           ALU.subtract, ALU.mult)
            last.then_inc(odn, 1)

            ada([13])

            def rope(x, ps, signal):
                ch(V.tensor_tensor(T[:, 512:768], x, odc("cos"), ALU.mult))
                ch(V.tensor_tensor(T[:, 768:1024], ps, odc("sin"), ALU.mult))
                V.tensor_tensor(x, T[:, 512:768], T[:, 768:1024], ALU.add).then_inc(signal, 1)

            dve.wait_ge(oddc_in, 32)
            dve.wait_ge(odt_a, 6)
            dve.wait_ge(rot_ps, 1)
            rope(KPT[:, 2 * P:4 * P], PS[:, 6, 0:DEC], kpt_ready)
            for q in range(4):
                j, seg = divmod(q, 2)
                dve.wait_ge(f1_ps, q + 1)
                dst = FA[:, j, 0:256] if seg == 0 else FA[:, j, 256:768]
                V.tensor_copy(dst, PS[:, q, 0:256 if seg == 0 else 512]).then_inc(fa, 1)
            for j in range(2):
                dve.wait_ge(f2_ps, j + 1)
                V.tensor_copy(FT[:, j, :], PS[:, 4 + j, 0:TOK]).then_inc(ft, 1)
            for j in range(2):
                dve.wait_ge(f3_ps, j + 1)
                V.tensor_copy(GT[:, j, :], PS[:, j, 0:TOK]).then_inc(gt if j == 0 else o_ready, 1)

            per = 2 + NC6 * 2
            base = ch.n
            with dve.Fori(0, NH // 2) as i:
                ch.n = i * per + base
                for q in range(3, 7):
                    dve.wait_ge(pj_ps, i * 7 + q + 1)
                    dst = KT[:, q - 3, :] if q < 5 else VV[:, 2 * (q - 5):2 * (q - 5) + 2, :].rearrange("p a n -> p (a n)")
                    V.tensor_copy(dst, PS[:, q, :]).then_inc(pj_d, 1)
                dve.wait_ge(pj_a, i * 3 + 3)
                dve.wait_ge(qrot_ps, i + 1)
                rope(QP[:, P:3 * P], PS[:, 7, 0:DEC], qp_ready)
                for cc in range(NC6 + 4):
                    if cc < NC6:
                        n = P * (keys(COMBOS[cc][1])[1] - keys(COMBOS[cc][1])[0])
                        mx, nm = SM[:, 108 + cc % 2:109 + cc % 2], SM[:, 104 + cc % 2:105 + cc % 2]
                        dve.wait_ge(s_ps, i * NC6 + cc + 1)
                        ch(V.reduce_max(mx, PS[:, cc % 2, 0:n], AX.X))
                        V.tensor_scalar(nm, mx, -SCALE, None, ALU.mult).then_inc(nmax, 1)
                    if 1 <= cc <= NC6:
                        b = cc - 1
                        n = P * (keys(COMBOS[b][1])[1] - keys(COMBOS[b][1])[0])
                        den = SM[:, 106 + b % 2:107 + b % 2]
                        dve.wait_ge(e_done, i * NC6 + b + 1)
                        ch(V.reciprocal(SM[:, 110 + b % 2:111 + b % 2], den))
                        V.tensor_scalar(PB[:, b % 2, 0:n], PB[:, b % 2, 0:n], SM[:, 110 + b % 2:111 + b % 2], None,
                                        ALU.mult).then_inc(p_ready, 1)
                    if cc >= 4:
                        b = cc - 4
                        h, qt = COMBOS[b]
                        dve.wait_ge(o_ps, i * NC6 + b + 1)
                        V.tensor_copy(HT[:, bass.ds(i * 2 + h, 1), qt * P:(qt + 1) * P],
                                      PS[:, 4 + b % 2:5 + b % 2, 0:P]).then_inc(o_ready, 1)
            ch.n = base + per * (NH // 2)
            layer_norm(2, 8, y_psum(2))
            ada([14])
            modulate(3)
            ada([15])

            b3 = lambda a: a.unsqueeze(2).broadcast_to([P, NG, NE])
            cut = iter(range(8, 900, 24))
            take = lambda: MS[:, next(cut) + 4:][:, 0:24].rearrange("p (g e) -> p g e", g=NG)
            L, EQ, VI, K1, K2, L2, G, G2, M, PMX = (take() for _ in range(10))
            small = MS[:, 270:300]
            m1, m2, im, w1, w2 = (small[:, 3 * j:3 * j + 3] for j in range(5))
            eidx = cst("expert").rearrange("p (g e) -> p g e", g=NG)
            dve.wait_ge(lg_ps, 1)
            dve.wait_ge(kv_out, 32)
            ch(V.tensor_copy(L, PS[:, 0, TOK:TOK + 24].rearrange("p (g e) -> p g e", g=NG)))

            def best(src, m, k):
                ch(V.tensor_reduce(m, src, AX.X, ALU.max))
                ch(V.tensor_tensor(EQ, src, b3(m), ALU.is_equal))
                ch(V.scalar_tensor_tensor(VI, EQ, -100.0, eidx, ALU.mult, ALU.add))
                ch(V.tensor_reduce(im, VI, AX.X, ALU.min))
                ch(V.tensor_tensor(k, VI, b3(im), ALU.is_equal))

            best(L, m1, K1)
            ch(V.scalar_tensor_tensor(L2, K1, -1e30, L, ALU.mult, ALU.add))
            best(L2, m2, K2)
            V.tensor_tensor(M, K1, K2, ALU.add).then_inc(m_ready, 1)
            V.tensor_tensor(MS[:, 0:3], m2, m1, ALU.subtract).then_inc(d_ready, 1)
            for q in range(2 * NG):
                g, half = divmod(q, 2)
                at = slice(half * 512, (half + 1) * 512)
                dve.wait_ge(hk, q + 1)
                V.tensor_tensor(HKS[:, 1, g, at], PS[:, 1 + q, :], HKS[:, 0, g, at].bitcast(F32), ALU.subtract).then_inc(hk_lo, 1)
            dve.wait_ge(ex_ready, 1)
            ch(V.tensor_scalar(w1, MS[:, 3:6], 1.0, None, ALU.add))
            ch(V.reciprocal(w1, w1))
            ch(V.tensor_tensor(w2, MS[:, 3:6], w1, ALU.mult))
            ch(V.tensor_tensor(G, K1, b3(w1), ALU.mult))
            ch(V.tensor_tensor(G2, K2, b3(w2), ALU.mult))
            ch(V.tensor_tensor(G, G, G2, ALU.add))
            dve.wait_ge(m_ready, 1)
            dve.wait_ge(pos_ps, 1)
            ch(V.scalar_tensor_tensor(PMX, PS[:, 0, 0:24].rearrange("p (g e) -> p g e", g=NG), 1.0, M, ALU.add, ALU.mult))
            posa = POSA.rearrange("p (r e g) -> p r e g", r=3, e=NE)
            ga = GA.rearrange("p (r e g) -> p r e g", r=3, e=NE)
            for r in range(3):
                V.tensor_scalar(posa[:, r].rearrange("p e g -> p g e"), PMX, -1.0 - P * r, None, ALU.add)
                last = V.tensor_copy(ga[:, r].rearrange("p e g -> p g e"), G)
            last.then_inc(pos_ready, 1)
            dve.wait_ge(pos_ready, 1)
            for g in range(NG):
                last = V.tensor_scalar(PM[:, g, :], cst("iota"), POSA[:, g:g + 1], None, ALU.is_equal)
            last.then_inc(mp_ready, 1)
            for c in range(4):
                low(E_FIRST[c])
            row = lambda at, n: MS[0:1, at:at + n]
            EX, PF, IX, CB, TF = row(320, 16), row(336, 16), row(352, 16), row(370, 256), row(640, 33)
            cand = lambda name: cst(name, 1)
            for r in range(2):
                ch(V.tensor_scalar(EX.rearrange("o (e r) -> o e r", r=2)[:, :, r], PS[0:1, 0, 24:32], float(P * (r + 1)), None,
                                   ALU.is_gt))
            ch(V.tensor_tensor_scan(PF, cst("ones", 1)[:, 0:16], EX, 0.0, ALU.mult, ALU.add))
            ch(V.scalar_tensor_tensor(IX, PF, float(NE), EX, ALU.add, ALU.mult))
            ch(V.tensor_scalar(IX, IX, -1.0, None, ALU.add))
            cb = CB.rearrange("o (j c) -> o j c", j=TABLE)
            jc = [1, TABLE, 16]
            ch(V.tensor_scalar(TF[:, 0:1], PF[:, 15:16], float(NE - 1), None, ALU.add))
            for b, name in enumerate(("cand_code", "cand_expert")):
                part = TF[:, 1 + TABLE * b:1 + TABLE * (b + 1)]
                ch(V.tensor_tensor(cb, cand("item").unsqueeze(2).broadcast_to(jc), IX.unsqueeze(1).broadcast_to(jc),
                                   ALU.is_equal))
                ch(V.tensor_tensor(cb, cb, cand(name).unsqueeze(1).broadcast_to(jc), ALU.mult))
                ch(V.tensor_reduce(part, cb, AX.X, ALU.add))
                ch(V.tensor_tensor(part, part, cand("base"), ALU.add))
            V.tensor_copy(TAB[:, :], TF).then_inc(tab_ready, 1)
            more = more_items(dve)

            def one_hot(dst, i, signal):
                code = dve.value_load(TAB[0:1, bass.ds(i + 1, 1)] if not isinstance(i, int) else TAB[0:1, i + 1:i + 2],
                                      min_val=0, max_val=CODES - 1)
                for g in range(NG):
                    at = bass.ds(code * NG + g, 1)
                    last = V.tensor_scalar(dst[:, g, :], cst("iota"), POSA[:, at], None, ALU.is_equal)
                last.then_inc(signal, 1)
                return code

            def turned(i):
                dve.wait_ge(ptt_ps, i)
                V.tensor_copy(PT[:, :], PS[:, 6, 0:TOK]).then_inc(pt_sb, 1)

            def y_split(i):
                dve.wait_ge(ysb, i)
                V.tensor_tensor(YS[:, 1, :], PS[:, 2:4, :].rearrange("p a n -> p (a n)"), YS[:, 0, :].bitcast(F32),
                                ALU.subtract).then_inc(y_lo, 1)

            def combined(j, q, code):
                g, half = divmod(q, 2)
                y = YACC[:, g, half * 512:(half + 1) * 512]
                dve.wait_ge(cb_ps, j * 2 * NG + q + 1)
                V.scalar_tensor_tensor(y, PS[:, 6 + q % 2, :], GA[:, bass.ds(code * NG + g, 1)], y, ALU.mult, ALU.add)\
                    .then_inc(cb_done, 1)

            def dispatched(i):
                dve.wait_ge(xe_hi, i + 1)
                V.tensor_tensor(XES[:, 1, :], PS[:, 4:6, :].rearrange("p a n -> p (a n)"), XES[:, 0, :].bitcast(F32),
                                ALU.subtract).then_inc(xe_done, 1)

            def item(i, first, j=0):
                for u in range(UNITS_E):
                    v = i * UNITS_E + u
                    dve.wait_ge(esil, v + 1)
                    V.tensor_tensor(EH, ESIL, PS[:, 0, UCOL:2 * UCOL], ALU.mult).then_inc(eh, 1)
                    if u == UNITS_E - 1:
                        dispatched(i + 1)
                    for c in range(SOON):
                        low(e_piece(v, c))
                    if u == 0 and not first:
                        y_split(i)
                    dve.wait_ge(eht_hi, v + 1)
                    V.tensor_tensor(EHS[:, 1, :], PS[:, 1, 0:UCOL], EHS[:, 0, :].bitcast(F32), ALU.subtract)\
                        .then_inc(eht_lo, 1)
                    for c in range(SOON, RING):
                        low(e_piece(v, c))
                    if u == 0:
                        dve.wait_ge(dx_ps, i + 1)
                        one_hot(PM, i + 1, mp_ready)
                        code = None if first else one_hot(PG, j, pg_ready)
                    if u == 1 and not first:
                        turned(i)
                    if u in (2, 3, 4) and not first:
                        if u == 2:
                            dve.wait_ge(cb_done, j * 2 * NG + 1)
                        for q in (2 * u - 4, 2 * u - 3):
                            combined(j, q, code)

            dispatched(0)
            V.memset(YACC.rearrange("p a n -> p (a n)"), 0.0).then_inc(cb_done, 1)
            item(0, True)
            with dve.Fori(0, more) as j:
                item(j + 1, False, j)
            code = one_hot(PG, more, pg_ready)
            y_split(more + 1)
            turned(more + 1)
            dve.wait_ge(cb_done, more * 2 * NG + 1)

            def experts_sum(g):
                for q in (2 * g, 2 * g + 1):
                    combined(more, q, code)
                dve.wait_ge(cb_done, more * 2 * NG + (2 * g + 3))
                return YACC[:, g, :]

            layer_norm(3, 11, experts_sum)

        @block.tensor
        def _(pe):
            mm, tr = nc.tensor.matmul, nc.tensor.transpose
            pe.wait_ge(cst_in, 16)
            pe.wait_ge(rows_in, 128)
            nb = DEPTH * 6 * KD
            tr(PS[:, 0, NROWS:NROWS + nb], BROWS[:, :], ident[0:nb, 0:nb])
            tr(PS[:, 0, 0:NROWS], ROWS[:, :], ident[0:NROWS, 0:NROWS]).then_inc(rows_t, 1)

            def ada(group, after=None, between={}):
                def turn(n):
                    pe.wait_ge(st_a, n + 1)
                    pe.wait_ge(st_b, n + 1)
                    for k in range(PANEL // P):
                        last = tr(PS[:, 7, 384 + 2 * k:386 + 2 * k], STG[:, n % 2, k * P:(k + 1) * P], ident[0:2, 0:2])
                        if k == 0:
                            release(last, ("ada", n))
                    last.then_inc(cols_t, 1)

                for n in group:
                    w = slot(("ada", n)).rearrange("p (k n) -> p k n", k=KD)
                    if n:
                        wait_unit(pe, ("ada", n))
                    else:
                        pe.wait_ge(half_in, 16)
                    if n:
                        pe.wait_ge(st_a, n)
                    for h in range(2):
                        if h and n > group[0]:
                            pe.wait_ge(cols_done, n)
                        if h and n == 0:
                            wait_unit(pe, ("ada", 0))
                        for k in range(KD):
                            if (h, k) == (0, 4) and n > group[0]:
                                turn(n - 1)
                            last = mm(PS[0:2, 6 + h, 0:384], SC[:, k, :], w[:, k, h * 384:(h + 1) * 384],
                                      start=(k == 0), stop=(k == KD - 1))
                            if (n, h, k) == (group[0], 0, 0) and after:
                                release(last, after)
                        last.then_inc((mm_a, mm_b)[h], 1)
                    if n in between:
                        between[n]()
                turn(group[-1])
                pe.wait_ge(cols_done, group[-1] + 1)
                for n in GATES_AT.get(group[-1], ()):
                    l, j = divmod(n, 2)
                    for cond in range(2):
                        at = (2 * j + cond) * P
                        last = tr(PS[0:KD, 6, at:at + P], MT[:, l, (3 * j + 2) * KD:(3 * j + 3) * KD, cond], ident)
                    last.then_inc(gates_t, 1)

            def release(ins, name):
                ins.then_inc(used[ring.units[name][0]], 1)

            def x_turned(st, after=None):
                for q in range(2 * NG):
                    g, half = divmod(q, 2)
                    if half == 0:
                        pe.wait_ge(ln_x, NG * (st - 1) + g + 1) if st else pe.wait_ge(x_in, 32)
                    for b in range(4):
                        k = half * 4 + b
                        last = tr(PS[:, q, b * P:(b + 1) * P], X[:, g, k * P:(k + 1) * P], ident)
                        if (q, b) == (0, 0) and after:
                            release(last, after)
                    last.then_inc(xt_t, 1)

            def h_ready(st):
                pe.wait_ge(ht_a, 5 * (st + 1))
                pe.wait_ge(ht_d, st + 1)

            pe.wait_ge(sc_ready, 1)
            ada(range(NPANEL), between={3: lambda: x_turned(0)})
            h_ready(0)
            for t in range(16):
                w = slot(("evin", t // 4))[:, 0:4096].rearrange("p (k n) -> p k n", k=KD)
                if t % 4 == 0:
                    wait_unit(pe, ("evin", t // 4))
                if t >= 4:
                    pe.wait_ge(u_act, t - 3)
                for k in range(KD):
                    last = mm(PS[:, t % 4, 0:TOK], w[:, k, (t % 4) * P:(t % 4 + 1) * P], HT[:, k, :],
                              start=(k == 0), stop=(k == KD - 1))
                    if t % 4 == 0 and t and k == 0:
                        release(last, ("evin", t // 4 - 1))
                last.then_inc(u_ps, 1)
                if t == 11:
                    pe.wait_ge(pw_in, 16)
                    for g in range(NPOOL):
                        pe.wait_ge(pp_ready, g + 1)
                        if g >= 2:
                            pe.wait_ge(mix_pool, g - 1)
                        mm(PS[:, 6 + g % 2, 0:TOK], PW[:, g, :], PP[:, g, :], start=True, stop=True).then_inc(pm_ps, 1)

            def project_out(units, per, lhs, ready, after=None):
                n = len(units) * per
                for k in range(n):
                    w = slot(units[k // per])[:, 0:per * D].rearrange("p (k n) -> p k n", k=per)
                    if k % per == 0:
                        wait_unit(pe, units[k // per])
                    ready(k)
                    for g in range(NG):
                        for h in range(2):
                            last = mm(PS[:, 2 * g + h, :], lhs(k)[:, g * P:(g + 1) * P], w[:, k % per, h * 512:(h + 1) * 512],
                                      start=(k == 0), stop=(k == n - 1))
                            if (k, g, h) == (0, 0, 0) and after:
                                release(last, after)
                        if k == n - 1:
                            last.then_inc(y_ps, 1)
                    if k % per == per - 1 and k < n - 1:
                        release(last, units[k // per])

            def mix_ready(k):
                if k == 0:
                    pe.wait_ge(u_dve, 4)
                    pe.wait_ge(mix_pool, 4)
                if k >= 4:
                    pe.wait_ge(mix_conv, k - 3)

            project_out([("evout", 0), ("evout", 1)], 4, lambda k: MIX[:, (k + 4) % 8, :], mix_ready, ("evin", 3))
            ada(range(8, 12), ("evout", 1), {8: lambda: x_turned(1)})
            h_ready(1)

            def product(out, left, right, start, stop):
                (lh, ll), (rh, rl) = left, right
                first = mm(out, lh, rh, start=start, stop=False)
                mm(out, lh, rl, start=False, stop=False)
                return first, mm(out, ll, rh, start=False, stop=stop)

            def halves(buf, *at):
                return buf[(slice(None), 0) + at], buf[(slice(None), 1) + at]

            def gate_up_w(piece, k, cols):
                at = (k % 2) * 2 * UCOL
                return tuple(WS[:, piece[1], part, at + cols.start:at + cols.stop] for part in range(2))

            def down_w(piece, h):
                return tuple(WS[:, piece[1], part, h * 512:(h + 1) * 512] for part in range(2))

            def ff_gate_up(f, b, four):
                if not (isinstance(f, int) and f == 0):
                    pe.wait_ge(ff_h, f)
                for j, sig in enumerate((g_ps, up_ps)):
                    for k in range(KD):
                        if (b, j, k % 2) == (0, 0, 0):
                            pe.wait_ge(lo_done, four[k // 2][0] + 1)
                        if isinstance(f, int) and (f, j) == (0, 0):
                            pe.wait_ge(hx_lo, k + 1)
                        cols = slice(j * UCOL + b * P, j * UCOL + (b + 1) * P)
                        _, last = product(PS[:, 6 + j, 0:TOK], gate_up_w(four[k // 2], k, cols), halves(HX, k),
                                          k == 0, k == KD - 1)
                        if (b, j, k % 2) == (1, 1, 1) and k < KD - 1:
                            last.then_inc(w_used, 1)
                    last.then_inc(sig, 1)

            def ff_down(f, b, piece, start=False, stop=False, after=False):
                pe.wait_ge(fh_lo, f + 1)
                pe.wait_ge(lo_done, piece[0] + 1)
                for g in range(NG):
                    for h in range(2):
                        left = tuple(HFS[:, b, part, g * P:(g + 1) * P] for part in range(2))
                        first, last = product(PS[:, 2 * g + h, :], left, down_w(piece, h), start, stop)
                        if after and (g, h) == (0, 0):
                            first.then_inc(w_used, 1)
                    if stop:
                        last.then_inc(y_ps, 1)
                if not stop:
                    last.then_inc(w_used, 1)

            pe.wait_ge(gates_out, 3)
            ff_gate_up(0, 0, FF_FIRST[0:4])
            ff_gate_up(1, 1, FF_FIRST[0:4])
            ff_down(0, 0, FF_FIRST[4], start=True, after=True)
            with pe.Fori(0, FF_ITERS) as i:
                for b in range(2):
                    f = i * 4 + (2 + 2 * b)
                    unit = [ff_piece(i * 2 + b, c) for c in range(RING)]
                    ff_gate_up(f, 0, unit[0:4])
                    ff_down(f - 1, 1, unit[4])
                    ff_gate_up(f + 1, 1, unit[0:4])
                    ff_down(f, 0, unit[5], after=True)
            ff_down(NF - 1, 1, FF_LAST, stop=True)
            x_turned(2)
            ada([12])
            h_ready(2)
            for q in range(2 * NG):
                h, g = divmod(q, NG)
                w = slot(("odin", h))[:, 0:3840].rearrange("p (k n) -> p k n", k=KD)
                if g == 0:
                    wait_unit(pe, ("odin", h))
                for k in range(KD):
                    last = mm(PS[:, q, 0:480], HT[:, k, g * P:(g + 1) * P], w[:, k, :], start=(k == 0), stop=(k == KD - 1))
                    if (q, k) == (NG, 0):
                        release(last, ("odin", 0))
                last.then_inc(odi_ps, 1)
            def latents_turned():
                pe.wait_ge(odu, 2 * NG)
                pe.wait_ge(odn, 1)
                for q in range(3):
                    for g in range(NG):
                        last = tr(PS[:, q, g * P:(g + 1) * P], U[:, g, q * P:(q + 1) * P], ident)
                    last.then_inc(odt_ps, 1)
                pe.wait_ge(cache_in, 48)
                pe.wait_ge(odn, 2)
                for q in range(2):
                    for kg in range(4):
                        src = CK[:, q * P:(q + 1) * P] if kg == 1 else U[:, max(kg - 1, 0), QR + q * P:QR + (q + 1) * P]
                        last = tr(PS[:, 3 + q, kg * P:(kg + 1) * P], src, ident)
                    last.then_inc(odt_ps, 1)
                pe.wait_ge(kd_ready, 1)
                for kg in range(4):
                    last = tr(PS[:, 5, kg * P:(kg + 1) * P], KDUP[:, kg, :], ident)
                last.then_inc(odt_ps, 1)

            ada([13], ("odin", 1), {13: latents_turned})
            pe.wait_ge(oddc_in, 32)
            pe.wait_ge(odt_a, 6)
            mm(PS[:, 6, 0:DEC], odc("rot"), KPT[:, 2 * P:4 * P], start=True, stop=True).then_inc(rot_ps, 1)
            pe.wait_ge(odn, 3)
            dl = dft("latent").rearrange("p (k n) -> p k n", k=2)
            f0 = QR + KVR + ROPE
            for j in range(2):
                cols = slice(f0 + j * P, f0 + (j + 1) * P)
                mm(PS[:, 2 * j, 0:256], U[:, 0, cols], dft("prompt"), start=True, stop=True).then_inc(f1_ps, 1)
                for k in range(2):
                    last = mm(PS[:, 2 * j + 1, :], U[:, 1 + k, cols], dl[:, k, :], start=(k == 0), stop=(k == 1))
                last.then_inc(f1_ps, 1)
            for j in range(2):
                pe.wait_ge(fa, 2 * j + 2)
                for lo, n, a in ((0, SEQ, 0), (SEQ, DEC, 256)):
                    mm(PS[:, 4 + j, lo:lo + n], odc("chan_cos"), FA[:, j, a:a + n], start=True, stop=False)
                    last = mm(PS[:, 4 + j, lo:lo + n], odc("chan_nsin"), FA[:, j, a + n:a + 2 * n], start=False, stop=True)
                last.then_inc(f2_ps, 1)
            pe.wait_ge(fnw_in, 16)
            pe.wait_ge(ft, 2)
            for j in range(2):
                for k in range(2):
                    last = mm(PS[:, j, 0:TOK], FNW[:, k, j * P:(j + 1) * P], FT[:, k, :], start=(k == 0), stop=(k == 1))
                last.then_inc(f3_ps, 1)
            pe.wait_ge(kpt_ready, 1)

            wq = WR[:, 3, 0:768].rearrange("p (k h c) -> p k h c", k=3, h=2)
            wp = WR[:, 3, 768:1152].rearrange("p (k n) -> p k n", k=3)
            wk = WR[:, 3, 1152:1664].rearrange("p (k h c) -> p k h c", k=2, h=2)
            wv = WR[:, 3, 1664:2176].rearrange("p (k n) -> p k n", k=2)
            with pe.Fori(0, NH // 2) as i:
                pe.wait_ge(landed[3], i * 16 * PAIR_DMAS + (pair_base[0][3] + 16 * PAIR_DMAS))
                pe.wait_ge(o_ready, i * NC6 + 1)
                for h in range(2):
                    for k in range(3):
                        last = mm(PS[:, h, 0:TOK], wq[:, k, h, :], QHT[:, k, :], start=(k == 0), stop=(k == 2))
                    last.then_inc(pj_ps, 1)
                for k in range(3):
                    last = mm(PS[:, 2, 0:TOK], wp[:, k, :], QHT[:, k, :], start=(k == 0), stop=(k == 2))
                last.then_inc(pj_ps, 1)
                for h in range(2):
                    for k in range(2):
                        last = mm(PS[:, 3 + h, :], wk[:, k, h, :], CKT[:, k, :], start=(k == 0), stop=(k == 1))
                    last.then_inc(pj_ps, 1)
                for kg in range(4):
                    for k in range(2):
                        last = mm(PS[:, 5 + kg // 2, (kg % 2) * 256:(kg % 2 + 1) * 256], CKT[:, k, kg * P:(kg + 1) * P],
                                  wv[:, k, :], start=(k == 0), stop=(k == 1))
                    if kg % 2:
                        last.then_inc(pj_ps, 1)
                pe.wait_ge(pj_a, i * 3 + 3)
                mm(PS[:, 7, 0:DEC], odc("rot"), QP[:, P:3 * P], start=True, stop=True).then_inc(qrot_ps, 1)
                pe.wait_ge(pj_d, i * 4 + 4)
                pe.wait_ge(qp_ready, i + 1)
                for cc in range(NC6 + 3):
                    if cc < NC6:
                        h, qt = COMBOS[cc]
                        lo, hi = (P * v for v in keys(qt))
                        if cc >= 2:
                            pe.wait_ge(e_done, i * NC6 + cc - 1)
                        first = mm(PS[:, cc % 2, 0:hi - lo], QN[:, h, qt * P:(qt + 1) * P], KT[:, h, lo:hi],
                                   start=True, stop=False)
                        if cc == 0:
                            first.then_inc(used[3], 1)
                        mm(PS[:, cc % 2, 0:hi - lo], QP[h * ROPE:(h + 1) * ROPE, qt * P:(qt + 1) * P],
                           KPT[h * ROPE:(h + 1) * ROPE, lo:hi], start=False, stop=True).then_inc(s_ps, 1)
                    if 2 <= cc < NC6 + 2:
                        b = cc - 2
                        lo, hi = keys(COMBOS[b][1])
                        pe.wait_ge(p_ready, i * NC6 + b + 1)
                        for j in range(hi - lo):
                            last = tr(PS[:, 2 + b % 2, j * P:(j + 1) * P], PB[:, b % 2, j * P:(j + 1) * P], ident)
                        last.then_inc(pt_ps, 1)
                    if cc >= 3:
                        b = cc - 3
                        h, qt = COMBOS[b]
                        lo, hi = keys(qt)
                        pe.wait_ge(pt_ready, i * NC6 + b + 1)
                        if b >= 2:
                            pe.wait_ge(o_ready, i * NC6 + b)
                        for j in range(hi - lo):
                            last = mm(PS[:, 4 + b % 2, 0:P], VV[:, lo + j, h * P:(h + 1) * P], PTB[:, b % 2, j * P:(j + 1) * P],
                                      start=(j == 0), stop=(j == hi - lo - 1))
                        last.then_inc(o_ps, 1)

            def attn_ready(k):
                if k == 0:
                    pe.wait_ge(o_ready, NC6 * NH // 2 + 1)
                    pe.wait_ge(gt, 1)

            project_out([("odout", 0), ("odout", 1)], 5, lambda k: HT[:, k, :] if k < 8 else GT[:, k - 8, :], attn_ready)
            ada([14], ("odout", 1), {14: lambda: x_turned(3)})
            ada([15])
            h_ready(3)

            pe.wait_ge(rout_in, 16)
            for k in range(KD):
                last = mm(PS[0:NE, 0, 0:TOK], ROUT[:, k, :], HT[:, k, :], start=(k == 0), stop=(k == KD - 1))
            last.then_inc(lgt_ps, 1)
            for q in range(2 * NG):
                if q == 5:
                    pe.wait_ge(gates_out, 4)
                if q == 1:
                    pe.wait_ge(lgt_sb, 1)
                    for g in range(NG):
                        last = tr(PS[:, 0, TOK + g * NE:TOK + (g + 1) * NE], LT[:, g * P:(g + 1) * P], ident[0:NE, 0:NE])
                    last.then_inc(lg_ps, 1)
                g, half = divmod(q, 2)
                for b in range(4):
                    last = tr(PS[:, 1 + q, b * P:(b + 1) * P], HT[:, half * 4 + b, g * P:(g + 1) * P], ident)
                last.then_inc(hkt_ps, 1)
            pe.wait_ge(m_ready, 1)
            mask = MS[:, 8 + 4 + 8 * 24:8 + 4 + 9 * 24].rearrange("p (g e) -> p g e", g=NG)
            for g in range(NG + 1):
                for b in range(min(g + 1, NG)):
                    m = cst("before") if b == g else cst("ones")
                    last = mm(PS[:, 0, g * NE:(g + 1) * NE], m, mask[:, b, :], start=(b == 0), stop=(b == min(g, NG - 1)))
            last.then_inc(pos_ps, 1)
            pe.wait_ge(pos_ready, 1)

            def dispatch(i):
                pe.wait_ge(mp_ready, i + 1)
                if not (isinstance(i, int) and i == 0):
                    pe.wait_ge(xe_done, i)
                for half in range(2):
                    for g in range(NG):
                        for part in range(2):
                            last = mm(PS[:, 4 + half, :], PM[:, g, :], HKS[:, part, g, half * 512:(half + 1) * 512],
                                      start=(g == 0 and part == 0), stop=(g == NG - 1 and part == 1))
                last.then_inc(dx_ps, 1)

            def turn_tokens(i):
                pe.wait_ge(dx_sb, i + 1)
                for k in range(KD):
                    last = tr(PS[:, 4 + k // 4, (k % 4) * P:(k % 4 + 1) * P], XT[:, k * P:(k + 1) * P], ident)
                last.then_inc(disp_ps, 1)

            def gate_up(i, u):
                if not (isinstance(i, int) and i == 0 and u == 0):
                    pe.wait_ge(eh, i * UNITS_E + u)
                for k in range(KD):
                    if isinstance(i, int) and i == 0 and u == 0:
                        piece = E_FIRST[k // 2]
                    else:
                        piece = e_piece(i * UNITS_E + u - 1, k // 2)
                    if k % 2 == 0:
                        pe.wait_ge(lo_done, piece[0] + 1)
                    _, last = product(PS[:, 0, :], halves(XES, slice(k * P, (k + 1) * P)),
                                      gate_up_w(piece, k, slice(0, 2 * UCOL)), k == 0, k == KD - 1)
                    if k % 2 and k < KD - 1:
                        last.then_inc(w_used, 1)
                last.then_inc(gu_ps, 1)

            def down(i, u, after=True):
                pe.wait_ge(eht_lo, i * UNITS_E + u + 1)
                if u == 0 and not (isinstance(i, int) and i == 0):
                    pe.wait_ge(y_lo, i)
                for b in range(2):
                    piece = e_piece(i * UNITS_E + u, 4 + b)
                    pe.wait_ge(lo_done, piece[0] + 1)
                    for h in range(2):
                        first, last = product(PS[:, 2 + h, :], halves(EHS, slice(b * P, (b + 1) * P)), down_w(piece, h),
                                              u == 0 and b == 0, u == UNITS_E - 1 and b == 1)
                        if after and (b, h) == (0, 0):
                            first.then_inc(w_used, 1)
                    if b == 0 or u < UNITS_E - 1:
                        last.then_inc(w_used, 1)
                if u == UNITS_E - 1:
                    last.then_inc(yd, 1)

            def turn_selection(i):
                pe.wait_ge(pg_ready, i)
                for g in range(NG):
                    last = tr(PS[:, 6, g * P:(g + 1) * P], PG[:, g, :], ident)
                last.then_inc(ptt_ps, 1)

            def combine(i, j, chunks):
                if chunks[0] == 0:
                    pe.wait_ge(y_lo, i)
                    pe.wait_ge(pt_sb, i)
                for q in chunks:
                    g, half = divmod(q, 2)
                    if q >= 2:
                        pe.wait_ge(cb_done, j * 2 * NG + q)
                    for part in range(2):
                        last = mm(PS[:, 6 + q % 2, :], PT[:, g * P:(g + 1) * P], YS[:, part, half * 512:(half + 1) * 512],
                                  start=(part == 0), stop=(part == 1))
                    last.then_inc(cb_ps, 1)

            def item(i, first, j=0):
                for u in range(UNITS_E):
                    if u == 0:
                        pe.wait_ge(xe_done, i + 1)
                    gate_up(i, u)
                    if u == 0 and not first:
                        down(j, UNITS_E - 1)
                    if u > 0:
                        down(i, u - 1)
                    if u == 1 and not first:
                        pe.wait_ge(cb_done, j * 2 * NG + 1)
                        turn_selection(i)
                    if u in (2, 3, 4) and not first:
                        combine(i, j, (2 * u - 4, 2 * u - 3))
                    if u == 2:
                        dispatch(i + 1)
                    if u == 4:
                        turn_tokens(i + 1)
                    pe.wait_ge(eh, i * UNITS_E + u + 1)
                    for b in range(2):
                        last = tr(PS[:, 1, b * P:(b + 1) * P], EH[:, b * P:(b + 1) * P], ident)
                        if (u, b) == (0, 0):
                            last.then_inc(w_used, 1)
                    last.then_inc(t_ps, 1)

            dispatch(0)
            turn_tokens(0)
            more = more_items(pe)
            item(0, True)
            with pe.Fori(0, more) as j:
                item(j + 1, False, j)
            down(more, UNITS_E - 1, after=False)
            pe.wait_ge(cb_done, more * 2 * NG + 1)
            turn_selection(more + 1)
            combine(more + 1, more, range(2 * NG))


_INS = ["x_prompt", "x_sample", "cache_ckv", "cache_kpe", "c", "c_ctx", "ada_w", "ada_b", "ln_g", "ln_b", "ev_w_in",
        "ev_conv_w", "ev_pool_w", "ev_pool_scale", "ev_w_out", "ffn_w_gate", "ffn_w_up", "ffn_w_down", "od_w_in",
        "od_q_norm", "od_kv_norm", "od_w_q_b", "od_w_kv_b", "od_fnet_w", "od_w_out", "moe_router", "moe_w_gate",
        "moe_w_up", "moe_w_down"]
_OUTS = [(1, SEQ, D), (1, DEC, D), (1, 1, SEQ, KVR), (1, 1, SEQ, ROPE)]


def kernel(**inputs):
    import concourse.bacc as _bacc
    from concourse.bass_utils import run_bass_kernel_spmd as _run

    nc = _bacc.Bacc("TRN2", target_bir_lowering=False, num_devices=1)
    arrays, args = {}, []
    given = {name: np.ascontiguousarray(inputs[name]) for name in _INS}
    given |= {"base_rows": BASE_ROWS, "odd_rows": ODD_ROWS, "dft_rows": DFT_ROWS, "pool_inv": pool_counts()}
    for name, a in given.items():
        arrays[f"in_{name}"] = a
        args.append(nc.dram_tensor(f"in_{name}", a.shape, mybir.dt.from_np(a.dtype), kind="ExternalInput").ap())
    for i, shape in enumerate(_OUTS):
        args.append(nc.dram_tensor(f"out_{i}", shape, F32, kind="ExternalOutput").ap())
    build(nc, *args)
    r = _run(nc, [arrays], core_ids=[0])
    return tuple(r.results[0][f"out_{i}"] for i in range(len(_OUTS)))
```
